# Optimizing a Trainium2 kernel written in Bass

```python
import jax, jax.numpy as jnp
from jax import lax
import numpy as np

D_MODEL = 1024
BATCH = 1
SEQ = 256
DEPTH = 2

N_A_LAYERS = DEPTH // 2
N_B_LAYERS = DEPTH - N_A_LAYERS
EPS = 1e-6

GLA_HEADS = 4
GLA_QK_TOT = D_MODEL // 2
GLA_V_TOT = D_MODEL
GLA_DK = GLA_QK_TOT // GLA_HEADS
GLA_DV = GLA_V_TOT // GLA_HEADS
GLA_GATE_RANK = 16
GLA_TAU = 16.0
GLA_CHUNK = 64
GLA_SPLITS = [GLA_QK_TOT, 2 * GLA_QK_TOT, 2 * GLA_QK_TOT + GLA_V_TOT, 2 * GLA_QK_TOT + 2 * GLA_V_TOT]
GLA_IN_TOT = 2 * GLA_QK_TOT + 2 * GLA_V_TOT + GLA_GATE_RANK

FOX_HD = 64
FOX_HEADS = D_MODEL // FOX_HD
FOX_BLOCK = 128
KV_SPLITS = [D_MODEL, 2 * D_MODEL]
KV_TOT = 2 * D_MODEL + FOX_HEADS

PEER_HEADS = 8
PEER_KEYS = 128
PEER_N = PEER_KEYS * PEER_KEYS
PEER_TOPK = 16
PEER_DHALF = 128
PEER_DQ = 2 * PEER_DHALF
PEER_CHUNK = 128

kernel_name = "yoco_gla_fox_peer_hybrid"

def rmsnorm(x, g):
    xf = x.astype(jnp.float32)
    y = xf * lax.rsqrt(jnp.mean(xf * xf, axis=-1, keepdims=True) + EPS)
    return (y * g.astype(jnp.float32)).astype(x.dtype)

def gla_mixer(xn, w_in, w_g2, b_g, g_o, w_o):
    B, S, _ = xn.shape
    C = GLA_CHUNK
    p = jnp.einsum('bsd,de->bse', xn, w_in).astype(jnp.float32)
    q, k, v, r, glr = jnp.split(p, GLA_SPLITS, axis=-1)
    log_a = jax.nn.log_sigmoid(glr @ w_g2.astype(jnp.float32) + b_g.astype(jnp.float32)) / GLA_TAU

    def heads(t, d):
        return t.reshape(B, S // C, C, GLA_HEADS, d).transpose(1, 0, 3, 2, 4)

    qh = heads(q * (GLA_DK ** -0.5), GLA_DK)
    kh = heads(k, GLA_DK)
    vh = heads(v, GLA_DV)
    lah = heads(log_a, GLA_DK)
    causal = jnp.tril(jnp.ones((C, C), dtype=bool))

    def step(state, inp):
        qc, kc, vc, lac = inp
        bcum = jnp.cumsum(lac, axis=2)
        o_inter = jnp.einsum('bhik,bhkv->bhiv', qc * jnp.exp(bcum), state)
        diff = bcum[:, :, :, None, :] - bcum[:, :, None, :, :]
        diff = jnp.where(causal[:, :, None], diff, -jnp.inf)
        attn = jnp.einsum('bhik,bhjk,bhijk->bhij', qc, kc, jnp.exp(diff))
        o_intra = jnp.einsum('bhij,bhjv->bhiv', attn, vc)
        b_last = bcum[:, :, -1:, :]
        k_dec = kc * jnp.exp(b_last - bcum)
        state = state * jnp.exp(b_last[:, :, 0, :, None]) + jnp.einsum('bhjk,bhjv->bhkv', k_dec, vc)
        return state, o_inter + o_intra

    state0 = jnp.zeros((B, GLA_HEADS, GLA_DK, GLA_DV), jnp.float32)
    _, o = lax.scan(step, state0, (qh, kh, vh, lah))
    o = o.transpose(1, 0, 3, 2, 4).reshape(B, S, GLA_HEADS, GLA_DV)
    o = o * lax.rsqrt(jnp.mean(o * o, axis=-1, keepdims=True) + EPS)
    o = o * g_o.astype(jnp.float32).reshape(GLA_HEADS, GLA_DV)
    o = o.reshape(B, S, GLA_V_TOT) * jax.nn.silu(r)
    return jnp.einsum('bse,ed->bsd', o.astype(xn.dtype), w_o)

def shared_kv(h, g_kv, w_kv, b_f):
    B, S, _ = h.shape
    hn = rmsnorm(h, g_kv)
    p = jnp.einsum('bsd,de->bse', hn, w_kv)
    k, v, fl = jnp.split(p, KV_SPLITS, axis=-1)
    k = k.reshape(B, S, FOX_HEADS, FOX_HD).transpose(0, 2, 1, 3).astype(jnp.float32)
    v = v.reshape(B, S, FOX_HEADS, FOX_HD).transpose(0, 2, 1, 3).astype(jnp.float32)
    log_f = jax.nn.log_sigmoid(fl.astype(jnp.float32) + b_f.astype(jnp.float32))
    c = jnp.cumsum(log_f, axis=1).transpose(0, 2, 1)
    return k, v, c

def fox_mixer(hn, w_q, w_o, k, v, c):
    B, S, _ = hn.shape
    q = jnp.einsum('bsd,de->bse', hn, w_q).astype(jnp.float32)
    q = q.reshape(B, S, FOX_HEADS, FOX_HD).transpose(0, 2, 1, 3) * (FOX_HD ** -0.5)
    outs = []
    for blk in range(S // FOX_BLOCK):
        lo, hi = blk * FOX_BLOCK, (blk + 1) * FOX_BLOCK
        logits = jnp.einsum('bhqd,bhkd->bhqk', q[:, :, lo:hi], k[:, :, :hi])
        logits = logits + c[:, :, lo:hi, None] - c[:, :, None, :hi]
        mask = jnp.arange(lo, hi)[:, None] >= jnp.arange(hi)[None, :]
        probs = jax.nn.softmax(jnp.where(mask, logits, -jnp.inf), axis=-1)
        outs.append(jnp.einsum('bhqk,bhkd->bhqd', probs, v[:, :, :hi]))
    o = jnp.concatenate(outs, axis=2)
    o = o.transpose(0, 2, 1, 3).reshape(B, S, D_MODEL).astype(hn.dtype)
    return jnp.einsum('bse,ed->bsd', o, w_o)

def peer_ffn(xn, w_pq, sub_keys, u_tab, v_tab):
    B, S, D = xn.shape
    T = B * S
    xt = xn.reshape(T, D)
    q = jnp.einsum('td,de->te', xt, w_pq).reshape(T, PEER_HEADS, 2, PEER_DHALF)
    s = jnp.einsum('thcd,hcnd->thcn', q, sub_keys)
    s_top, i_top = lax.top_k(s, PEER_TOPK)
    cand = s_top[:, :, 0, :, None] + s_top[:, :, 1, None, :]
    cand_idx = i_top[:, :, 0, :, None] * PEER_KEYS + i_top[:, :, 1, None, :]
    best, pos = lax.top_k(cand.reshape(T, PEER_HEADS, PEER_TOPK * PEER_TOPK), PEER_TOPK)
    ids = jnp.take_along_axis(cand_idx.reshape(T, PEER_HEADS, PEER_TOPK * PEER_TOPK), pos, axis=-1)
    gates = jax.nn.softmax(best.astype(jnp.float32), axis=-1).astype(xn.dtype)
    n_chunks = T // PEER_CHUNK

    def expert_chunk(args):
        xc, idc, gc = args
        u = jnp.take(u_tab, idc, axis=0)
        a = jax.nn.gelu(jnp.einsum('cd,chkd->chk', xc, u), approximate=False)
        vv = jnp.take(v_tab, idc, axis=0)
        return jnp.einsum('chk,chkd->cd', gc * a, vv)

    out = lax.map(expert_chunk, (xt.reshape(n_chunks, PEER_CHUNK, D),
                                 ids.reshape(n_chunks, PEER_CHUNK, PEER_HEADS, PEER_TOPK),
                                 gates.reshape(n_chunks, PEER_CHUNK, PEER_HEADS, PEER_TOPK)))
    return out.reshape(B, S, D)

def setup_inputs(seed: int = 0) -> dict:
    key = jax.random.key(seed)
    ks = jax.random.split(key, 20)
    f32 = jnp.float32
    D = D_MODEL
    nrm = lambda k, shp, sc: jax.random.normal(k, shp, f32) * sc
    return {
        'x': nrm(ks[0], (BATCH, SEQ, D), 1.0),
        'norm_mix': 1.0 + nrm(ks[1], (DEPTH, D), 0.02),
        'norm_ffn': 1.0 + nrm(ks[2], (DEPTH, D), 0.02),
        'gla_w_in': nrm(ks[3], (N_A_LAYERS, D, GLA_IN_TOT), D ** -0.5),
        'gla_w_g2': nrm(ks[4], (N_A_LAYERS, GLA_GATE_RANK, GLA_QK_TOT), GLA_GATE_RANK ** -0.5),
        'gla_b_g': nrm(ks[5], (N_A_LAYERS, GLA_QK_TOT), 0.5),
        'gla_norm_o': 1.0 + nrm(ks[6], (N_A_LAYERS, GLA_V_TOT), 0.02),
        'gla_w_o': nrm(ks[7], (N_A_LAYERS, GLA_V_TOT, D), 0.5 * GLA_V_TOT ** -0.5),
        'kv_norm': 1.0 + nrm(ks[8], (D,), 0.02),
        'kv_w': nrm(ks[9], (D, KV_TOT), D ** -0.5),
        'fox_b_f': jax.random.uniform(ks[10], (FOX_HEADS,), f32, 1.0, 4.0),
        'fox_w_q': nrm(ks[11], (N_B_LAYERS, D, D), D ** -0.5),
        'fox_w_o': nrm(ks[12], (N_B_LAYERS, D, D), 0.5 * D ** -0.5),
        'peer_w_q': nrm(ks[13], (DEPTH, D, PEER_HEADS * PEER_DQ), D ** -0.5),
        'peer_sub_keys': nrm(ks[14], (DEPTH, PEER_HEADS, 2, PEER_KEYS, PEER_DHALF), PEER_DHALF ** -0.5),
        'peer_u': nrm(ks[15], (DEPTH, PEER_N, D), D ** -0.5),
        'peer_v': nrm(ks[16], (DEPTH, PEER_N, D), PEER_HEADS ** -0.5),
        'norm_final': 1.0 + nrm(ks[17], (D,), 0.02),
    }

def reference(x, norm_mix, norm_ffn, gla_w_in, gla_w_g2, gla_b_g, gla_norm_o, gla_w_o,
              kv_norm, kv_w, fox_b_f, fox_w_q, fox_w_o,
              peer_w_q, peer_sub_keys, peer_u, peer_v, norm_final):
    h = x
    k_sh = v_sh = c_sh = None
    for layer in range(DEPTH):
        hn = rmsnorm(h, norm_mix[layer])
        if layer < N_A_LAYERS:
            h = h + gla_mixer(hn, gla_w_in[layer], gla_w_g2[layer], gla_b_g[layer],
                              gla_norm_o[layer], gla_w_o[layer])
        else:
            if layer == N_A_LAYERS:
                k_sh, v_sh, c_sh = shared_kv(h, kv_norm, kv_w, fox_b_f)
            j = layer - N_A_LAYERS
            hn_q = hn
            h = h + fox_mixer(hn_q, fox_w_q[j], fox_w_o[j], k_sh, v_sh, c_sh)
        h = h + peer_ffn(rmsnorm(h, norm_ffn[layer]), peer_w_q[layer], peer_sub_keys[layer],
                         peer_u[layer], peer_v[layer])
    return rmsnorm(h, norm_final)


_drawn_inputs = setup_inputs


def setup_inputs(seed=0):
    import zlib

    import numpy as np

    out = dict(_drawn_inputs(seed))
    spreads = {}
    factors = {'kv_norm': 4.488, 'norm_final': 2.874}
    for name, (base, spread) in spreads.items():
        noise = np.random.default_rng([zlib.crc32(name.encode()), seed]).standard_normal(out[name].shape)
        drawn = base * np.exp(spread * noise) if base else spread * noise
        out[name] = __import__('jax').numpy.asarray(drawn.astype(out[name].dtype))
    for name, factor in factors.items():
        out[name] = (out[name] * factor).astype(out[name].dtype)
    return out
```

```python
from contextlib import ExitStack

import concourse.bass as bass
from concourse import mybir

F32 = mybir.dt.float32
BF16 = mybir.dt.bfloat16
U32 = mybir.dt.uint32
U8 = mybir.dt.uint8
ALU = mybir.AluOpType
ACT = mybir.ActivationFunctionType
AX_X = mybir.AxisListType.X

P = 128
D = 1024
KC = D // P
HALF = 512
TILES = 2
EPS = 1e-6
LOW = -3.0e38

GH, GDK, GDV, GRANK, GTAU = 4, 128, 256, 16, 16.0
LEVELS = 8
FH, FHD = 16, 64
RH, RK, RTOP = 8, 128, 16
EXPERTS = RK * RK
SLOTS = RH * RTOP

RING = 8
SUB = 4
ISSUE = 2
ROUNDS = SLOTS // RING
GROUPS = 8
PHASES = [(layer, b) for layer in range(2) for b in range(TILES)]

WCOLS = 256
NW = 3


def weight_blocks(a):
    w_in, w_kv = a["gla_w_in"][0], a["kv_w"]
    out = [("gain", ("mix", 0), a["norm_mix"][0:1, :])]

    def cols(key, w, first, n):
        for i in range(0, n, WCOLS):
            out.append(("w", (key, i // WCOLS), w[:, first + i:first + min(i + WCOLS, n)]))

    cols("glr", w_in, 3 * D, GRANK)
    cols("q", w_in, 0, HALF)
    cols("k", w_in, HALF, HALF)
    cols("v", w_in, D, D)
    out.append(("gain", ("go",), a["gla_norm_o"][0:1, :]))
    cols("r", w_in, 2 * D, D)
    out.append(("keys", (("keys", 0), 0), a["peer_sub_keys"][0]))
    out.append(("gain", ("ffn", 0), a["norm_ffn"][0:1, :]))
    for b in range(TILES):
        cols(("wo", 0, b), a["gla_w_o"][0], 0, D)
        cols(("pq", 0, b), a["peer_w_q"][0], 0, 2 * D)
    out.append(("keys", (("keys", 1), 0), a["peer_sub_keys"][1]))
    for b in range(TILES):
        out.append(("gain", ("kv", b), a["kv_norm"].rearrange("(o d) -> o d", o=1)))
        cols(("K", b), w_kv, 0, D)
        out.append(("gain", ("mix1", b), a["norm_mix"][1:2, :]))
        cols(("V", b), w_kv, D, D)
        cols(("fl", b), w_kv, 2 * D, FH)
        cols(("Q", b), a["fox_w_q"][0], 0, D)
        out.append(("gain", ("ffn1", b), a["norm_ffn"][1:2, :]))
        cols(("wo", 1, b), a["fox_w_o"][0], 0, D)
        cols(("pq", 1, b), a["peer_w_q"][1], 0, 2 * D)
    out.append(("gain", ("final",), a["norm_final"].rearrange("(o d) -> o d", o=1)))
    return out


def pair_uses():
    out = [("T", "mix0", 0), ("T", "mix0", 1), "glr", "z", "q", "k", ("v", 0), ("v", 1), ("r", 0), ("r", 1),
           ("keys", 0, 0), ("keys", 0, 1)]

    def route(layer, b):
        return [("T", f"ffn{layer}", b)] + [("route", layer, b, j) for j in range(4)]

    for b in range(TILES):
        if b == 0:
            out += ["kdec", "state"]
        out += [("level", b, i) for i in range(LEVELS)] + [("o", b), ("T", "o0", b), ("wo", 0, b)] + route(0, b)
    out += [("keys", 1, 0), ("keys", 1, 1)]
    for b in range(TILES):
        out += [("T", "kv", b), ("K", b), ("V", b), ("fl", b), ("T", "mix1", b), ("Q", b)]
        out += [("att", b, c) for c in range(FH // 2)]
        out += [("T", "o1", b), ("wo", 1, b)] + route(1, b)
    return out


T_USES = [("mix0", 0), ("mix0", 1), ("o0", 0), ("ffn0", 0), ("o0", 1), ("ffn0", 1)]
for _b in range(TILES):
    T_USES += [("kv", _b), ("mix1", _b), ("o1", _b), ("ffn1", _b)]
NORMS = [("mix0", 0), ("mix0", 1), ("ffn0", 0), ("ffn0", 1), ("kv", 0), ("ffn1", 0), ("kv", 1), ("ffn1", 1),
         ("final", 0), ("final", 1)]
GAIN_OF = {("mix0", 0): 0, ("mix0", 1): 0, ("ffn0", 0): 2, ("ffn0", 1): 2, ("kv", 0): 3, ("mix1", 0): 4,
           ("ffn1", 0): 5, ("kv", 1): 6, ("mix1", 1): 7, ("ffn1", 1): 8, ("final", 0): 9, ("final", 1): 9}
GAIN_LAST = {("mix0", 1), ("ffn0", 1), ("kv", 0), ("mix1", 0), ("ffn1", 0), ("kv", 1), ("mix1", 1), ("ffn1", 1)}
H_VERSIONS = [("mixed", 0, 0), ("mixed", 0, 1), ("done", 0, 0), ("mixed", 1, 0), ("done", 0, 1), ("mixed", 1, 1),
              ("done", 1, 0), ("done", 1, 1)]
H_OF_NORM = {("ffn0", 0): ("mixed", 0, 0), ("ffn0", 1): ("mixed", 0, 1), ("kv", 0): ("done", 0, 0),
             ("ffn1", 0): ("mixed", 1, 0), ("kv", 1): ("done", 0, 1), ("ffn1", 1): ("mixed", 1, 1),
             ("final", 0): ("done", 1, 0), ("final", 1): ("done", 1, 1)}


def yoco_kernel(nc, a, out):
    STREAM = weight_blocks(a)
    BLOCK_OF = {e[1]: i for i, e in enumerate(x for x in STREAM if x[0] != "gain")}
    PAIR_USE = {key: u for u, key in enumerate(pair_uses())}

    with ExitStack() as ctx:
        def sb(name, shape, dt=F32):
            return ctx.enter_context(nc.sbuf_tensor(name, shape, dt))

        def sem(name):
            return ctx.enter_context(nc.semaphore(name))

        h = sb("h", [P, TILES, D])
        xn = sb("xn", [P, TILES, D])
        rows = sb("rows", [P, D])
        xT = sb("xT", [P, 2, KC, P])
        gain = sb("gain", [P, D])
        wbuf = sb("wbuf", [P, NW, KC, WCOLS])
        u_ring = sb("u_ring", [P, RING, D])
        v_ring = sb("v_ring", [P, RING, D])
        square = sb("square", [P, D], BF16)
        ident = sb("ident", [P, P])
        ident16 = sb("ident16", [P, P], BF16)
        zeros16 = sb("zeros16", [P, HALF], BF16)
        causal16 = sb("causal16", [P, P], BF16)
        ones = sb("ones", [P, P])
        eps = sb("eps", [P, 1])
        sumsq = sb("sumsq", [P, len(NORMS)])
        rms = sb("rms", [P, len(NORMS)])
        rstd = sb("rstd", [P, len(NORMS)])
        qkT = sb("qkT", [P, TILES, 2, GH, P])
        vtok = sb("vtok", [P, TILES, D])
        gate_o = sb("gate_o", [P, TILES, D])
        glrT = sb("glrT", [GRANK, TILES * P])
        w_g2 = sb("w_g2", [GRANK, GH * GDK])
        b_g = sb("b_g", [P, GH])
        decay = sb("decay", [P, TILES, GH, P])
        scratch = sb("scratch", [P, 4096])
        masks = sb("masks", [P, LEVELS, P], U8)
        attnT = sb("attnT", [P, GH, P])
        kdec = sb("kdec", [P, GH, P])
        state = sb("state", [P, GH, GDV])
        head_ss = sb("head_ss", [P, TILES, GH])
        head_rms = sb("head_rms", [P, TILES, GH])
        head_rstd = sb("head_rstd", [P, TILES, GH])
        b_f = sb("b_f", [FH, 1])
        forget = sb("forget", [FH, 4, P])
        cumT = sb("cumT", [FH, TILES * P])
        neg_cumT = sb("neg_cumT", [FH, TILES * P])
        neg_max = sb("neg_max", [P, TILES, FH])
        prob_sum = sb("prob_sum", [P, TILES, FH])
        prob_inv = sb("prob_inv", [P, TILES, FH])
        keysT = sb("keysT", [P, 2 * RH, RK])
        queryT = sb("queryT", [P, 4, P])
        top = sb("top", [P, 4, RTOP])
        top_at = sb("top_at", [P, 4, RTOP], U32)
        top_id = sb("top_id", [P, 4, RTOP])
        best = sb("best", [P, TILES, RH, RTOP])
        best_at = sb("best_at", [P, 2, RTOP], U32)
        digit = sb("digit", [P, 2, 2 * RTOP], U32)
        picked = sb("picked", [P, 2, 2 * RTOP])
        ids_f = sb("ids_f", [P, 2 * RTOP])
        iota16 = sb("iota16", [P, RTOP])
        ids = sb("ids", [P, TILES, SLOTS], U32)
        gates = sb("gates", [P, TILES, SLOTS])
        gate_e = sb("gate_e", [P, SLOTS])
        gate_sum = sb("gate_sum", [P, RH])
        gate_inv = sb("gate_inv", [P, RH])
        row_ids = sb("row_ids", [P, RING], U32)
        dots = sb("dots", [P, RING])
        gelus = sb("gelus", [P, RING])
        weights_s = sb("weights_s", [P, RING])
        diag = sb("diag", [P, RING, P])

        q2T = [gate_o[:, g, :].rearrange("p (c t) -> p c t", c=KC) for g in range(2)]
        v2 = vtok

        acc = ctx.enter_context(nc.psum_tensor("acc", [P, 2, HALF], F32))
        pairs = [ctx.enter_context(nc.psum_tensor(f"pair{i}", [P, 2, HALF], F32)) for i in range(3)]

        def flat(t):
            return t[:, :, :].rearrange("p a b -> p (a b)")

        x_loaded = [sem(f"x_loaded{b}") for b in range(TILES)]
        small_loaded = sem("small_loaded")
        gain_loaded, gain_used = sem("gain_loaded"), sem("gain_used")
        w_loaded = [sem(f"w_loaded{i}") for i in range(NW)]
        w_used = sem("w_used")
        consts = sem("consts")
        masks_f_ready, masks_ready = sem("masks_f_ready"), sem("masks_ready")
        pair_full = [sem(f"pair_full{i}") for i in range(3)]
        pair_free = [sem(f"pair_free{i}") for i in range(3)]
        dve_step, act_step = sem("dve_step"), sem("act_step")
        dve_const = sem("dve_const")
        h_ready = sem("h_ready")
        rms_ready = sem("rms_ready")
        q_zeroed = sem("q_zeroed")
        rows_ready = sem("rows_ready")
        z_ready, z_exp_ready, z_log_ready = sem("z_ready"), sem("z_exp_ready"), sem("z_log_ready")
        z_abs_ready = sem("z_abs_ready")
        diff_ready, fade_ready, faded_ready = sem("diff_ready"), sem("fade_ready"), sem("faded_ready")
        attn_ready = sem("attn_ready")
        head_ss_ready = sem("head_ss_ready")
        silu_ready = sem("silu_ready")
        f_abs_ready, f_log_ready, cum_ready = sem("f_abs_ready"), sem("f_log_ready"), sem("cum_ready")
        max_ready, probs_ready, probsT_full, probsT_ready = (sem("max_ready"), sem("probs_ready"),
                                                              sem("probsT_full"), sem("probsT_ready"))
        pv_full = sem("pv_full")
        queryT_full, queryT_ready = sem("queryT_full"), sem("queryT_ready")
        gate_x_ready, gate_e_ready, routed = sem("gate_x_ready"), sem("gate_e_ready"), sem("routed")
        keys_ready = sem("keys_ready")
        ids_laid, issued = sem("ids_laid"), sem("issued")
        u_loaded = [sem(f"u_loaded{j}") for j in range(RING)]
        v_loaded = [sem(f"v_loaded{j}") for j in range(RING)]
        u_free, v_free = sem("u_free"), sem("v_free")
        dots_free = sem("dots_free")
        gelu_ready = sem("gelu_ready")
        diag_ready = sem("diag_ready")
        acc_full, acc_free = sem("acc_full"), sem("acc_free")
        out_ready, out_stored = sem("out_ready"), sem("out_stored")

        def pair_of(key):
            return pairs[PAIR_USE[key] % 3]

        def full(key):
            u = PAIR_USE[key]
            assert not of_weights(key)
            return pair_full[u % 3], sum(v % 3 == u % 3 and v <= u and not of_weights(k) for k, v in PAIR_USE.items())

        def freed(key):
            u = PAIR_USE[key]
            return pair_free[u % 3], u // 3 + 1

        def frees(key, ins):
            ins.then_inc(pair_free[PAIR_USE[key] % 3], 1)

        def of_weights(key):
            name = key if isinstance(key, str) else key[0]
            return name in ("glr", "q", "k", "v", "r", "wo", "K", "V", "fl", "Q")

        def multiplied(key):
            return w_used, BLOCK_OF[key] + 1

        def t_at(key):
            return T_USES.index(key)

        def version(key):
            return h_ready, H_VERSIONS.index(key) + 1

        block = ctx.enter_context(nc.Block())

        @block.sync
        def _(sp):
            for b in range(TILES):
                sp.dma_start(h[:, b, :], a["x"][0, b * P:(b + 1) * P, :]).then_inc(x_loaded[b], 16)
            n_gain = n_block = 0
            for kind, key, src in STREAM:
                if kind == "gain":
                    if n_gain:
                        sp.wait_ge(gain_used, n_gain)
                    sp.dma_start(gain[:, :], src.broadcast_to([P, D])).then_inc(gain_loaded, 16)
                    n_gain += 1
                else:
                    if n_block >= NW:
                        sp.wait_ge(w_used, n_block - NW + 1)
                    at = n_block % NW
                    if kind == "keys":
                        dst = wbuf[:, at, :, :].rearrange("p c n -> p (c n)").rearrange("p (g d) -> p g d", d=RK)
                        sp.dma_start(dst, src.rearrange("h c n d -> n (h c) d")).then_inc(w_loaded[at], 16)
                    else:
                        sp.dma_start(wbuf[:, at, :, 0:src.shape[1]],
                                     src.rearrange("(c p) n -> p c n", p=P)).then_inc(w_loaded[at], 16)
                    n_block += 1
                    if n_block == 1:
                        sp.dma_start(w_g2[:, :], a["gla_w_g2"][0]).then_inc(small_loaded, 16)
                        with nc.allow_non_contiguous_dma(reason="640 numbers"):
                            sp.dma_start(b_g[:, :], a["gla_b_g"][0].rearrange("(h k) -> k h", k=GDK)
                                         ).then_inc(small_loaded, 16)
                            sp.dma_start(b_f[:, :], a["fox_b_f"].rearrange("(h o) -> h o", o=1)
                                         ).then_inc(small_loaded, 16)
            for b in range(TILES):
                sp.wait_ge(out_ready, b + 1)
                sp.dma_start(out[0, b * P:(b + 1) * P, :], xn[:, b, :]).then_inc(out_stored, 16)
            sp.wait_ge(out_stored, 16 * TILES)

        @block.gpsimd
        def _(pool):
            made = 0

            def chained(ins):
                nonlocal made
                made += 1
                ins.then_inc(consts, 1)
                pool.wait_ge(consts, made)

            nc.gpsimd.memset(zeros16[:, :], 0.0)
            nc.gpsimd.memset(ones[:, :], 1.0)
            nc.gpsimd.memset(eps[:, :], EPS)
            nc.gpsimd.memset(causal16[:, :], 0.0)
            nc.gpsimd.iota(iota16[:, :], pattern=[[1, RTOP]], base=0, channel_multiplier=0,
                           allow_small_or_imprecise_dtypes=True)
            nc.gpsimd.memset(ident16[:, :], 0.0)
            chained(nc.gpsimd.memset(ident[:, :], 0.0))
            nc.gpsimd.affine_select(out=ident16[:, :], in_=ident16[:, :], compare_op=ALU.not_equal, fill=1.0,
                                    base=0, pattern=[[-1, P]], channel_multiplier=1)
            chained(nc.gpsimd.affine_select(out=ident[:, :], in_=ident[:, :], compare_op=ALU.not_equal, fill=1.0,
                                            base=0, pattern=[[-1, P]], channel_multiplier=1))
            nc.gpsimd.affine_select(out=causal16[:, :], in_=causal16[:, :], compare_op=ALU.is_ge, fill=-1.0e38,
                                    base=0, pattern=[[-1, P]], channel_multiplier=1)
            mf = scratch[:, 0:LEVELS * P].rearrange("p (l t) -> p l t", l=LEVELS)
            chained(nc.gpsimd.memset(mf, 1.0))
            for i in range(LEVELS - 1):
                m = P >> (i + 1)
                v = mf[:, i, :].rearrange("p (n c) -> p n c", c=2 * m)
                n = P // (2 * m)
                chained(nc.gpsimd.affine_select(out=v, in_=v, compare_op=ALU.is_ge, fill=0.0, base=0,
                                                pattern=[[-2 * m, n], [0, 2 * m]], channel_multiplier=1))
                chained(nc.gpsimd.affine_select(out=v, in_=v, compare_op=ALU.is_ge, fill=0.0, base=m - 1,
                                                pattern=[[2 * m, n], [0, 2 * m]], channel_multiplier=-1))
                chained(nc.gpsimd.affine_select(out=v, in_=v, compare_op=ALU.is_ge, fill=0.0, base=-m,
                                                pattern=[[0, n], [1, 2 * m]], channel_multiplier=0))
            nc.gpsimd.affine_select(out=mf[:, LEVELS - 1, :], in_=mf[:, LEVELS - 1, :], compare_op=ALU.is_equal,
                                    fill=0.0, base=0, pattern=[[-1, P]], channel_multiplier=1
                                    ).then_inc(masks_f_ready, 1)
            u_rows = a["peer_u"].rearrange("l n d -> (l n) d")
            v_rows = a["peer_v"].rearrange("l n d -> (l n) d")
            for ph, (layer, b) in enumerate(PHASES):
                pool.wait_ge(routed, ph + 1)
                with pool.Fori(ph * ROUNDS, (ph + 1) * ROUNDS) as r:
                    for q in range(RING // ISSUE):
                        j0 = q * ISSUE
                        pool.wait_ge(u_free, r * RING + (j0 + ISSUE))
                        pool.sem_inc(issued, 1)
                        pool.wait_ge(v_free, r * RING + (j0 + ISSUE))
                        pool.sem_inc(issued, 1)
                        nc.gpsimd.tensor_copy(
                            row_ids[:, j0:j0 + ISSUE],
                            ids[:, b, bass.ds(r * RING + (j0 - ph * SLOTS), ISSUE)]).then_inc(ids_laid, 1)
                        pool.wait_ge(ids_laid, r * (RING // ISSUE) + (q + 1))
                        pool.sem_inc(issued, 1)
                        for j in range(j0, j0 + ISSUE):
                            at = bass.IndirectOffsetOnAxis(ap=row_ids[:, j:j + 1], axis=0)
                            pool.indirect_dma_start(u_ring[:, j, :], None, u_rows, at).then_inc(u_loaded[j], 16)
                            pool.indirect_dma_start(v_ring[:, j, :], None, v_rows, at).then_inc(v_loaded[j], 16)

        @block.vector
        def _(dve):
            steps = 0

            def chained(ins):
                nonlocal steps
                steps += 1
                ins.then_inc(dve_step, 1)
                dve.wait_ge(dve_step, steps)

            def norm(key, dst, n):
                b = key[1]
                g = GAIN_OF[key]
                dve.wait_ge(rms_ready, n + 1)
                if key[0] != "mix1":
                    chained(nc.vector.reciprocal(rstd[:, n:n + 1], rms[:, n:n + 1]))
                dve.wait_ge(gain_loaded, 16 * (g + 1))
                nc.vector.scalar_tensor_tensor(out=dst, in0=h[:, b, :], scalar=rstd[:, n:n + 1], in1=gain[:, :],
                                               op0=ALU.mult, op1=ALU.mult
                                               ).then_inc(rows_ready if key[0] != "final" else out_ready, 1)
                if key in GAIN_LAST:
                    if key in T_USES:
                        dve.wait_ge(rows_ready, t_at(key) + 1)
                    dve.sem_inc(gain_used, 1)

            def level_refs(b, m):
                s = decay[:, b, :, :].rearrange("p h (n c) -> p (h n) c", c=2 * m)
                return s, s[:, :, m - 1:m].broadcast_to([P, GH * P // (2 * m), m])

            def level_diff(b, i):
                m = P >> (i + 1)
                s, ref = level_refs(b, m)
                d = scratch[:, (i % 2) * HALF:(i % 2 + 1) * HALF].rearrange("p (n c) -> p n c", c=2 * m)
                if i >= 2:
                    dve.wait_ge(faded_ready, b * (LEVELS - 1) + i - 1)
                nc.vector.tensor_tensor(d[:, :, 0:m], ref, s[:, :, 0:m], ALU.subtract)
                nc.vector.tensor_tensor(d[:, :, m:2 * m], s[:, :, m:2 * m], ref, ALU.subtract
                                        ).then_inc(diff_ready, 1)

            def level_apply(b, i):
                m = P >> (i + 1)
                e = scratch[:, (i % 2) * HALF:(i % 2 + 1) * HALF].rearrange("p (n c) -> p n c", c=2 * m)
                x = scratch[:, D + (i % 2) * HALF:D + (i % 2 + 1) * HALF].rearrange("p (n c) -> p n c", c=2 * m)
                kk = qkT[:, b, 1, :, :].rearrange("p h (n c) -> p (h n) c", c=2 * m)
                qq = qkT[:, b, 0, :, :].rearrange("p h (n c) -> p (h n) c", c=2 * m)
                dve.wait_ge(fade_ready, fades(b, i))
                if i >= 2:
                    dve.wait_ge(*full(("level", b, i - 2)))
                nc.vector.tensor_tensor(x[:, :, 0:m], kk[:, :, 0:m], e[:, :, 0:m], ALU.mult)
                nc.vector.tensor_tensor(x[:, :, m:2 * m], qq[:, :, m:2 * m], e[:, :, m:2 * m], ALU.mult
                                        ).then_inc(faded_ready, 1)

            def level_take(b, i):
                key = ("level", b, i)
                dve.wait_ge(*full(key))
                ins = nc.vector.copy_predicated(attnT[:, :, :],
                                                masks[:, i, :].unsqueeze(1).broadcast_to([P, GH, P]),
                                                pair_of(key)[:, 0, :].rearrange("p (h t) -> p h t", h=GH))
                frees(key, ins)
                dve.wait_ge(*freed(key))

            def fades(b, i):
                return b * (LEVELS - 1) + i + 1

            def levels(b, first, last):
                if first == 0:
                    if b:
                        dve.wait_ge(*full(("o", b - 1)))
                    chained(nc.vector.memset(attnT[:, :, :], 0.0))
                    level_diff(b, 0)
                for i in range(first, last):
                    if i + 1 < LEVELS - 1:
                        level_diff(b, i + 1)
                    if i < LEVELS - 1:
                        level_apply(b, i)
                    if i:
                        level_take(b, i - 1)
                if last == LEVELS:
                    level_take(b, LEVELS - 1)
                    dve.sem_inc(attn_ready, 1)

            def gla_out(b):
                key = ("o", b)
                dve.wait_ge(head_ss_ready, b + 1)
                chained(nc.vector.reciprocal(head_rstd[:, b, :], head_rms[:, b, :]))
                dve.wait_ge(*full(("T", "mix0", 1) if b == 0 else ("T", "o0", 0)))
                o = flat(pair_of(key))
                for g in range(GH):
                    c = slice(g * GDV, (g + 1) * GDV)
                    ins = nc.vector.scalar_tensor_tensor(out=rows[:, c], in0=o[:, c], scalar=head_rstd[:, b, g:g + 1],
                                                         in1=gate_o[:, b, c], op0=ALU.mult, op1=ALU.mult)
                frees(key, ins)
                dve.wait_ge(*freed(key))
                dve.sem_inc(rows_ready, 1)

            def residual(layer, b):
                key = ("wo", layer, b)
                dve.wait_ge(*multiplied((key, 3)))
                frees(key, nc.vector.tensor_tensor(h[:, b, :], h[:, b, :], flat(pair_of(key)), ALU.add))
                dve.wait_ge(*freed(key))
                dve.sem_inc(h_ready, 1)

            def top16(src, n, groups, vals, at, work):
                for g in range(groups):
                    ins = nc.vector.max(vals[:, g, 0:8], src[:, g, :])
                chained(ins)
                for g in range(groups):
                    nc.vector.max_index(at[:, g, 0:8], vals[:, g, 0:8], src[:, g, :])
                    ins = nc.vector.match_replace(work[:, g, :], vals[:, g, 0:8], src[:, g, :], LOW)
                chained(ins)
                for g in range(groups):
                    ins = nc.vector.max(vals[:, g, 8:16], work[:, g, :])
                chained(ins)
                for g in range(groups):
                    ins = nc.vector.max_index(at[:, g, 8:16], vals[:, g, 8:16], work[:, g, :])
                return ins

            def route(layer, b, j):
                key = ("route", layer, b, j)
                dve.wait_ge(*full(key))
                s = pair_of(key)[:, 1, :].rearrange("p (g n) -> p g n", g=4)
                work = scratch[:, 0:HALF].rearrange("p (g n) -> p g n", g=4)
                ins = top16(s, RK, 4, top, top_at, work)
                frees(key, ins)
                dve.wait_ge(*freed(key))
                nc.vector.tensor_copy(top_id[:, :, :], top_at[:, :, :])
                cand = scratch[:, HALF:2 * HALF].rearrange("p (g i j) -> p g i j", g=2, i=RTOP)
                tv = top[:, :, :].rearrange("p (g c) k -> p g c k", c=2)
                chained(nc.vector.tensor_tensor(cand, tv[:, :, 0, :].unsqueeze(3).broadcast_to([P, 2, RTOP, RTOP]),
                                                tv[:, :, 1, :].unsqueeze(2).broadcast_to([P, 2, RTOP, RTOP]),
                                                ALU.add))
                cv = scratch[:, HALF:2 * HALF].rearrange("p (g n) -> p g n", g=2)
                if j == 0 and (layer, b) != (0, 0):
                    dve.wait_ge(gate_e_ready, layer * TILES + b)
                chained(top16(cv, RTOP * RTOP, 2, best[:, b, 2 * j:2 * j + 2, :], best_at,
                              scratch[:, 2 * HALF:3 * HALF].rearrange("p (g n) -> p g n", g=2)))
                at = best_at[:, :, :].rearrange("p g k -> p (g k)")
                nc.vector.tensor_scalar(digit[:, 0, :], at, 4, None, ALU.logical_shift_right)
                chained(nc.vector.tensor_scalar(digit[:, 1, :], at, RTOP - 1, None, ALU.bitwise_and))
                hot = scratch[:, 3 * HALF:5 * HALF].rearrange("p (c s k) -> p c s k", c=2, k=RTOP)
                ti = top_id[:, :, :].rearrange("p (g c) k -> p g c k", c=2)
                for c in range(2):
                    ins = nc.vector.tensor_tensor(
                        hot[:, c, :, :], iota16[:, :].unsqueeze(1).broadcast_to([P, 2 * RTOP, RTOP]),
                        digit[:, c, :].unsqueeze(2).broadcast_to([P, 2 * RTOP, RTOP]), ALU.is_equal)
                chained(ins)
                for c in range(2):
                    hc = hot[:, c, :, :].rearrange("p (g s) k -> p g s k", g=2)
                    ins = nc.vector.tensor_tensor(
                        hc, hc, ti[:, :, c, :].unsqueeze(2).broadcast_to([P, 2, RTOP, RTOP]), ALU.mult)
                chained(ins)
                chained(nc.vector.tensor_reduce(picked[:, :, :].rearrange("p c s -> p (c s)"),
                                                hot.rearrange("p c s k -> p (c s) k"), AX_X, ALU.add))
                chained(nc.vector.scalar_tensor_tensor(out=ids_f[:, :], in0=picked[:, 0, :], scalar=float(RK),
                                                       in1=picked[:, 1, :], op0=ALU.mult, op1=ALU.add))
                chained(nc.vector.tensor_scalar(ids[:, b, j * 2 * RTOP:(j + 1) * 2 * RTOP], ids_f[:, :],
                                                float(layer * EXPERTS), None, ALU.add))

            def gating(layer, b):
                n = layer * TILES + b
                e = gate_e[:, :].rearrange("p (h k) -> p h k", h=RH)
                nc.vector.tensor_tensor(e, best[:, b, :, :],
                                        best[:, b, :, 0:1].broadcast_to([P, RH, RTOP]), ALU.subtract
                                        ).then_inc(gate_x_ready, 1)
                dve.wait_ge(gate_e_ready, n + 1)
                chained(nc.vector.tensor_reduce(gate_sum[:, :], e, AX_X, ALU.add))
                chained(nc.vector.reciprocal(gate_inv[:, :], gate_sum[:, :]))
                nc.vector.tensor_tensor(gates[:, b, :].rearrange("p (h k) -> p h k", h=RH), e,
                                        gate_inv[:, :].unsqueeze(2).broadcast_to([P, RH, RTOP]), ALU.mult
                                        ).then_inc(routed, 1)
                dve.wait_ge(routed, n + 1)

            def forget_gate(b):
                key = ("fl", b)
                z = pair_of(key)[0:FH, 0, 0:P]
                dve.wait_ge(*multiplied((key, 0)))
                dve.wait_ge(f_abs_ready, b + 1)
                ins = nc.vector.tensor_scalar(forget[:, 1, :], z, b_f[:, 0:1], 0.0, ALU.add, ALU.min)
                frees(key, ins)
                dve.wait_ge(*freed(key))
                dve.wait_ge(f_log_ready, b + 1)
                chained(nc.vector.tensor_tensor(forget[:, 3, :], forget[:, 1, :], forget[:, 2, :], ALU.subtract))
                t = slice(b * P, (b + 1) * P)
                chained(nc.vector.tensor_tensor_scan(cumT[:, t], ones[0:FH, :], forget[:, 3, :],
                                                     cumT[:, b * P - 1:b * P] if b else 0.0, ALU.mult, ALU.add))
                nc.vector.tensor_scalar(neg_cumT[:, t], cumT[:, t], -1.0, None, ALU.mult).then_inc(cum_ready, 1)

            def att_max(b, c):
                key = ("att", b, c)
                dve.wait_ge(*full(key))
                n = (b + 1) * P
                s = pair_of(key)[:, 0, 0:2 * n].rearrange("p (g s) -> p g s", g=2)
                nc.vector.tensor_reduce(neg_max[:, b, 2 * c:2 * c + 2], s, AX_X, ALU.max, negate=True
                                        ).then_inc(max_ready, 1)

            def att_norm(b, c):
                key = ("att", b, c)
                n = b * (FH // 2) + c
                dve.wait_ge(probs_ready, n + 1)
                chained(nc.vector.reciprocal(prob_inv[:, b, 2 * c:2 * c + 2], prob_sum[:, b, 2 * c:2 * c + 2]))
                dve.wait_ge(pv_full, n + 1)
                if c == 0:
                    dve.wait_ge(*full(("T", "mix1", b)))
                ins = nc.vector.tensor_tensor(
                    rows[:, c * P:(c + 1) * P].rearrange("p (g d) -> p g d", g=2),
                    pair_of(key)[:, 0, 0:P].rearrange("p (g d) -> p g d", g=2),
                    prob_inv[:, b, 2 * c:2 * c + 2].unsqueeze(2).broadcast_to([P, 2, FHD]), ALU.mult)
                frees(key, ins)
                if c == FH // 2 - 1:
                    dve.wait_ge(*freed(key))
                    dve.sem_inc(rows_ready, 1)

            def attention(b, first, last):
                for i in range(first, last):
                    if i < FH // 2:
                        att_max(b, i)
                    if i >= 2:
                        att_norm(b, i - 2)

            def experts(ph, first, last):
                layer, b = PHASES[ph]
                with dve.Fori(ph * ROUNDS + first, ph * ROUNDS + last) as r:
                    for q in range(RING // SUB):
                        dve.wait_ge(dots_free, r * (RING // SUB) + (q + 1))
                        for j in range(q * SUB, (q + 1) * SUB):
                            dve.wait_ge(u_loaded[j], r * 16 + 16)
                            nc.vector.tensor_tensor_reduce(
                                out=u_ring[:, j, :], in0=u_ring[:, j, :], in1=xn[:, b, :], scale=1.0, scalar=0.0,
                                op0=ALU.mult, op1=ALU.add, accum_out=dots[:, j:j + 1]).then_inc(u_free, 1)

            def experts_end(ph):
                layer, b = PHASES[ph]
                dve.wait_ge(acc_full, ph + 1)
                nc.vector.tensor_copy(h[:, b, :], flat(acc)).then_inc(acc_free, 1)
                dve.wait_ge(acc_free, ph + 1)
                dve.sem_inc(h_ready, 1)

            dve.sem_inc(u_free, RING)
            dve.wait_ge(masks_f_ready, 1)
            nc.vector.tensor_copy(masks[:, :, :], scratch[:, 0:LEVELS * P].rearrange("p (l t) -> p l t", l=LEVELS)
                                  ).then_inc(masks_ready, 1)
            dve.wait_ge(x_loaded[0], 16)
            norm(("mix0", 0), rows[:, :], 0)
            dve.wait_ge(*full(("T", "mix0", 0)))
            dve.wait_ge(x_loaded[1], 16)
            norm(("mix0", 1), rows[:, :], 1)
            dve.wait_ge(small_loaded, 48)
            dve.wait_ge(*full("z"))
            zp = flat(pair_of("z")).rearrange("p (h b t) -> p h b t", h=GH, b=TILES)
            dve.wait_ge(z_abs_ready, 1)
            zm = scratch[:, 2 * D:3 * D].rearrange("p (b h t) -> p b h t", b=TILES, h=GH)
            for g in range(GH):
                ins = nc.vector.tensor_scalar(zm[:, :, g, :], zp[:, g, :, :], b_g[:, g:g + 1], 0.0, ALU.add, ALU.min)
            frees("z", ins)
            dve.wait_ge(*freed("z"))
            dve.wait_ge(z_log_ready, 1)
            dflat = decay[:, :, :, :].rearrange("p b h t -> p (b h t)")
            chained(nc.vector.tensor_tensor(dflat, scratch[:, 2 * D:3 * D], scratch[:, D:2 * D], ALU.subtract))
            chained(nc.vector.tensor_scalar(dflat, dflat, 1.0 / GTAU, None, ALU.mult))
            for b in range(TILES):
                for g in range(GH):
                    t = scratch[:, 3 * D + (b * GH + g) * P:3 * D + (b * GH + g + 1) * P]
                    ins = nc.vector.tensor_tensor_scan(t, ones[:, :], decay[:, b, g, :], 0.0, ALU.mult, ALU.add)
            chained(ins)
            chained(nc.vector.tensor_copy(dflat, scratch[:, 3 * D:4 * D]))
            kd = scratch[:, 3 * D:3 * D + HALF].rearrange("p (h t) -> p h t", h=GH)
            nc.vector.tensor_tensor(kd, decay[:, 0, :, P - 1:P].broadcast_to([P, GH, P]), decay[:, 0, :, :],
                                    ALU.subtract).then_inc(z_ready, 1)
            dve.wait_ge(z_exp_ready, 1)
            dve.wait_ge(*freed("k"))
            nc.vector.tensor_tensor(kd, kd, qkT[:, 0, 1, :, :], ALU.mult).then_inc(z_ready, 1)
            for b in range(TILES):
                dve.wait_ge(silu_ready, b + 1)
                dve.wait_ge(gain_loaded, 32)
                chained(nc.vector.tensor_tensor(gate_o[:, b, :], gate_o[:, b, :], gain[:, :], ALU.mult))
            dve.sem_inc(gain_used, 1)

            def gla_piece(b, i):
                if i == 0:
                    levels(b, 0, 3)
                elif i == 1:
                    levels(b, 3, 6)
                elif i == 2:
                    levels(b, 6, 8)
                    if b:
                        dve.wait_ge(z_exp_ready, 2)
                        qf = scratch[:, 3 * D:3 * D + HALF].rearrange("p (h t) -> p h t", h=GH)
                        nc.vector.tensor_tensor(qf, qf, qkT[:, 1, 0, :, :], ALU.mult).then_inc(z_ready, 1)
                    gla_out(b)
                elif i == 3:
                    residual(0, b)
                    norm(("ffn0", b), xn[:, b, :], NORMS.index(("ffn0", b)))
                elif i < 8:
                    route(0, b, i - 4)
                    if i == 7:
                        gating(0, b)

            def fox_piece(b, i):
                if i == 0:
                    if b == 0:
                        nc.vector.memset(gate_o[FHD:P, 0, :], 0.0)
                        nc.vector.memset(gate_o[0:FHD, 1, :], 0.0).then_inc(q_zeroed, 1)
                    norm(("kv", b), rows[:, :], NORMS.index(("kv", b)))
                elif i == 1:
                    forget_gate(b)
                    dve.wait_ge(*full(("T", "kv", b)))
                    norm(("mix1", b), rows[:, :], NORMS.index(("kv", b)))
                elif i == 3:
                    attention(b, 0, FH // 2 + 2)
                elif i == 4:
                    residual(1, b)
                    norm(("ffn1", b), xn[:, b, :], NORMS.index(("ffn1", b)))
                elif i == 5:
                    route(1, b, 0)
                    route(1, b, 1)
                elif i == 6:
                    route(1, b, 2)
                    route(1, b, 3)
                elif i == 7:
                    gating(1, b)

            for i in range(8):
                gla_piece(0, i)
            step = ROUNDS // GROUPS
            for ph in range(len(PHASES)):
                if ph < 3:
                    for g in range(GROUPS):
                        experts(ph, g * step, (g + 1) * step)
                        if ph == 0:
                            gla_piece(1, g)
                        else:
                            fox_piece(ph - 1, g)
                else:
                    norm(("final", 0), xn[:, 0, :], 8)
                    experts(ph, 0, ROUNDS)
                experts_end(ph)
            norm(("final", 1), xn[:, 1, :], 9)

        @block.scalar
        def _(act):
            steps = 0

            def chained(ins):
                nonlocal steps
                steps += 1
                ins.then_inc(act_step, 1)
                act.wait_ge(act_step, steps)

            def mean_square(n):
                key = NORMS[n]
                if key in H_OF_NORM:
                    act.wait_ge(*version(H_OF_NORM[key]))
                chained(nc.scalar.activation(square[:, :], h[:, key[1], :], ACT.Square,
                                             accum_out=sumsq[:, n:n + 1]))
                nc.scalar.activation(rms[:, n:n + 1], sumsq[:, n:n + 1], ACT.Sqrt, bias=eps[:, 0:1], scale=1.0 / D
                                     ).then_inc(rms_ready, 1)

            def take_rows(key):
                use = ("T",) + key
                act.wait_ge(*full(use))
                frees(use, nc.scalar.activation(
                    xT[:, t_at(key) % 2, :, :].rearrange("p c t -> p (c t)"), flat(pair_of(use)), ACT.Copy))

            def fade(b, i):
                act.wait_ge(diff_ready, b * (LEVELS - 1) + i + 1)
                d = scratch[:, (i % 2) * HALF:(i % 2 + 1) * HALF]
                nc.scalar.activation(d, d, ACT.Exp).then_inc(fade_ready, 1)

            def heads_square(b):
                key = ("o", b)
                act.wait_ge(*full(key))
                o = flat(pair_of(key))
                for g in range(GH):
                    ins = nc.scalar.activation(square[:, g * GDV:(g + 1) * GDV], o[:, g * GDV:(g + 1) * GDV],
                                               ACT.Square, accum_out=head_ss[:, b, g:g + 1])
                chained(ins)
                nc.scalar.activation(head_rms[:, b, :], head_ss[:, b, :], ACT.Sqrt, bias=eps[:, 0:1],
                                     scale=1.0 / GDV).then_inc(head_ss_ready, 1)

            def take_query(layer, b, j):
                n = (layer * TILES + b) * 4 + j
                act.wait_ge(queryT_full, n + 1)
                nc.scalar.activation(queryT[:, :, :].rearrange("p c t -> p (c t)"),
                                     pair_of(("route", layer, b, j))[:, 0, :], ACT.Copy).then_inc(queryT_ready, 1)

            def gate_exp(layer, b):
                act.wait_ge(gate_x_ready, layer * TILES + b + 1)
                nc.scalar.activation(gate_e[:, :], gate_e[:, :], ACT.Exp).then_inc(gate_e_ready, 1)

            def take_keys(layer):
                for i in range(2):
                    use = ("keys", layer, i)
                    act.wait_ge(*full(use))
                    frees(use, nc.scalar.activation(
                        keysT[:, i * KC:(i + 1) * KC, :].rearrange("p g n -> p (g n)"), flat(pair_of(use)), ACT.Copy))

            def probs_of(n):
                o = (n % 2) * D
                return scratch[:, o:o + 2 * TILES * P], scratch[:, o + HALF:o + D]

            def att_exp(b, c):
                n = b * (FH // 2) + c
                s_n = (b + 1) * P
                act.wait_ge(max_ready, n + 1)
                if c >= 2:
                    act.wait_ge(probsT_full, n - 1)
                for g in range(2):
                    hh = 2 * c + g
                    ins = nc.scalar.activation(probs_of(n)[0][:, g * s_n:(g + 1) * s_n],
                                               pair_of(("att", b, c))[:, 0, g * s_n:(g + 1) * s_n], ACT.Exp,
                                               bias=neg_max[:, b, hh:hh + 1], accum_out=prob_sum[:, b, hh:hh + 1])
                ins.then_inc(probs_ready, 1)

            def att_take(b, c):
                n = b * (FH // 2) + c
                act.wait_ge(probsT_full, n + 1)
                if c >= 2:
                    act.wait_ge(pv_full, n - 1)
                w = 2 * (b + 1) * P
                nc.scalar.activation(probs_of(n)[1][:, 0:w], pair_of(("att", b, c))[:, 1, 0:w], ACT.Copy
                                     ).then_inc(probsT_ready, 1)

            def experts(ph, first, last):
                layer, b = PHASES[ph]
                with act.Fori(ph * ROUNDS + first, ph * ROUNDS + last) as r:
                    for q in range(RING // SUB):
                        s = slice(q * SUB, (q + 1) * SUB)
                        act.wait_ge(u_free, r * RING + (RING + (q + 1) * SUB))
                        nc.scalar.activation(gelus[:, s], dots[:, s], ACT.Gelu).then_inc(dots_free, 1)
                        act.wait_ge(dots_free, r * (RING // SUB) + (RING // SUB + q + 1))
                        for j in range(q * SUB, (q + 1) * SUB):
                            ins = nc.scalar.activation(
                                weights_s[:, j:j + 1], gelus[:, j:j + 1], ACT.Copy,
                                scale=gates[:, b, bass.ds(r * RING + (j - ph * SLOTS), 1)])
                        ins.then_inc(gelu_ready, 1)
                        act.wait_ge(gelu_ready, r * (RING // SUB) + (q + 1))
                        for j in range(q * SUB, (q + 1) * SUB):
                            act.wait_ge(v_free, r * RING + (j + 1))
                            nc.scalar.activation(diag[:, j, :], ident[:, :], ACT.Copy,
                                                 scale=weights_s[:, j:j + 1]).then_inc(diag_ready, 1)

            act.sem_inc(dots_free, RING // SUB)
            act.wait_ge(consts, 3)
            for b in range(TILES):
                act.wait_ge(x_loaded[b], 16)
                mean_square(b)
            for b in range(TILES):
                take_rows(("mix0", b))
            act.wait_ge(*multiplied(("glr", 0)))
            frees("glr", nc.scalar.activation(glrT[:, :], pair_of("glr")[0:GRANK, 0, 0:TILES * P], ACT.Copy))
            za = scratch[:, D:2 * D]
            act.wait_ge(*full("z"))
            act.wait_ge(small_loaded, 48)
            zp = flat(pair_of("z")).rearrange("p (h b t) -> p h b t", h=GH, b=TILES)
            za4 = za.rearrange("p (b h t) -> p b h t", b=TILES, h=GH)
            for g in range(GH):
                ins = nc.scalar.activation(za4[:, :, g, :], zp[:, g, :, :], ACT.Abs, bias=b_g[:, g:g + 1])
            ins.then_inc(z_abs_ready, 1)
            act.wait_ge(z_abs_ready, 1)
            chained(nc.scalar.activation(za, za, ACT.Exp, scale=-1.0))
            nc.scalar.activation(za, za, ACT.Ln, bias=1.0).then_inc(z_log_ready, 1)
            for key, at, scale in (("q", 0, float(GDK) ** -0.5), ("k", 1, 1.0)):
                act.wait_ge(*multiplied((key, 1)))
                frees(key, nc.scalar.activation(
                    qkT[:, :, at, :, :], flat(pair_of(key)).rearrange("p (h b t) -> p b h t", h=GH, b=TILES),
                    ACT.Copy, scale=scale))
            act.wait_ge(z_ready, 1)
            kd = scratch[:, 3 * D:3 * D + HALF]
            nc.scalar.activation(kd, kd, ACT.Exp).then_inc(z_exp_ready, 1)
            act.wait_ge(*multiplied(("v", 3)))
            for b in range(TILES):
                frees(("v", b), nc.scalar.activation(vtok[:, b, :], flat(pair_of(("v", b))), ACT.Copy))
            act.wait_ge(*multiplied(("r", 3)))
            for b in range(TILES):
                frees(("r", b), nc.scalar.activation(gate_o[:, b, :], flat(pair_of(("r", b))), ACT.Silu))
                act.wait_ge(*freed(("r", b)))
                act.sem_inc(silu_ready, 1)
            take_keys(0)

            def gla_piece(b, i):
                if i == 0:
                    if b == 0:
                        act.wait_ge(*full("kdec"))
                        frees("kdec", nc.scalar.activation(kdec[:, :, :].rearrange("p h k -> p (h k)"),
                                                           pair_of("kdec")[:, 0, :], ACT.Copy))
                        act.wait_ge(*full("state"))
                        frees("state", nc.scalar.activation(state[:, :, :].rearrange("p h v -> p (h v)"),
                                                            flat(pair_of("state")), ACT.Copy))
                    for n in range(4):
                        fade(b, n)
                elif i == 1:
                    for n in range(4, 7):
                        fade(b, n)
                elif i == 2:
                    if b:
                        act.wait_ge(*freed("kdec"))
                        nc.scalar.activation(scratch[:, 3 * D:3 * D + HALF],
                                             decay[:, 1, :, :].rearrange("p h t -> p (h t)"), ACT.Exp
                                             ).then_inc(z_exp_ready, 1)
                    heads_square(b)
                elif i == 3:
                    take_rows(("o0", b))
                    mean_square(NORMS.index(("ffn0", b)))
                    take_rows(("ffn0", b))
                elif i < 8:
                    take_query(0, b, i - 4)
                    if i == 7:
                        gate_exp(0, b)
                        if b:
                            take_keys(1)

            def fox_piece(b, i):
                if i == 0:
                    mean_square(NORMS.index(("kv", b)))
                    take_rows(("kv", b))
                    act.wait_ge(*multiplied((("K", b), 3)))
                    frees(("K", b), nc.scalar.activation(
                        kT2(b), flat(pair_of(("K", b))).rearrange("p (c t) -> p c t", c=KC), ACT.Copy))
                elif i == 1:
                    act.wait_ge(*multiplied((("V", b), 3)))
                    frees(("V", b), nc.scalar.activation(v2[:, b, :], flat(pair_of(("V", b))), ACT.Copy))
                    act.wait_ge(*multiplied((("fl", b), 0)))
                    if b:
                        act.wait_ge(cum_ready, b)
                    nc.scalar.activation(forget[:, 0, :], pair_of(("fl", b))[0:FH, 0, 0:P], ACT.Abs,
                                         bias=b_f[:, 0:1]).then_inc(f_abs_ready, 1)
                    act.wait_ge(f_abs_ready, b + 1)
                    chained(nc.scalar.activation(forget[:, 2, :], forget[:, 0, :], ACT.Exp, scale=-1.0))
                    nc.scalar.activation(forget[:, 2, :], forget[:, 2, :], ACT.Ln, bias=1.0).then_inc(f_log_ready, 1)
                    take_rows(("mix1", b))
                elif i == 2:
                    act.wait_ge(*multiplied((("Q", b), 3)))
                    act.wait_ge(q_zeroed, 1)
                    src = flat(pair_of(("Q", b))).rearrange("p (c t) -> p c t", c=KC)
                    for g in range(2):
                        pp = slice(g * FHD, (g + 1) * FHD)
                        ins = nc.scalar.activation(q2T[g][pp, :, :], src[pp, :, :], ACT.Copy,
                                                   scale=float(FHD) ** -0.5)
                    frees(("Q", b), ins)
                elif i == 3:
                    for n in range(FH // 2 + 1):
                        if n < FH // 2:
                            att_exp(b, n)
                        if n:
                            att_take(b, n - 1)
                elif i == 4:
                    take_rows(("o1", b))
                    mean_square(NORMS.index(("ffn1", b)))
                    take_rows(("ffn1", b))
                elif i == 5:
                    take_query(1, b, 0)
                    take_query(1, b, 1)
                elif i == 6:
                    take_query(1, b, 2)
                    take_query(1, b, 3)
                elif i == 7:
                    gate_exp(1, b)

            def kT2(b):
                return qkT[:, b, :, :, :].rearrange("p a c t -> p (a c) t")

            for i in range(8):
                gla_piece(0, i)
            step = ROUNDS // GROUPS
            for ph in range(len(PHASES)):
                act.wait_ge(routed, ph + 1)
                if ph < 3:
                    for g in range(GROUPS):
                        experts(ph, g * step, (g + 1) * step)
                        if ph == 0:
                            gla_piece(1, g)
                        else:
                            fox_piece(ph - 1, g)
                else:
                    mean_square(8)
                    experts(ph, 0, ROUNDS)
            mean_square(9)

        @block.tensor
        def _(pe):
            order = list(PAIR_USE)
            taken = 0

            def take(key):
                nonlocal taken
                u = PAIR_USE[key]
                assert u == taken, (key, order[taken])
                taken += 1
                if u >= 3:
                    pe.wait_ge(pair_free[u % 3], u // 3)
                return pairs[u % 3]

            def fills(key, ins):
                ins.then_inc(pair_full[PAIR_USE[key] % 3], 1)

            def block_of(key):
                n = BLOCK_OF[key]
                pe.wait_ge(w_loaded[n % NW], 16 * (n // NW + 1))
                return wbuf[:, n % NW, :, :]

            def transpose_rows(key, src):
                use = ("T",) + key
                dst = take(use)
                pe.wait_ge(rows_ready, t_at(key) + 1)
                for c in range(KC):
                    ins = nc.tensor.transpose(dst[:, c // 4, (c % 4) * P:(c % 4 + 1) * P],
                                              src[:, c * P:(c + 1) * P], ident[:, :])
                fills(use, ins)

            def product_T(key, i, slots, dst, n=WCOLS):
                w = block_of((key, i))
                nt = len(slots) * P
                for m in range(0, n, P):
                    mm = min(P, n - m)
                    for c in range(KC):
                        rhs = xT[:, slots[0], c, :] if len(slots) == 1 else xT[:, :, c, :]
                        ins = nc.tensor.matmul(dst(m // P, mm, nt), w[:, c, m:m + mm], rhs,
                                               start=(c == 0), stop=(c == KC - 1))
                ins.then_inc(w_used, 1)

            def product(key, i, slots, dsts):
                w = block_of((key, i))
                for slot, dst in zip(slots, dsts):
                    for c in range(KC):
                        ins = nc.tensor.matmul(dst[:, i // 2, (i % 2) * WCOLS:(i % 2 + 1) * WCOLS],
                                               xT[:, slot, c, :], w[:, c, :], start=(c == 0), stop=(c == KC - 1))
                ins.then_inc(w_used, 1)

            def transpose_keys(layer):
                n = BLOCK_OF[(("keys", layer), 0)]
                pe.wait_ge(w_loaded[n % NW], 16 * (n // NW + 1))
                raw = wbuf[:, n % NW, :, :].rearrange("p c n -> p (c n)").rearrange("p (g d) -> p g d", d=RK)
                for i in range(2):
                    dst = take(("keys", layer, i))
                    for c in range(KC):
                        ins = nc.tensor.transpose(dst[:, c // 4, (c % 4) * P:(c % 4 + 1) * P],
                                                  raw[:, i * KC + c, :], ident[:, :])
                    fills(("keys", layer, i), ins)
                pe.wait_ge(*full(("keys", layer, 1)))
                pe.sem_inc(w_used, 1)

            def level(b, i):
                key = ("level", b, i)
                dst = take(key)
                if i < LEVELS - 1:
                    pe.wait_ge(faded_ready, b * (LEVELS - 1) + i + 1)
                for g in range(GH):
                    if i < LEVELS - 1:
                        o = D + (i % 2) * HALF + g * P
                        kk = qq = scratch[:, o:o + P]
                    else:
                        kk, qq = qkT[:, b, 1, g, :], qkT[:, b, 0, g, :]
                    ins = nc.tensor.matmul(dst[:, 0, g * P:(g + 1) * P], kk, qq, start=True, stop=True)
                fills(key, ins)

            def gla_heads(b):
                key = ("o", b)
                dst = flat(take(key))
                pe.wait_ge(attn_ready, b + 1)
                if b:
                    pe.wait_ge(z_ready, 3)
                    pe.wait_ge(*freed("state"))
                for g in range(GH):
                    c = slice(g * GDV, (g + 1) * GDV)
                    if b:
                        nc.tensor.matmul(dst[:, c], scratch[:, 3 * D + g * P:3 * D + (g + 1) * P], state[:, g, :],
                                         start=True, stop=False)
                    ins = nc.tensor.matmul(dst[:, c], attnT[:, g, :], vtok[:, b, c], start=(b == 0), stop=True)
                fills(key, ins)

            def route(layer, b, j):
                key = ("route", layer, b, j)
                n = (layer * TILES + b) * 4 + j
                dst = take(key)
                slot = t_at((f"ffn{layer}", b)) % 2
                for i in (2 * j, 2 * j + 1):
                    w = block_of((("pq", layer, b), i))
                    for m in range(2):
                        o = ((i % 2) * 2 + m) * P
                        for c in range(KC):
                            ins = nc.tensor.matmul(dst[:, 0, o:o + P], w[:, c, m * P:(m + 1) * P], xT[:, slot, c, :],
                                                   start=(c == 0), stop=(c == KC - 1))
                    if i == 2 * j:
                        ins.then_inc(w_used, 1)
                    else:
                        ins.then_inc(queryT_full, 1)
                pe.wait_ge(queryT_full, n + 1)
                pe.sem_inc(w_used, 1)
                pe.wait_ge(queryT_ready, n + 1)
                for g in range(4):
                    ins = nc.tensor.matmul(dst[:, 1, g * P:(g + 1) * P], queryT[:, g, :], keysT[:, 4 * j + g, :],
                                           start=True, stop=True)
                fills(key, ins)

            def att_logits(b, c):
                key = ("att", b, c)
                dst = take(key)
                n = (b + 1) * P
                for g in range(2):
                    o = g * n
                    for s in range(b + 1):
                        last = s == b
                        nc.tensor.matmul(dst[:, 0, o + s * P:o + (s + 1) * P], q2T[g][:, c, :],
                                         qkT[:, s, c // 4, c % 4, :], start=True, stop=False)
                        ins = nc.tensor.matmul(dst[:, 0, o + s * P:o + (s + 1) * P],
                                               ident[0:FH, 2 * c + g:2 * c + g + 1].broadcast_to([FH, P]),
                                               neg_cumT[:, s * P:(s + 1) * P], start=False, stop=not last)
                        if last:
                            ins = nc.tensor.matmul(dst[:, 0, o + s * P:o + (s + 1) * P], ident16[:, :],
                                                   causal16[:, :], start=False, stop=True)
                fills(key, ins)

            def att_turn(b, c):
                n = b * (FH // 2) + c
                pe.wait_ge(probs_ready, n + 1)
                o = (n % 2) * D
                for i in range(2 * (b + 1)):
                    ins = nc.tensor.transpose(pair_of(("att", b, c))[:, 1, i * P:(i + 1) * P],
                                              scratch[:, o + i * P:o + (i + 1) * P], ident[:, :])
                ins.then_inc(probsT_full, 1)

            def att_values(b, c):
                n = b * (FH // 2) + c
                pe.wait_ge(probsT_ready, n + 1)
                o = (n % 2) * D + HALF
                for g in range(2):
                    for s in range(b + 1):
                        i = g * (b + 1) + s
                        ins = nc.tensor.matmul(pair_of(("att", b, c))[:, 0, g * FHD:(g + 1) * FHD],
                                               scratch[:, o + i * P:o + (i + 1) * P],
                                               v2[:, s, (2 * c + g) * FHD:(2 * c + g + 1) * FHD],
                                               start=(s == 0), stop=(s == b))
                ins.then_inc(pv_full, 1)

            def experts_begin(ph):
                layer, b = PHASES[ph]
                if ph:
                    pe.wait_ge(acc_free, ph)
                pe.wait_ge(*version(("mixed", layer, b)))
                for i in range(2):
                    nc.tensor.matmul(acc[:, i, :], ident[:, :], h[:, b, i * HALF:(i + 1) * HALF],
                                     start=True, stop=False)

            def experts(ph, first, last):
                with pe.Fori(ph * ROUNDS + first, ph * ROUNDS + last) as r:
                    for j in range(RING):
                        pe.wait_ge(v_loaded[j], r * 16 + 16)
                        pe.wait_ge(diag_ready, r * RING + (j + 1))
                        for i in range(2):
                            ins = nc.tensor.matmul(acc[:, i, :], diag[:, j, :], v_ring[:, j, i * HALF:(i + 1) * HALF],
                                                   start=False, stop=False)
                        ins.then_inc(v_free, 1)

            def experts_end(ph):
                for i in range(2):
                    ins = nc.tensor.matmul(acc[:, i, :], zeros16[:, 0:P], zeros16[:, :], start=False, stop=True)
                ins.then_inc(acc_full, 1)

            pe.sem_inc(v_free, RING)
            pe.wait_ge(consts, 3)
            for b in range(TILES):
                transpose_rows(("mix0", b), rows)
            for b in range(TILES):
                pe.wait_ge(*freed(("T", "mix0", b)))
            dst = take("glr")
            product_T("glr", 0, [0, 1], lambda m, mm, nt: dst[0:mm, 0, 0:nt], GRANK)
            pe.wait_ge(*freed("glr"))
            pe.wait_ge(small_loaded, 48)
            dst = flat(take("z"))
            for g in range(GH):
                ins = nc.tensor.matmul(dst[:, g * TILES * P:(g + 1) * TILES * P], w_g2[:, g * P:(g + 1) * P],
                                       glrT[:, :], start=True, stop=True)
            fills("z", ins)
            for key in ("q", "k"):
                dst = flat(take(key))
                for i in range(2):
                    product_T(key, i, [0, 1], lambda m, mm, nt: dst[0:mm, (2 * i + m) * nt:(2 * i + m + 1) * nt])
            for key in ("v", "r"):
                dsts = [take((key, b)) for b in range(TILES)]
                for i in range(4):
                    product(key, i, [0, 1], dsts)
            transpose_keys(0)

            def gla_piece(b, i):
                if i == 0:
                    if b == 0:
                        pe.wait_ge(z_ready, 2)
                        dst = take("kdec")
                        for g in range(GH):
                            ins = nc.tensor.transpose(dst[:, 0, g * P:(g + 1) * P],
                                                      scratch[:, 3 * D + g * P:3 * D + (g + 1) * P], ident[:, :])
                        fills("kdec", ins)
                        pe.wait_ge(*freed("kdec"))
                        dst = flat(take("state"))
                        for g in range(GH):
                            c = slice(g * GDV, (g + 1) * GDV)
                            ins = nc.tensor.matmul(dst[:, c], kdec[:, g, :], vtok[:, 0, c], start=True, stop=True)
                        fills("state", ins)
                    for n in range(3):
                        level(b, n)
                elif i == 1:
                    for n in range(3, 6):
                        level(b, n)
                elif i == 2:
                    for n in range(6, 8):
                        level(b, n)
                    gla_heads(b)
                    transpose_rows(("o0", b), rows)
                elif i == 3:
                    mix_out(0, b)
                elif i < 8:
                    route(0, b, i - 4)
                    if i == 7 and b:
                        transpose_keys(1)

            def mix_out(layer, b):
                pe.wait_ge(*freed(("T", f"o{layer}", b)))
                dst = take(("wo", layer, b))
                for i in range(4):
                    product(("wo", layer, b), i, [t_at((f"o{layer}", b)) % 2], [dst])
                transpose_rows((f"ffn{layer}", b), xn[:, b, :])
                pe.wait_ge(*freed(("T", f"ffn{layer}", b)))

            def fox_piece(b, i):
                if i == 0:
                    transpose_rows(("kv", b), rows)
                    pe.wait_ge(*freed(("T", "kv", b)))
                    s = t_at(("kv", b)) % 2
                    dst = flat(take(("K", b)))
                    for n in range(4):
                        product_T(("K", b), n, [s], lambda m, mm, nt: dst[:, (2 * n + m) * P:(2 * n + m + 1) * P])
                elif i == 1:
                    s = t_at(("kv", b)) % 2
                    dst = take(("V", b))
                    for n in range(4):
                        product(("V", b), n, [s], [dst])
                    dst2 = take(("fl", b))
                    product_T(("fl", b), 0, [s], lambda m, mm, nt: dst2[0:mm, 0, 0:P], FH)
                    transpose_rows(("mix1", b), rows)
                elif i == 2:
                    pe.wait_ge(*freed(("T", "mix1", b)))
                    s = t_at(("mix1", b)) % 2
                    dst = flat(take(("Q", b)))
                    for n in range(4):
                        product_T(("Q", b), n, [s], lambda m, mm, nt: dst[:, (2 * n + m) * P:(2 * n + m + 1) * P])
                elif i == 3:
                    pe.wait_ge(*freed(("Q", b)))
                    pe.wait_ge(*freed(("K", b)))
                    pe.wait_ge(*freed(("V", b)))
                    pe.wait_ge(cum_ready, b + 1)
                    for n in range(FH // 2 + 2):
                        if n < FH // 2:
                            att_logits(b, n)
                        if 1 <= n <= FH // 2:
                            att_turn(b, n - 1)
                        if n >= 2:
                            att_values(b, n - 2)
                elif i == 4:
                    transpose_rows(("o1", b), rows)
                    mix_out(1, b)
                elif i == 5:
                    route(1, b, 0)
                    route(1, b, 1)
                elif i == 6:
                    route(1, b, 2)
                    route(1, b, 3)

            for i in range(8):
                gla_piece(0, i)
            step = ROUNDS // GROUPS
            for ph in range(len(PHASES)):
                experts_begin(ph)
                if ph < 3:
                    for g in range(GROUPS):
                        experts(ph, g * step, (g + 1) * step)
                        if ph == 0:
                            gla_piece(1, g)
                        else:
                            fox_piece(ph - 1, g)
                else:
                    experts(ph, 0, ROUNDS)
                experts_end(ph)


_INS = ["x", "norm_mix", "norm_ffn", "gla_w_in", "gla_w_g2", "gla_b_g", "gla_norm_o", "gla_w_o", "kv_norm", "kv_w",
        "fox_b_f", "fox_w_q", "fox_w_o", "peer_w_q", "peer_sub_keys", "peer_u", "peer_v", "norm_final"]


def kernel(**inputs):
    import numpy as _np
    import concourse.bacc as _bacc
    from concourse import mybir as _mybir
    from concourse.bass_utils import run_bass_kernel_spmd as _run

    nc = _bacc.Bacc("TRN2", target_bir_lowering=False, num_devices=1)
    arrays, args = {}, {}
    for name in _INS:
        v = _np.ascontiguousarray(inputs[name])
        arrays[f"in_{name}"] = v
        args[name] = nc.dram_tensor(f"in_{name}", v.shape, _mybir.dt.from_np(v.dtype), kind="ExternalInput").ap()
    out = nc.dram_tensor("out_0", inputs["x"].shape, _mybir.dt.from_np(_np.dtype("float32")),
                         kind="ExternalOutput").ap()
    yoco_kernel(nc, args, out)
    r = _run(nc, [arrays], core_ids=[0])
    return r.results[0]["out_0"]
```

```python
from contextlib import ExitStack

import concourse.bass as bass
from concourse import mybir

F32 = mybir.dt.float32
BF16 = mybir.dt.bfloat16
U32 = mybir.dt.uint32
U8 = mybir.dt.uint8
ALU = mybir.AluOpType
ACT = mybir.ActivationFunctionType
AX_X = mybir.AxisListType.X

P = 128
D = 1024
KC = D // P
HALF = 512
TILES = 2
EPS = 1e-6
LOW = -3.0e38

GH, GDK, GDV, GRANK, GTAU = 4, 128, 256, 16, 16.0
LEVELS = 8
FH, FHD = 16, 64
RH, RK, RTOP = 8, 128, 16
EXPERTS = RK * RK
SLOTS = RH * RTOP

RING = 8
SUB = 4
ISSUE = 4
ROUNDS = SLOTS // RING
VEC_SLOTS = [2, 3]
PE_SLOTS = [j for j in range(RING) if j not in VEC_SLOTS]
VEC = len(VEC_SLOTS)
QUARTER = ROUNDS // 4
HALVES = ROUNDS * RING // SUB
LAST_VEC = RING - 3
PHASES = [(layer, b) for layer in range(2) for b in range(TILES)]

WCOLS = 256
NW = 4
RING_BLOCKS = 8


def weight_blocks(a):
    w_in, w_kv = a["gla_w_in"][0], a["kv_w"]
    out = [("gain", ("mix", 0), a["norm_mix"][0:1, :])]

    def cols(key, w, first, n):
        for i in range(0, n, WCOLS):
            out.append(("w", (key, i // WCOLS), w[:, first + i:first + min(i + WCOLS, n)]))

    cols("glr", w_in, 3 * D, GRANK)
    cols("q", w_in, 0, HALF)
    cols("k", w_in, HALF, HALF)
    cols("v", w_in, D, D)
    out.append(("go", None, a["gla_norm_o"][0:1, :]))
    cols("r", w_in, 2 * D, D)
    out.append(("keys", (("keys", 0), 0), a["peer_sub_keys"][0]))
    out.append(("gain", ("ffn", 0), a["norm_ffn"][0:1, :]))
    peer_q = a["peer_w_q"]

    def route(layer, b, j):
        for i in (2 * j, 2 * j + 1):
            out.append(("w", (("pq", layer, b), i), peer_q[layer][:, i * WCOLS:(i + 1) * WCOLS]))

    cols(("wo", 0, 0), a["gla_w_o"][0], 0, D)
    for j in range(4):
        route(0, 0, j)
    cols(("wo", 0, 1), a["gla_w_o"][0], 0, D)
    route(0, 1, 0)
    for b in range(TILES):
        before = (0, 1) if b == 0 else (1, 0)
        out.append(("gain", ("kv", b), a["kv_norm"].rearrange("(o d) -> o d", o=1)))
        route(*before, 1)
        cols(("K", b), w_kv, 0, D)
        route(*before, 2)
        cols(("V", b), w_kv, D, D)
        cols(("fl", b), w_kv, 2 * D, FH)
        out.append(("gain", ("mix1", b), a["norm_mix"][1:2, :]))
        route(*before, 3)
        cols(("Q", b), a["fox_w_q"][0], 0, D)
        out.append(("gain", ("ffn1", b), a["norm_ffn"][1:2, :]))
        cols(("wo", 1, b), a["fox_w_o"][0], 0, D)
        if b == 0:
            out.append(("keys", (("keys", 1), 0), a["peer_sub_keys"][1]))
        route(1, b, 0)
    for j in range(1, 4):
        route(1, 1, j)
    out.append(("gain", ("final",), a["norm_final"].rearrange("(o d) -> o d", o=1)))
    return out


def weight_releases(stream):
    out = [key for kind, key, _ in stream if kind in ("w", "keys") and key[0] not in ("v", "r")]
    for before, held in (((("keys", 0), 0), [("v", 0), ("v", 1)]), ((("pq", 0, 0), 0), [("v", 2), ("v", 3)]),
                         ((("pq", 0, 0), 2), [("r", i) for i in range(4)])):
        at = out.index(before)
        out[at:at] = held
    return out


def weight_places(stream):
    out, turn, last = {}, 0, {}
    for kind, key, _ in stream:
        if kind not in ("w", "keys"):
            continue
        if key[0] in ("v", "r"):
            place = NW + 4 * (key[0] == "r") + key[1]
        else:
            place, turn = turn % NW, turn + 1
        n, before = last.get(place, (0, None))
        out[key] = (place, n + 1, before)
        last[place] = (n + 1, key)
    return out


def pair_uses():
    out = []

    def turn(*keys, among=(0, 1, 2)):
        for key in keys:
            last = next((p for _, p in reversed(out) if p in among), among[-1])
            out.append((key, among[(among.index(last) + 1) % len(among)]))

    turn(("T", "mix0", 0), ("T", "mix0", 1), "glr", "z", "q", "k")
    for i in range(LEVELS):
        if i % 4 == 0:
            out.append((("v" if i == 0 else "r", 0), 0))
        turn(("level", 0, i), among=(1, 2))
    turn(("o", 0))
    out.append((("v", 1), 3))
    turn(("keys", 0, 0), ("keys", 0, 1), ("T", "o0", 0), ("wo", 0, 0), ("T", "ffn0", 0), ("route", 0, 0, 0))
    out.append((("r", 1), 3))
    turn(*[("route", 0, 0, j) for j in range(1, 4)])
    turn("kdec", "state", *[("level", 1, i) for i in range(LEVELS)])
    turn(("o", 1), ("T", "o0", 1), ("wo", 0, 1), ("T", "ffn0", 1), ("route", 0, 1, 0))
    for b in range(TILES):
        before = (0, 1) if b == 0 else (1, 0)
        turn(("route", *before, 1), ("T", "kv", b), ("K", b), ("route", *before, 2), ("V", b), ("fl", b),
             ("route", *before, 3), ("T", "mix1", b), ("Q", b), *[("att", b, c) for c in range(FH // 2)])
        turn(("T", "o1", b), ("wo", 1, b))
        if b == 0:
            turn(("keys", 1, 0), ("keys", 1, 1))
        turn(("T", "ffn1", b), ("route", 1, b, 0))
    turn(*[("route", 1, 1, j) for j in range(1, 4)])
    return out


T_USES = [("mix0", 0), ("mix0", 1), ("o0", 0), ("ffn0", 0), ("o0", 1), ("ffn0", 1)]
for _b in range(TILES):
    T_USES += [("kv", _b), ("mix1", _b), ("o1", _b), ("ffn1", _b)]
NORMS = [("mix0", 0), ("mix0", 1), ("ffn0", 0), ("ffn0", 1), ("kv", 0), ("ffn1", 0), ("kv", 1), ("ffn1", 1),
         ("final", 0), ("final", 1)]
GAIN_OF = {("mix0", 0): 0, ("mix0", 1): 0, ("ffn0", 0): 1, ("ffn0", 1): 1, ("kv", 0): 2, ("mix1", 0): 3,
           ("ffn1", 0): 4, ("kv", 1): 5, ("mix1", 1): 6, ("ffn1", 1): 7, ("final", 0): 8, ("final", 1): 8}
GAIN_LAST = {("mix0", 1), ("ffn0", 1), ("kv", 0), ("mix1", 0), ("ffn1", 0), ("kv", 1), ("mix1", 1), ("ffn1", 1)}
H_VERSIONS = [("mixed", 0, 0), ("mixed", 0, 1), ("done", 0, 0), ("mixed", 1, 0), ("done", 0, 1), ("mixed", 1, 1),
              ("done", 1, 0), ("done", 1, 1)]
H_OF_NORM = {("ffn0", 0): ("mixed", 0, 0), ("ffn0", 1): ("mixed", 0, 1), ("kv", 0): ("done", 0, 0),
             ("ffn1", 0): ("mixed", 1, 0), ("kv", 1): ("done", 0, 1), ("ffn1", 1): ("mixed", 1, 1),
             ("final", 0): ("done", 1, 0), ("final", 1): ("done", 1, 1)}


def yoco_kernel(nc, a, out):
    STREAM = weight_blocks(a)
    RELEASE_OF = {key: i for i, key in enumerate(weight_releases(STREAM))}
    PLACE_OF = weight_places(STREAM)
    PAIR_USE, PAIR_COUNT = {}, [0] * 4
    for key, p in pair_uses():
        PAIR_USE[key] = (p, PAIR_COUNT[p])
        PAIR_COUNT[p] += 1

    with ExitStack() as ctx:
        def sb(name, shape, dt=F32):
            return ctx.enter_context(nc.sbuf_tensor(name, shape, dt))

        def sem(name):
            return ctx.enter_context(nc.semaphore(name))

        h = sb("h", [P, TILES, D])
        xn = sb("xn", [P, TILES, D])
        rows = sb("rows", [P, D])
        xT = sb("xT", [P, 2, KC, P])
        gain = sb("gain", [P, D])
        wbuf = sb("wbuf", [P, NW, KC, WCOLS])
        u_ring = sb("u_ring", [P, RING, D])
        v_ring = sb("v_ring", [P, RING, D])
        square = sb("square", [P, D], BF16)
        ident = sb("ident", [P, P])
        ident16 = sb("ident16", [P, P], BF16)
        zeros16 = sb("zeros16", [P, HALF], BF16)
        causal16 = sb("causal16", [P, P], BF16)
        ones = sb("ones", [P, P])
        eps = sb("eps", [P, 1])
        sumsq = sb("sumsq", [P, len(NORMS)])
        rms = sb("rms", [P, len(NORMS)])
        rstd = sb("rstd", [P, len(NORMS)])
        qkT = sb("qkT", [P, TILES, 2, GH, P])
        vtok = sb("vtok", [P, TILES, D])
        gate_o = sb("gate_o", [P, TILES, D])
        b_g = sb("b_g", [P, GH])
        decay = sb("decay", [P, TILES, GH, P])
        scratch = sb("scratch", [P, 4096])
        masks = sb("masks", [P, LEVELS, P], U8)
        attnT = sb("attnT", [P, GH, P])
        kdec = attnT
        state = sb("state", [P, GH, GDV])
        head_ss = sb("head_ss", [P, TILES, GH])
        head_rms = sb("head_rms", [P, TILES, GH])
        head_rstd = sb("head_rstd", [P, TILES, GH])
        b_f = sb("b_f", [FH, 1])
        forget = sb("forget", [FH, 4, P])
        cumT = sb("cumT", [FH, TILES * P])
        neg_cumT = sb("neg_cumT", [FH, TILES * P])
        neg_max = sb("neg_max", [P, TILES, FH])
        prob_sum = sb("prob_sum", [P, TILES, FH])
        prob_inv = sb("prob_inv", [P, TILES, FH])
        keysT = sb("keysT", [P, 2 * RH, RK])
        glrT = keysT[0:GRANK, 0:TILES, :].rearrange("p g n -> p (g n)")
        w_g2 = keysT[0:GRANK, TILES:TILES + GH, :].rearrange("p g n -> p (g n)")
        queryT = sb("queryT", [P, 4, P])
        top = sb("top", [P, 4, RTOP])
        top_at = sb("top_at", [P, 4, RTOP], U32)
        top_id = sb("top_id", [P, 4, RTOP])
        best = sb("best", [P, TILES, RH, RTOP])
        best_at = sb("best_at", [P, 2, RTOP], U32)
        digit = sb("digit", [P, 2, 2, RTOP], U32)
        picked = sb("picked", [P, 2, 2, RTOP])
        ids_f = sb("ids_f", [P, 2, RTOP])
        iota16 = sb("iota16", [P, RTOP])
        ids = sb("ids", [P, TILES, SLOTS], U32)
        gates = sb("gates", [P, TILES, SLOTS])
        gate_e = sb("gate_e", [P, SLOTS])
        gate_sum = sb("gate_sum", [P, RH])
        gate_inv = sb("gate_inv", [P, RH])
        u_ids = sb("u_ids", [P, RING], U32)
        v_ids = sb("v_ids", [P, RING], U32)
        dots = sb("dots", [P, RING])
        gelus = sb("gelus", [P, RING])
        weights_s = sb("weights_s", [P, RING])
        diag = sb("diag", [P, len(PE_SLOTS), P])

        q2T = [gate_o[:, g, :].rearrange("p (c t) -> p c t", c=KC) for g in range(2)]
        v2 = vtok

        places = [wbuf[:, i, :, :] for i in range(NW)] + [
            ring[:, 2 * i:2 * i + 2, :].rearrange("p s d -> p (s d)").rearrange("p (c n) -> p c n", c=KC)
            for ring in (u_ring, v_ring) for i in range(RING_BLOCKS // 2)]
        xT_kept = xn[:, 1, :].rearrange("p (c t) -> p c t", c=KC)
        gain_o = gate_o[:, 1, :]

        acc = ctx.enter_context(nc.psum_tensor("acc", [P, 2, HALF], F32))
        pairs = [ctx.enter_context(nc.psum_tensor(f"pair{i}", [P, 2, HALF], F32)) for i in range(3)] + [acc]

        def flat(t):
            return t[:, :, :].rearrange("p a b -> p (a b)")

        x_loaded = [sem(f"x_loaded{b}") for b in range(TILES)]
        small_loaded = sem("small_loaded")
        gain_loaded, gain_used = sem("gain_loaded"), sem("gain_used")
        gain_o_loaded = sem("gain_o_loaded")
        kept_ready = sem("kept_ready")
        w_loaded = [sem(f"w_loaded{i}") for i in range(NW + RING_BLOCKS)]
        w_used = sem("w_used")
        consts = sem("consts")
        masks_f_ready, masks_ready = sem("masks_f_ready"), sem("masks_ready")
        pair_full = [sem(f"pair_full{i}") for i in range(4)]
        pair_free = [sem(f"pair_free{i}") for i in range(4)]
        dve_step, act_step = sem("dve_step"), sem("act_step")
        dve_const = sem("dve_const")
        h_ready = sem("h_ready")
        rms_ready = sem("rms_ready")
        q_zeroed = sem("q_zeroed")
        rows_ready = sem("rows_ready")
        z_ready, z_exp_ready, z_log_ready = sem("z_ready"), sem("z_exp_ready"), sem("z_log_ready")
        z_abs_ready = sem("z_abs_ready")
        diff_ready, fade_ready, faded_ready = sem("diff_ready"), sem("fade_ready"), sem("faded_ready")
        attn_ready = sem("attn_ready")
        head_ss_ready = sem("head_ss_ready")
        silu_ready = sem("silu_ready")
        f_abs_ready, f_log_ready, cum_ready = sem("f_abs_ready"), sem("f_log_ready"), sem("cum_ready")
        max_ready, probs_ready, probsT_full, probsT_ready = (sem("max_ready"), sem("probs_ready"),
                                                              sem("probsT_full"), sem("probsT_ready"))
        pv_full = sem("pv_full")
        queryT_full, queryT_ready = sem("queryT_full"), sem("queryT_ready")
        gate_x_ready, gate_e_ready, routed = sem("gate_x_ready"), sem("gate_e_ready"), sem("routed")
        keys_ready = sem("keys_ready")
        ids_laid, issued = sem("ids_laid"), sem("issued")
        u_loaded = [sem(f"u_loaded{j}") for j in range(RING)]
        v_loaded = [sem(f"v_loaded{j}") for j in range(RING)]
        u_free, v_free, vec_free = sem("u_free"), sem("v_free"), sem("vec_free")
        dots_free = sem("dots_free")
        gelu_ready = sem("gelu_ready")
        diag_ready = sem("diag_ready")
        acc_full, acc_free = sem("acc_full"), sem("acc_free")
        out_ready, out_stored = sem("out_ready"), sem("out_stored")

        def pair_of(key):
            return pairs[PAIR_USE[key][0]]

        def full(key):
            p, n = PAIR_USE[key]
            assert not of_weights(key)
            return pair_full[p], sum(q == p and m <= n and not of_weights(k) for k, (q, m) in PAIR_USE.items())

        def freed(key):
            p, n = PAIR_USE[key]
            return pair_free[p], n + 1

        def frees(key, ins):
            ins.then_inc(pair_free[PAIR_USE[key][0]], 1)

        def of_weights(key):
            name = key if isinstance(key, str) else key[0]
            if key in (("v", 0), ("r", 0)):
                return False
            return name in ("glr", "q", "k", "v", "r", "wo", "K", "V", "fl", "Q")

        def multiplied(key):
            return w_used, RELEASE_OF[key] + 1

        def t_at(key):
            return T_USES.index(key)

        def version(key):
            return h_ready, H_VERSIONS.index(key) + 1

        def is_last(r, j):
            return type(r) is int and r == len(PHASES) * ROUNDS - 1 and j >= LAST_VEC

        def in_halves(eng, half, ph, first, last):
            at, turns = first, ph * ROUNDS
            if at % 2 and at < last:
                half(ph, turns + at // 2, 1)
                at += 1
            if last - at >= 4:
                with eng.Fori(turns + at // 2, turns + last // 2) as r:
                    half(ph, r, 0)
                    half(ph, r, 1)
                at = last // 2 * 2
            for i in range(at, last):
                half(ph, turns + i // 2, i % 2)

        block = ctx.enter_context(nc.Block())

        @block.sync
        def _(sp):
            for b in range(TILES):
                sp.dma_start(h[:, b, :], a["x"][0, b * P:(b + 1) * P, :]).then_inc(x_loaded[b], 16)
            n_gain = n_block = 0
            for kind, key, src in STREAM:
                if kind == "go":
                    sp.dma_start(gain_o, src.broadcast_to([P, D])).then_inc(gain_o_loaded, 16)
                elif kind == "gain":
                    if n_gain:
                        sp.wait_ge(gain_used, n_gain)
                    sp.dma_start(gain[:, :], src.broadcast_to([P, D])).then_inc(gain_loaded, 16)
                    n_gain += 1
                else:
                    place, _, before = PLACE_OF[key]
                    if before:
                        sp.wait_ge(*multiplied(before))
                    if kind == "keys":
                        dst = places[place].rearrange("p c n -> p (c n)").rearrange("p (g d) -> p g d", d=RK)
                        sp.dma_start(dst, src.rearrange("h c n d -> n (h c) d")).then_inc(w_loaded[place], 16)
                    else:
                        sp.dma_start(places[place][:, :, 0:src.shape[1]],
                                     src.rearrange("(c p) n -> p c n", p=P)).then_inc(w_loaded[place], 16)
                    n_block += 1
                    if n_block == 1:
                        sp.dma_start(w_g2[:, :], a["gla_w_g2"][0]).then_inc(small_loaded, 16)
                        with nc.allow_non_contiguous_dma(reason="640 numbers"):
                            sp.dma_start(b_g[:, :], a["gla_b_g"][0].rearrange("(h k) -> k h", k=GDK)
                                         ).then_inc(small_loaded, 16)
                            sp.dma_start(b_f[:, :], a["fox_b_f"].rearrange("(h o) -> h o", o=1)
                                         ).then_inc(small_loaded, 16)
            for b in range(TILES):
                sp.wait_ge(out_ready, b + 1)
                sp.dma_start(out[0, b * P:(b + 1) * P, :], xn[:, b, :]).then_inc(out_stored, 16)
            sp.wait_ge(out_stored, 16 * TILES)

        @block.gpsimd
        def _(pool):
            made = 0

            def chained(ins):
                nonlocal made
                made += 1
                ins.then_inc(consts, 1)
                pool.wait_ge(consts, made)

            nc.gpsimd.memset(zeros16[:, :], 0.0)
            nc.gpsimd.memset(ones[:, :], 1.0)
            nc.gpsimd.memset(eps[:, :], EPS)
            nc.gpsimd.memset(causal16[:, :], 0.0)
            nc.gpsimd.iota(iota16[:, :], pattern=[[1, RTOP]], base=0, channel_multiplier=0,
                           allow_small_or_imprecise_dtypes=True)
            nc.gpsimd.memset(ident16[:, :], 0.0)
            chained(nc.gpsimd.memset(ident[:, :], 0.0))
            nc.gpsimd.affine_select(out=ident16[:, :], in_=ident16[:, :], compare_op=ALU.not_equal, fill=1.0,
                                    base=0, pattern=[[-1, P]], channel_multiplier=1)
            chained(nc.gpsimd.affine_select(out=ident[:, :], in_=ident[:, :], compare_op=ALU.not_equal, fill=1.0,
                                            base=0, pattern=[[-1, P]], channel_multiplier=1))
            nc.gpsimd.affine_select(out=causal16[:, :], in_=causal16[:, :], compare_op=ALU.is_ge, fill=-1.0e38,
                                    base=0, pattern=[[-1, P]], channel_multiplier=1)
            mf = scratch[:, 0:LEVELS * P].rearrange("p (l t) -> p l t", l=LEVELS)
            chained(nc.gpsimd.memset(mf, 1.0))
            for i in range(LEVELS - 1):
                m = P >> (i + 1)
                v = mf[:, i, :].rearrange("p (n c) -> p n c", c=2 * m)
                n = P // (2 * m)
                chained(nc.gpsimd.affine_select(out=v, in_=v, compare_op=ALU.is_ge, fill=0.0, base=0,
                                                pattern=[[-2 * m, n], [0, 2 * m]], channel_multiplier=1))
                chained(nc.gpsimd.affine_select(out=v, in_=v, compare_op=ALU.is_ge, fill=0.0, base=m - 1,
                                                pattern=[[2 * m, n], [0, 2 * m]], channel_multiplier=-1))
                chained(nc.gpsimd.affine_select(out=v, in_=v, compare_op=ALU.is_ge, fill=0.0, base=-m,
                                                pattern=[[0, n], [1, 2 * m]], channel_multiplier=0))
            nc.gpsimd.affine_select(out=mf[:, LEVELS - 1, :], in_=mf[:, LEVELS - 1, :], compare_op=ALU.is_equal,
                                    fill=0.0, base=0, pattern=[[-1, P]], channel_multiplier=1
                                    ).then_inc(masks_f_ready, 1)
            u_rows = a["peer_u"].rearrange("l n d -> (l n) d")
            v_rows = a["peer_v"].rearrange("l n d -> (l n) d")
            pool.wait_ge(*multiplied(("r", 3)))
            for ph, (layer, b) in enumerate(PHASES):
                for quarter in range(4):
                    pool.wait_ge(routed, ph * 4 + quarter + 1)
                    first = ph * ROUNDS + quarter * QUARTER
                    with pool.Fori(first, first + QUARTER) as r:
                        for j0 in range(0, RING, ISSUE):
                            n_ids = bass.ds(r * RING + (j0 - ph * SLOTS), ISSUE)
                            slots = range(j0, j0 + ISSUE)
                            pool.wait_ge(u_free, r * RING + (j0 + ISSUE))
                            pool.sem_inc(issued, 1)
                            nc.gpsimd.tensor_copy(u_ids[:, j0:j0 + ISSUE], ids[:, b, n_ids]).then_inc(ids_laid, 1)
                            pool.wait_ge(ids_laid, r * (2 * RING // ISSUE) + (2 * (j0 // ISSUE) + 1))
                            pool.sem_inc(issued, 1)
                            for j in slots:
                                pool.indirect_dma_start(
                                    u_ring[:, j, :], None, u_rows, bass.IndirectOffsetOnAxis(ap=u_ids[:, j:j + 1], axis=0)
                                ).then_inc(u_loaded[j], 16)
                            on_pe = sum(j < j0 + ISSUE for j in PE_SLOTS)
                            on_dve = sum(j < j0 + ISSUE for j in VEC_SLOTS)
                            if any(j in PE_SLOTS for j in slots):
                                pool.wait_ge(v_free, r * len(PE_SLOTS) + on_pe)
                                pool.sem_inc(issued, 1)
                            if any(j in VEC_SLOTS for j in slots):
                                pool.wait_ge(vec_free, r * VEC + on_dve)
                                pool.sem_inc(issued, 1)
                            nc.gpsimd.tensor_copy(v_ids[:, j0:j0 + ISSUE], ids[:, b, n_ids]).then_inc(ids_laid, 1)
                            pool.wait_ge(ids_laid, r * (2 * RING // ISSUE) + (2 * (j0 // ISSUE) + 2))
                            pool.sem_inc(issued, 1)
                            for j in slots:
                                pool.indirect_dma_start(
                                    v_ring[:, j, :], None, v_rows, bass.IndirectOffsetOnAxis(ap=v_ids[:, j:j + 1], axis=0)
                                ).then_inc(v_loaded[j], 16)

        @block.vector
        def _(dve):
            steps = 0

            def chained(ins):
                nonlocal steps
                steps += 1
                ins.then_inc(dve_step, 1)
                dve.wait_ge(dve_step, steps)

            def norm(key, dst, n):
                b = key[1]
                g = GAIN_OF[key]
                dve.wait_ge(rms_ready, n + 1)
                if key[0] != "mix1":
                    chained(nc.vector.reciprocal(rstd[:, n:n + 1], rms[:, n:n + 1]))
                dve.wait_ge(gain_loaded, 16 * (g + 1))
                nc.vector.scalar_tensor_tensor(out=dst, in0=h[:, b, :], scalar=rstd[:, n:n + 1], in1=gain[:, :],
                                               op0=ALU.mult, op1=ALU.mult
                                               ).then_inc(rows_ready if key[0] != "final" else out_ready, 1)
                if key in GAIN_LAST:
                    if key in T_USES:
                        dve.wait_ge(rows_ready, t_at(key) + 1)
                    dve.sem_inc(gain_used, 1)

            def level_refs(b, m):
                s = decay[:, b, :, :].rearrange("p h (n c) -> p (h n) c", c=2 * m)
                return s, s[:, :, m - 1:m].broadcast_to([P, GH * P // (2 * m), m])

            def level_diff(b, i):
                m = P >> (i + 1)
                s, ref = level_refs(b, m)
                d = scratch[:, (i % 2) * HALF:(i % 2 + 1) * HALF].rearrange("p (n c) -> p n c", c=2 * m)
                if i >= 2:
                    dve.wait_ge(faded_ready, b * (LEVELS - 1) + i - 1)
                nc.vector.tensor_tensor(d[:, :, 0:m], ref, s[:, :, 0:m], ALU.subtract)
                nc.vector.tensor_tensor(d[:, :, m:2 * m], s[:, :, m:2 * m], ref, ALU.subtract
                                        ).then_inc(diff_ready, 1)

            def level_apply(b, i):
                m = P >> (i + 1)
                e = scratch[:, (i % 2) * HALF:(i % 2 + 1) * HALF].rearrange("p (n c) -> p n c", c=2 * m)
                x = scratch[:, D + (i % 2) * HALF:D + (i % 2 + 1) * HALF].rearrange("p (n c) -> p n c", c=2 * m)
                kk = qkT[:, b, 1, :, :].rearrange("p h (n c) -> p (h n) c", c=2 * m)
                qq = qkT[:, b, 0, :, :].rearrange("p h (n c) -> p (h n) c", c=2 * m)
                dve.wait_ge(fade_ready, fades(b, i))
                if i >= 2:
                    dve.wait_ge(*full(("level", b, i - 2)))
                nc.vector.tensor_tensor(x[:, :, 0:m], kk[:, :, 0:m], e[:, :, 0:m], ALU.mult)
                nc.vector.tensor_tensor(x[:, :, m:2 * m], qq[:, :, m:2 * m], e[:, :, m:2 * m], ALU.mult
                                        ).then_inc(faded_ready, 1)

            def level_take(b, i):
                key = ("level", b, i)
                dve.wait_ge(*full(key))
                ins = nc.vector.copy_predicated(attnT[:, :, :],
                                                masks[:, i, :].unsqueeze(1).broadcast_to([P, GH, P]),
                                                pair_of(key)[:, 0, :].rearrange("p (h t) -> p h t", h=GH))
                frees(key, ins)
                dve.wait_ge(*freed(key))

            def fades(b, i):
                return b * (LEVELS - 1) + i + 1

            def level_begin(b):
                if b:
                    dve.wait_ge(*full("state"))
                chained(nc.vector.memset(attnT[:, :, :], 0.0))
                level_diff(b, 0)

            def level_step(b, i):
                if i + 1 < LEVELS - 1:
                    level_diff(b, i + 1)
                if i < LEVELS - 1:
                    level_apply(b, i)
                if i:
                    level_take(b, i - 1)
                if i == LEVELS:
                    dve.sem_inc(attn_ready, 1)

            def gla_out(b):
                key = ("o", b)
                dve.wait_ge(head_ss_ready, b + 1)
                chained(nc.vector.reciprocal(head_rstd[:, b, :], head_rms[:, b, :]))
                dve.wait_ge(*full(("T", "mix0", 1) if b == 0 else ("T", "o0", 0)))
                o = flat(pair_of(key))
                for g in range(GH):
                    c = slice(g * GDV, (g + 1) * GDV)
                    ins = nc.vector.scalar_tensor_tensor(out=rows[:, c], in0=o[:, c], scalar=head_rstd[:, b, g:g + 1],
                                                         in1=gate_o[:, b, c], op0=ALU.mult, op1=ALU.mult)
                frees(key, ins)
                dve.wait_ge(*freed(key))
                dve.sem_inc(rows_ready, 1)

            def residual(layer, b):
                key = ("wo", layer, b)
                dve.wait_ge(*multiplied((key, 3)))
                frees(key, nc.vector.tensor_tensor(h[:, b, :], h[:, b, :], flat(pair_of(key)), ALU.add))
                dve.wait_ge(*freed(key))
                dve.sem_inc(h_ready, 1)

            def top16(src, n, groups, vals, at, work):
                for g in range(groups):
                    ins = nc.vector.max(vals[:, g, 0:8], src[:, g, :])
                chained(ins)
                for g in range(groups):
                    nc.vector.max_index(at[:, g, 0:8], vals[:, g, 0:8], src[:, g, :])
                    ins = nc.vector.match_replace(work[:, g, :], vals[:, g, 0:8], src[:, g, :], LOW)
                chained(ins)
                for g in range(groups):
                    ins = nc.vector.max(vals[:, g, 8:16], work[:, g, :])
                chained(ins)
                for g in range(groups):
                    ins = nc.vector.max_index(at[:, g, 8:16], vals[:, g, 8:16], work[:, g, :])
                return ins

            def choose_keys(layer, b, j):
                key = ("route", layer, b, j)
                dve.wait_ge(*full(key))
                s = pair_of(key)[:, 1, :].rearrange("p (g n) -> p g n", g=4)
                work = scratch[:, 0:HALF].rearrange("p (g n) -> p g n", g=4)
                ins = top16(s, RK, 4, top, top_at, work)
                frees(key, ins)
                dve.wait_ge(*freed(key))
                chained(nc.vector.tensor_copy(top_id[:, :, :], top_at[:, :, :]))

            def choose_pairs(layer, b, j):
                cand = scratch[:, HALF:2 * HALF].rearrange("p (g i j) -> p g i j", g=2, i=RTOP)
                tv = top[:, :, :].rearrange("p (g c) k -> p g c k", c=2)
                chained(nc.vector.tensor_tensor(cand, tv[:, :, 0, :].unsqueeze(3).broadcast_to([P, 2, RTOP, RTOP]),
                                                tv[:, :, 1, :].unsqueeze(2).broadcast_to([P, 2, RTOP, RTOP]),
                                                ALU.add))
                cv = scratch[:, HALF:2 * HALF].rearrange("p (g n) -> p g n", g=2)
                chained(top16(cv, RTOP * RTOP, 2, best[:, b, 2 * j:2 * j + 2, :], best_at,
                              scratch[:, 2 * HALF:3 * HALF].rearrange("p (g n) -> p g n", g=2)))
                e = gate_e[:, j * 2 * RTOP:(j + 1) * 2 * RTOP].rearrange("p (h k) -> p h k", h=2)
                bb = best[:, b, 2 * j:2 * j + 2, :]
                nc.vector.tensor_tensor(e, bb, bb[:, :, 0:1].broadcast_to([P, 2, RTOP]), ALU.subtract
                                        ).then_inc(gate_x_ready, 1)

            def number(layer, b, j):
                nc.vector.tensor_scalar(digit[:, :, 0, :], best_at[:, :, :], 4, None, ALU.logical_shift_right)
                chained(nc.vector.tensor_scalar(digit[:, :, 1, :], best_at[:, :, :], RTOP - 1, None, ALU.bitwise_and))
                hot = scratch[:, 3 * HALF:5 * HALF].rearrange("p (g s k) -> p g s k", g=4, k=RTOP)
                hot_s = hot.rearrange("p g s k -> p (g s) k")
                chained(nc.vector.tensor_tensor(
                    hot_s, iota16[:, :].unsqueeze(1).broadcast_to([P, 4 * RTOP, RTOP]),
                    digit[:, :, :, :].rearrange("p g c s -> p (g c s)").unsqueeze(2).broadcast_to([P, 4 * RTOP, RTOP]),
                    ALU.is_equal))
                chained(nc.vector.tensor_tensor(
                    hot, hot, top_id[:, :, :].unsqueeze(2).broadcast_to([P, 4, RTOP, RTOP]), ALU.mult))
                chained(nc.vector.tensor_reduce(picked[:, :, :, :].rearrange("p g c s -> p (g c s)"), hot_s,
                                                AX_X, ALU.add))
                own = slice(j * 2 * RTOP, (j + 1) * 2 * RTOP)
                chained(nc.vector.scalar_tensor_tensor(out=ids_f[:, :, :], in0=picked[:, :, 0, :], scalar=float(RK),
                                                       in1=picked[:, :, 1, :], op0=ALU.mult, op1=ALU.add))
                nc.vector.tensor_scalar(ids[:, b, own].rearrange("p (g s) -> p g s", g=2), ids_f[:, :, :],
                                        float(layer * EXPERTS), None, ALU.add)
                n = (layer * TILES + b) * 4 + j
                e = gate_e[:, own].rearrange("p (h k) -> p h k", h=2)
                dve.wait_ge(gate_e_ready, n + 1)
                chained(nc.vector.tensor_reduce(gate_sum[:, 2 * j:2 * j + 2], e, AX_X, ALU.add))
                chained(nc.vector.reciprocal(gate_inv[:, 2 * j:2 * j + 2], gate_sum[:, 2 * j:2 * j + 2]))
                nc.vector.tensor_tensor(gates[:, b, own].rearrange("p (h k) -> p h k", h=2), e,
                                        gate_inv[:, 2 * j:2 * j + 2].unsqueeze(2).broadcast_to([P, 2, RTOP]), ALU.mult
                                        ).then_inc(routed, 1)
                dve.wait_ge(routed, n + 1)

            def forget_gate(b):
                key = ("fl", b)
                z = pair_of(key)[0:FH, 0, 0:P]
                dve.wait_ge(*multiplied((key, 0)))
                dve.wait_ge(f_abs_ready, b + 1)
                ins = nc.vector.tensor_scalar(forget[:, 1, :], z, b_f[:, 0:1], 0.0, ALU.add, ALU.min)
                frees(key, ins)
                dve.wait_ge(*freed(key))
                dve.wait_ge(f_log_ready, b + 1)
                chained(nc.vector.tensor_tensor(forget[:, 3, :], forget[:, 1, :], forget[:, 2, :], ALU.subtract))
                t = slice(b * P, (b + 1) * P)
                chained(nc.vector.tensor_tensor_scan(cumT[:, t], ones[0:FH, :], forget[:, 3, :],
                                                     cumT[:, b * P - 1:b * P] if b else 0.0, ALU.mult, ALU.add))
                nc.vector.tensor_scalar(neg_cumT[:, t], cumT[:, t], -1.0, None, ALU.mult).then_inc(cum_ready, 1)

            def att_max(b, c):
                key = ("att", b, c)
                dve.wait_ge(*full(key))
                n = (b + 1) * P
                s = pair_of(key)[:, 0, 0:2 * n].rearrange("p (g s) -> p g s", g=2)
                nc.vector.tensor_reduce(neg_max[:, b, 2 * c:2 * c + 2], s, AX_X, ALU.max, negate=True
                                        ).then_inc(max_ready, 1)

            def att_norm(b, c):
                key = ("att", b, c)
                n = b * (FH // 2) + c
                dve.wait_ge(probs_ready, n + 1)
                chained(nc.vector.reciprocal(prob_inv[:, b, 2 * c:2 * c + 2], prob_sum[:, b, 2 * c:2 * c + 2]))
                dve.wait_ge(pv_full, n + 1)
                if c == 0:
                    dve.wait_ge(*full(("T", "mix1", b)))
                ins = nc.vector.tensor_tensor(
                    rows[:, c * P:(c + 1) * P].rearrange("p (g d) -> p g d", g=2),
                    pair_of(key)[:, 0, 0:P].rearrange("p (g d) -> p g d", g=2),
                    prob_inv[:, b, 2 * c:2 * c + 2].unsqueeze(2).broadcast_to([P, 2, FHD]), ALU.mult)
                frees(key, ins)
                if c == FH // 2 - 1:
                    dve.wait_ge(*freed(key))
                    dve.sem_inc(rows_ready, 1)

            def attention(b, first, last):
                for i in range(first, last):
                    if i < FH // 2:
                        att_max(b, i)
                    if i >= 2:
                        att_norm(b, i - 2)

            def half(ph, r, q):
                layer, b = PHASES[ph]
                dve.wait_ge(dots_free, r * (RING // SUB) + (q + 1))
                for j in range(q * SUB, (q + 1) * SUB):
                    dve.wait_ge(u_loaded[j], r * 16 + 16)
                    nc.vector.tensor_tensor_reduce(
                        out=u_ring[:, j, :], in0=u_ring[:, j, :], in1=xn[:, b, :], scale=1.0, scalar=0.0,
                        op0=ALU.mult, op1=ALU.add, accum_out=dots[:, j:j + 1]).then_inc(u_free, 1)
                    if j != SUB:
                        continue
                    dve.wait_ge(gelu_ready, r * (RING // SUB) + 1)
                    for k, jv in enumerate(VEC_SLOTS):
                        dve.wait_ge(v_loaded[jv], r * 16 + 16)
                        dve.wait_ge(vec_free, r * VEC + (VEC + k))
                        nc.vector.scalar_tensor_tensor(
                            out=h[:, b, :], in0=v_ring[:, jv, :], scalar=weights_s[:, jv:jv + 1],
                            in1=h[:, b, :], op0=ALU.mult, op1=ALU.add).then_inc(vec_free, 1)

            def experts(ph, first, last):
                in_halves(dve, half, ph, first, last)

            def experts_end(ph):
                layer, b = PHASES[ph]
                dve.wait_ge(vec_free, (ph + 1) * ROUNDS * VEC + VEC)
                dve.wait_ge(acc_full, ph + 1)
                nc.vector.tensor_tensor(h[:, b, :], h[:, b, :], flat(acc), ALU.add).then_inc(acc_free, 1)
                dve.wait_ge(acc_free, ph + 1)
                dve.sem_inc(h_ready, 1)

            dve.sem_inc(u_free, RING)
            dve.sem_inc(vec_free, VEC)
            dve.wait_ge(x_loaded[0], 16)
            norm(("mix0", 0), rows[:, :], 0)
            dve.wait_ge(*full(("T", "mix0", 0)))
            dve.wait_ge(x_loaded[1], 16)
            norm(("mix0", 1), rows[:, :], 1)
            dve.wait_ge(small_loaded, 48)
            dve.wait_ge(*full("z"))
            zp = flat(pair_of("z")).rearrange("p (h b t) -> p h b t", h=GH, b=TILES)
            dve.wait_ge(z_abs_ready, 1)
            zm = scratch[:, 2 * D:3 * D].rearrange("p (b h t) -> p b h t", b=TILES, h=GH)
            for g in range(GH):
                ins = nc.vector.tensor_scalar(zm[:, :, g, :], zp[:, g, :, :], b_g[:, g:g + 1], 0.0, ALU.add, ALU.min)
            frees("z", ins)
            dve.wait_ge(*freed("z"))
            dve.wait_ge(z_log_ready, 1)
            dflat = decay[:, :, :, :].rearrange("p b h t -> p (b h t)")
            chained(nc.vector.tensor_tensor(dflat, scratch[:, 2 * D:3 * D], scratch[:, D:2 * D], ALU.subtract))
            chained(nc.vector.tensor_scalar(dflat, dflat, 1.0 / GTAU, None, ALU.mult))
            for b in range(TILES):
                for g in range(GH):
                    t = scratch[:, 3 * D + (b * GH + g) * P:3 * D + (b * GH + g + 1) * P]
                    ins = nc.vector.tensor_tensor_scan(t, ones[:, :], decay[:, b, g, :], 0.0, ALU.mult, ALU.add)
            chained(ins)
            chained(nc.vector.tensor_copy(dflat, scratch[:, 3 * D:4 * D]))
            kd = scratch[:, 3 * D:3 * D + HALF].rearrange("p (h t) -> p h t", h=GH)
            nc.vector.tensor_tensor(kd, decay[:, 0, :, P - 1:P].broadcast_to([P, GH, P]), decay[:, 0, :, :],
                                    ALU.subtract).then_inc(z_ready, 1)
            dve.wait_ge(masks_f_ready, 1)
            nc.vector.tensor_copy(masks[:, :, :], scratch[:, 0:LEVELS * P].rearrange("p (l t) -> p l t", l=LEVELS)
                                  ).then_inc(masks_ready, 1)
            dve.wait_ge(masks_ready, 1)
            level_begin(0)
            dve.wait_ge(z_exp_ready, 1)
            dve.wait_ge(*freed("k"))
            nc.vector.tensor_tensor(kd, kd, qkT[:, 0, 1, :, :], ALU.mult).then_inc(z_ready, 1)
            for i in range(LEVELS + 1):
                level_step(0, i)
            dve.wait_ge(silu_ready, 1)
            dve.wait_ge(gain_o_loaded, 16)
            chained(nc.vector.tensor_tensor(gate_o[:, 0, :], gate_o[:, 0, :], gain_o, ALU.mult))

            def first_fox(b):
                if b == 0:
                    nc.vector.memset(gate_o[FHD:P, 0, :], 0.0)
                    nc.vector.memset(gate_o[0:FHD, 1, :], 0.0).then_inc(q_zeroed, 1)
                norm(("kv", b), rows[:, :], NORMS.index(("kv", b)))

            def mixed(layer, b):
                residual(layer, b)
                norm((f"ffn{layer}", b), xn[:, b, :], NORMS.index((f"ffn{layer}", b)))

            gla_out(0)
            residual(0, 0)
            norm(("ffn0", 0), xn[:, 0, :], NORMS.index(("ffn0", 0)))
            choose_keys(0, 0, 0)
            choose_pairs(0, 0, 0)
            number(0, 0, 0)

            experts(0, 0, 1)
            dve.wait_ge(silu_ready, 2)
            nc.vector.tensor_tensor(gate_o[:, 1, :], rows[:, :], gain_o, ALU.mult)
            choose_keys(0, 0, 1)
            experts(0, 1, 2)
            choose_pairs(0, 0, 1)
            experts(0, 2, 3)
            number(0, 0, 1)
            choose_keys(0, 0, 2)
            experts(0, 3, 4)
            choose_pairs(0, 0, 2)
            experts(0, 4, 5)
            number(0, 0, 2)
            experts(0, 5, 6)
            choose_keys(0, 0, 3)
            experts(0, 6, 7)
            choose_pairs(0, 0, 3)
            experts(0, 7, 8)
            number(0, 0, 3)
            experts(0, 8, 9)
            level_begin(1)
            for i in range(LEVELS + 1):
                experts(0, 9 + i, 10 + i)
                level_step(1, i)
            dve.wait_ge(z_exp_ready, 2)
            qf = scratch[:, 3 * D:3 * D + HALF].rearrange("p (h t) -> p h t", h=GH)
            nc.vector.tensor_tensor(qf, qf, qkT[:, 1, 0, :, :], ALU.mult).then_inc(z_ready, 1)
            experts(0, 18, 20)
            gla_out(1)
            experts(0, 20, 23)
            residual(0, 1)
            experts(0, 23, 24)
            norm(("ffn0", 1), xn[:, 1, :], NORMS.index(("ffn0", 1)))
            experts(0, 24, 27)
            choose_keys(0, 1, 0)
            experts(0, 27, 28)
            choose_pairs(0, 1, 0)
            experts(0, 28, 29)
            number(0, 1, 0)
            experts(0, 29, HALVES)

            for ph, b in ((1, 0), (2, 1)):
                before = PHASES[ph]
                experts(ph, 0, 1)
                experts_end(ph - 1)
                experts(ph, 1, 3)
                first_fox(b)
                choose_keys(*before, 1)
                experts(ph, 3, 4)
                choose_pairs(*before, 1)
                experts(ph, 4, 5)
                number(*before, 1)
                experts(ph, 5, 9)
                choose_keys(*before, 2)
                experts(ph, 9, 10)
                norm(("mix1", b), rows[:, :], NORMS.index(("kv", b)))
                choose_pairs(*before, 2)
                experts(ph, 10, 11)
                forget_gate(b)
                number(*before, 2)
                experts(ph, 11, 12)
                choose_keys(*before, 3)
                experts(ph, 12, 13)
                choose_pairs(*before, 3)
                experts(ph, 13, 14)
                number(*before, 3)
                experts(ph, 14, 15)
                attention(b, 0, 3)
                experts(ph, 15, 17)
                attention(b, 3, 6)
                experts(ph, 17, 19)
                attention(b, 6, FH // 2 + 2)
                experts(ph, 19, 22)
                residual(1, b)
                experts(ph, 22, 23)
                norm(("ffn1", b), xn[:, b, :], NORMS.index(("ffn1", b)))
                experts(ph, 23, 26)
                choose_keys(1, b, 0)
                experts(ph, 26, 27)
                choose_pairs(1, b, 0)
                experts(ph, 27, 28)
                number(1, b, 0)
                experts(ph, 28, HALVES)

            experts(3, 0, 1)
            experts_end(2)
            experts(3, 1, 3)
            for j in range(1, 4):
                choose_keys(1, 1, j)
                experts(3, 3 * j, 3 * j + 1)
                choose_pairs(1, 1, j)
                experts(3, 3 * j + 1, 3 * j + 2)
                number(1, 1, j)
                experts(3, 3 * j + 2, 3 * j + 3)
            norm(("final", 0), xn[:, 0, :], NORMS.index(("final", 0)))
            experts(3, 12, HALVES - 2)
            experts(3, HALVES - 2, HALVES)
            dve.wait_ge(gelu_ready, len(PHASES) * HALVES)
            dve.wait_ge(vec_free, (len(PHASES) * ROUNDS + 1) * VEC)
            for j in range(LAST_VEC, RING):
                dve.wait_ge(v_loaded[j], 16 * len(PHASES) * ROUNDS)
                chained(nc.vector.scalar_tensor_tensor(
                    out=h[:, 1, :], in0=v_ring[:, j, :], scalar=weights_s[:, j:j + 1], in1=h[:, 1, :],
                    op0=ALU.mult, op1=ALU.add))
            experts_end(3)
            norm(("final", 1), xn[:, 1, :], NORMS.index(("final", 1)))

        @block.scalar
        def _(act):
            steps = 0

            def chained(ins):
                nonlocal steps
                steps += 1
                ins.then_inc(act_step, 1)
                act.wait_ge(act_step, steps)

            def mean_square(n):
                key = NORMS[n]
                if key in H_OF_NORM:
                    act.wait_ge(*version(H_OF_NORM[key]))
                square_sum(n)
                root(n)

            def square_sum(n):
                chained(nc.scalar.activation(square[:, :], h[:, NORMS[n][1], :], ACT.Square,
                                             accum_out=sumsq[:, n:n + 1]))

            def root(n):
                nc.scalar.activation(rms[:, n:n + 1], sumsq[:, n:n + 1], ACT.Sqrt, bias=eps[:, 0:1], scale=1.0 / D
                                     ).then_inc(rms_ready, 1)

            def take_rows(key):
                use = ("T",) + key
                act.wait_ge(*full(use))
                frees(use, nc.scalar.activation(
                    xT[:, t_at(key) % 2, :, :].rearrange("p c t -> p (c t)"), flat(pair_of(use)), ACT.Copy))

            def fade(b, i):
                act.wait_ge(diff_ready, b * (LEVELS - 1) + i + 1)
                d = scratch[:, (i % 2) * HALF:(i % 2 + 1) * HALF]
                nc.scalar.activation(d, d, ACT.Exp).then_inc(fade_ready, 1)

            def heads_square(b):
                key = ("o", b)
                act.wait_ge(*full(key))
                o = flat(pair_of(key))
                for g in range(GH):
                    ins = nc.scalar.activation(square[:, g * GDV:(g + 1) * GDV], o[:, g * GDV:(g + 1) * GDV],
                                               ACT.Square, accum_out=head_ss[:, b, g:g + 1])
                chained(ins)
                nc.scalar.activation(head_rms[:, b, :], head_ss[:, b, :], ACT.Sqrt, bias=eps[:, 0:1],
                                     scale=1.0 / GDV).then_inc(head_ss_ready, 1)

            def take_query(layer, b, j):
                n = (layer * TILES + b) * 4 + j
                act.wait_ge(queryT_full, n + 1)
                nc.scalar.activation(queryT[:, :, :].rearrange("p c t -> p (c t)"),
                                     pair_of(("route", layer, b, j))[:, 0, :], ACT.Copy).then_inc(queryT_ready, 1)

            def gate_exp(layer, b, j):
                act.wait_ge(gate_x_ready, (layer * TILES + b) * 4 + j + 1)
                e = gate_e[:, j * 2 * RTOP:(j + 1) * 2 * RTOP]
                nc.scalar.activation(e, e, ACT.Exp).then_inc(gate_e_ready, 1)

            def take_keys(layer):
                for i in range(2):
                    use = ("keys", layer, i)
                    act.wait_ge(*full(use))
                    frees(use, nc.scalar.activation(
                        keysT[:, i * KC:(i + 1) * KC, :].rearrange("p g n -> p (g n)"), flat(pair_of(use)), ACT.Copy))

            def probs_of(n):
                o = (n % 2) * D
                return scratch[:, o:o + 2 * TILES * P], scratch[:, o + HALF:o + D]

            def att_exp(b, c):
                n = b * (FH // 2) + c
                s_n = (b + 1) * P
                act.wait_ge(max_ready, n + 1)
                if c >= 2:
                    act.wait_ge(probsT_full, n - 1)
                for g in range(2):
                    hh = 2 * c + g
                    ins = nc.scalar.activation(probs_of(n)[0][:, g * s_n:(g + 1) * s_n],
                                               pair_of(("att", b, c))[:, 0, g * s_n:(g + 1) * s_n], ACT.Exp,
                                               bias=neg_max[:, b, hh:hh + 1], accum_out=prob_sum[:, b, hh:hh + 1])
                ins.then_inc(probs_ready, 1)

            def att_take(b, c):
                n = b * (FH // 2) + c
                act.wait_ge(probsT_full, n + 1)
                if c >= 2:
                    act.wait_ge(pv_full, n - 1)
                w = 2 * (b + 1) * P
                nc.scalar.activation(probs_of(n)[1][:, 0:w], pair_of(("att", b, c))[:, 1, 0:w], ACT.Copy
                                     ).then_inc(probsT_ready, 1)

            def half(ph, r, q):
                layer, b = PHASES[ph]
                s = slice(q * SUB, (q + 1) * SUB)
                act.wait_ge(u_free, r * RING + (RING + (q + 1) * SUB))
                nc.scalar.activation(gelus[:, s], dots[:, s], ACT.Gelu).then_inc(dots_free, 1)
                act.wait_ge(dots_free, r * (RING // SUB) + (RING // SUB + q + 1))
                if q == 0:
                    act.wait_ge(vec_free, r * VEC + VEC)
                for j in range(q * SUB, (q + 1) * SUB):
                    ins = nc.scalar.activation(
                        weights_s[:, j:j + 1], gelus[:, j:j + 1], ACT.Copy,
                        scale=gates[:, b, bass.ds(r * RING + (j - ph * SLOTS), 1)])
                ins.then_inc(gelu_ready, 1)
                act.wait_ge(gelu_ready, r * (RING // SUB) + (q + 1))
                for k, j in enumerate(PE_SLOTS):
                    if j // SUB == q and not is_last(r, j):
                        act.wait_ge(v_free, r * len(PE_SLOTS) + (k + 1))
                        nc.scalar.activation(diag[:, k, :], ident[:, :], ACT.Copy,
                                             scale=weights_s[:, j:j + 1]).then_inc(diag_ready, 1)

            def experts(ph, first, last):
                quarter = (last - 1) * 4 // HALVES
                act.wait_ge(routed, ph * 4 + quarter + 1)
                in_halves(act, half, ph, first, last)

            act.sem_inc(dots_free, RING // SUB)
            act.wait_ge(consts, 3)
            nc.scalar.activation(rms[:, 0:1], eps[:, :], ACT.Sqrt)
            for b in range(TILES):
                act.wait_ge(x_loaded[b], 16)
                square_sum(b)
            for b in range(TILES):
                root(b)
            for b in range(TILES):
                take_rows(("mix0", b))
            act.wait_ge(*multiplied(("glr", 0)))
            frees("glr", nc.scalar.activation(glrT[:, :], pair_of("glr")[0:GRANK, 0, 0:TILES * P], ACT.Copy))
            za = scratch[:, D:2 * D]
            act.wait_ge(*full("z"))
            act.wait_ge(small_loaded, 48)
            zp = flat(pair_of("z")).rearrange("p (h b t) -> p h b t", h=GH, b=TILES)
            za4 = za.rearrange("p (b h t) -> p b h t", b=TILES, h=GH)
            for g in range(GH):
                ins = nc.scalar.activation(za4[:, :, g, :], zp[:, g, :, :], ACT.Abs, bias=b_g[:, g:g + 1])
            ins.then_inc(z_abs_ready, 1)
            act.wait_ge(z_abs_ready, 1)
            chained(nc.scalar.activation(za, za, ACT.Exp, scale=-1.0))
            nc.scalar.activation(za, za, ACT.Ln, bias=1.0).then_inc(z_log_ready, 1)
            act.wait_ge(z_ready, 1)
            kd = scratch[:, 3 * D:3 * D + HALF]
            nc.scalar.activation(kd, kd, ACT.Exp).then_inc(z_exp_ready, 1)
            fade(0, 0)
            for key, at, scale in (("q", 0, float(GDK) ** -0.5), ("k", 1, 1.0)):
                act.wait_ge(*multiplied((key, 1)))
                frees(key, nc.scalar.activation(
                    qkT[:, :, at, :, :], flat(pair_of(key)).rearrange("p (h b t) -> p b h t", h=GH, b=TILES),
                    ACT.Copy, scale=scale))
            for i in range(1, 4):
                fade(0, i)
            nc.scalar.activation(xT_kept, xT[:, 1, :, :], ACT.Copy).then_inc(kept_ready, 1)
            act.wait_ge(*full(("v", 0)))
            frees(("v", 0), nc.scalar.activation(vtok[:, 0, :], flat(pair_of(("v", 0))), ACT.Copy))
            for i in range(4, LEVELS - 1):
                fade(0, i)
            act.wait_ge(*full(("r", 0)))
            frees(("r", 0), nc.scalar.activation(gate_o[:, 0, :], flat(pair_of(("r", 0))), ACT.Silu))
            act.wait_ge(*freed(("r", 0)))
            act.sem_inc(silu_ready, 1)

            def attention(b, first, last):
                for i in range(first, last):
                    if i < FH // 2:
                        att_exp(b, i)
                    if 1 <= i <= FH // 2:
                        att_take(b, i - 1)

            heads_square(0)
            take_keys(0)
            take_rows(("o0", 0))
            mean_square(NORMS.index(("ffn0", 0)))
            take_rows(("ffn0", 0))
            take_query(0, 0, 0)
            act.wait_ge(*multiplied(("v", 3)))
            frees(("v", 1), nc.scalar.activation(vtok[:, 1, :], flat(pair_of(("v", 1))), ACT.Copy))
            gate_exp(0, 0, 0)
            act.wait_ge(*multiplied(("r", 3)))
            frees(("r", 1), nc.scalar.activation(rows[:, :], flat(pair_of(("r", 1))), ACT.Silu))
            act.wait_ge(*freed(("r", 1)))
            act.sem_inc(silu_ready, 1)
            take_query(0, 0, 1)

            experts(0, 0, 2)
            take_query(0, 0, 2)
            gate_exp(0, 0, 1)
            experts(0, 2, 4)
            gate_exp(0, 0, 2)
            experts(0, 4, 5)
            take_query(0, 0, 3)
            experts(0, 5, 7)
            gate_exp(0, 0, 3)
            act.wait_ge(*full("kdec"))
            frees("kdec", nc.scalar.activation(kdec[:, :, :].rearrange("p h k -> p (h k)"),
                                               pair_of("kdec")[:, 0, :], ACT.Copy))
            experts(0, 7, 8)
            act.wait_ge(*full("state"))
            frees("state", nc.scalar.activation(state[:, :, :].rearrange("p h v -> p (h v)"),
                                                flat(pair_of("state")), ACT.Copy))
            for i in range(LEVELS - 1):
                experts(0, 8 + i, 9 + i)
                fade(1, i)
            experts(0, 15, 16)
            nc.scalar.activation(scratch[:, 3 * D:3 * D + HALF],
                                 decay[:, 1, :, :].rearrange("p h t -> p (h t)"), ACT.Exp).then_inc(z_exp_ready, 1)
            experts(0, 16, 19)
            heads_square(1)
            experts(0, 19, 21)
            take_rows(("o0", 1))
            experts(0, 21, 23)
            mean_square(NORMS.index(("ffn0", 1)))
            experts(0, 23, 25)
            take_rows(("ffn0", 1))
            experts(0, 25, 26)
            take_query(0, 1, 0)
            experts(0, 26, 28)
            gate_exp(0, 1, 0)
            experts(0, 28, HALVES)

            for ph, b in ((1, 0), (2, 1)):
                before = PHASES[ph]
                experts(ph, 0, 2)
                take_query(*before, 1)
                mean_square(NORMS.index(("kv", b)))
                experts(ph, 2, 4)
                gate_exp(*before, 1)
                take_rows(("kv", b))
                experts(ph, 4, 6)
                act.wait_ge(*multiplied((("K", b), 3)))
                frees(("K", b), nc.scalar.activation(
                    qkT[:, b, :, :, :].rearrange("p a c t -> p (a c) t"),
                    flat(pair_of(("K", b))).rearrange("p (c t) -> p c t", c=KC), ACT.Copy))
                experts(ph, 6, 8)
                take_query(*before, 2)
                experts(ph, 8, 10)
                act.wait_ge(*multiplied((("V", b), 3)))
                frees(("V", b), nc.scalar.activation(v2[:, b, :], flat(pair_of(("V", b))), ACT.Copy))
                act.wait_ge(*multiplied((("fl", b), 0)))
                if b:
                    act.wait_ge(cum_ready, b)
                nc.scalar.activation(forget[:, 0, :], pair_of(("fl", b))[0:FH, 0, 0:P], ACT.Abs,
                                     bias=b_f[:, 0:1]).then_inc(f_abs_ready, 1)
                act.wait_ge(f_abs_ready, b + 1)
                chained(nc.scalar.activation(forget[:, 2, :], forget[:, 0, :], ACT.Exp, scale=-1.0))
                nc.scalar.activation(forget[:, 2, :], forget[:, 2, :], ACT.Ln, bias=1.0).then_inc(f_log_ready, 1)
                gate_exp(*before, 2)
                experts(ph, 10, 11)
                take_query(*before, 3)
                experts(ph, 11, 12)
                take_rows(("mix1", b))
                experts(ph, 12, 13)
                gate_exp(*before, 3)
                experts(ph, 13, 14)
                act.wait_ge(*multiplied((("Q", b), 3)))
                act.wait_ge(q_zeroed, 1)
                src = flat(pair_of(("Q", b))).rearrange("p (c t) -> p c t", c=KC)
                for g in range(2):
                    pp = slice(g * FHD, (g + 1) * FHD)
                    ins = nc.scalar.activation(q2T[g][pp, :, :], src[pp, :, :], ACT.Copy,
                                               scale=float(FHD) ** -0.5)
                frees(("Q", b), ins)
                experts(ph, 14, 15)
                attention(b, 0, 3)
                experts(ph, 15, 17)
                attention(b, 3, 6)
                experts(ph, 17, 19)
                attention(b, 6, FH // 2 + 1)
                experts(ph, 19, 20)
                take_rows(("o1", b))
                experts(ph, 20, 22)
                mean_square(NORMS.index(("ffn1", b)))
                experts(ph, 22, 23)
                if b == 0:
                    take_keys(1)
                experts(ph, 23, 24)
                take_rows(("ffn1", b))
                experts(ph, 24, 25)
                take_query(1, b, 0)
                experts(ph, 25, 27)
                gate_exp(1, b, 0)
                experts(ph, 27, HALVES)

            experts(3, 0, 2)
            for j in range(1, 4):
                take_query(1, 1, j)
                experts(3, 3 * j - 1, 3 * j + 1)
                gate_exp(1, 1, j)
                experts(3, 3 * j + 1, 3 * j + 2)
            mean_square(NORMS.index(("final", 0)))
            experts(3, 11, HALVES - 2)
            experts(3, HALVES - 2, HALVES)
            nc.scalar.activation(rms[:, len(NORMS) - 1:], eps[:, :], ACT.Sqrt)
            mean_square(NORMS.index(("final", 1)))

        @block.tensor
        def _(pe):
            order = list(PAIR_USE)
            taken = 0

            def take(key):
                nonlocal taken
                p, n = PAIR_USE[key]
                assert key == order[taken], (key, order[taken])
                taken += 1
                if n:
                    pe.wait_ge(pair_free[p], n)
                return pairs[p]

            def fills(key, ins):
                ins.then_inc(pair_full[PAIR_USE[key][0]], 1)

            def block_of(key):
                place, n, _ = PLACE_OF[key]
                pe.wait_ge(w_loaded[place], 16 * n)
                return places[place]

            def transpose_rows(key, src):
                use = ("T",) + key
                dst = take(use)
                pe.wait_ge(rows_ready, t_at(key) + 1)
                for c in range(KC):
                    ins = nc.tensor.transpose(dst[:, c // 4, (c % 4) * P:(c % 4 + 1) * P],
                                              src[:, c * P:(c + 1) * P], ident[:, :])
                fills(use, ins)

            def product_T(key, i, slots, dst, n=WCOLS):
                w = block_of((key, i))
                nt = len(slots) * P
                for m in range(0, n, P):
                    mm = min(P, n - m)
                    for c in range(KC):
                        rhs = xT[:, slots[0], c, :] if len(slots) == 1 else xT[:, :, c, :]
                        ins = nc.tensor.matmul(dst(m // P, mm, nt), w[:, c, m:m + mm], rhs,
                                               start=(c == 0), stop=(c == KC - 1))
                ins.then_inc(w_used, 1)

            def product(key, i, x, dst):
                w = block_of((key, i))
                for c in range(KC):
                    ins = nc.tensor.matmul(dst[:, i // 2, (i % 2) * WCOLS:(i % 2 + 1) * WCOLS],
                                           x[:, c, :], w[:, c, :], start=(c == 0), stop=(c == KC - 1))
                return ins

            def last_product(key, i, x, dst):
                product(key, i, x, dst).then_inc(w_used, 1)

            def transpose_keys(layer):
                raw = block_of((("keys", layer), 0)).rearrange("p c n -> p (c n)").rearrange("p (g d) -> p g d", d=RK)
                for i in range(2):
                    dst = take(("keys", layer, i))
                    for c in range(KC):
                        ins = nc.tensor.transpose(dst[:, c // 4, (c % 4) * P:(c % 4 + 1) * P],
                                                  raw[:, i * KC + c, :], ident[:, :])
                    fills(("keys", layer, i), ins)
                pe.wait_ge(*full(("keys", layer, 1)))
                pe.sem_inc(w_used, 1)

            def level(b, i):
                key = ("level", b, i)
                dst = take(key)
                if i < LEVELS - 1:
                    pe.wait_ge(faded_ready, b * (LEVELS - 1) + i + 1)
                for g in range(GH):
                    if i < LEVELS - 1:
                        o = D + (i % 2) * HALF + g * P
                        kk = qq = scratch[:, o:o + P]
                    else:
                        kk, qq = qkT[:, b, 1, g, :], qkT[:, b, 0, g, :]
                    ins = nc.tensor.matmul(dst[:, 0, g * P:(g + 1) * P], kk, qq, start=True, stop=True)
                fills(key, ins)

            def gla_heads(b):
                key = ("o", b)
                dst = flat(take(key))
                pe.wait_ge(attn_ready, b + 1)
                if b:
                    pe.wait_ge(z_ready, 3)
                    pe.wait_ge(*freed("state"))
                for g in range(GH):
                    c = slice(g * GDV, (g + 1) * GDV)
                    if b:
                        nc.tensor.matmul(dst[:, c], scratch[:, 3 * D + g * P:3 * D + (g + 1) * P], state[:, g, :],
                                         start=True, stop=False)
                    ins = nc.tensor.matmul(dst[:, c], attnT[:, g, :], vtok[:, b, c], start=(b == 0), stop=True)
                fills(key, ins)

            def queries(layer, b, j):
                key = ("route", layer, b, j)
                n = (layer * TILES + b) * 4 + j
                dst = take(key)
                slot = t_at((f"ffn{layer}", b)) % 2
                for i in (2 * j, 2 * j + 1):
                    w = block_of((("pq", layer, b), i))
                    for m in range(2):
                        o = ((i % 2) * 2 + m) * P
                        for c in range(KC):
                            ins = nc.tensor.matmul(dst[:, 0, o:o + P], w[:, c, m * P:(m + 1) * P], xT[:, slot, c, :],
                                                   start=(c == 0), stop=(c == KC - 1))
                    if i == 2 * j:
                        ins.then_inc(w_used, 1)
                    else:
                        ins.then_inc(queryT_full, 1)
                pe.wait_ge(queryT_full, n + 1)
                pe.sem_inc(w_used, 1)

            def scores(layer, b, j):
                key = ("route", layer, b, j)
                n = (layer * TILES + b) * 4 + j
                dst = pair_of(key)
                pe.wait_ge(queryT_ready, n + 1)
                for g in range(4):
                    ins = nc.tensor.matmul(dst[:, 1, g * P:(g + 1) * P], queryT[:, g, :], keysT[:, 4 * j + g, :],
                                           start=True, stop=True)
                fills(key, ins)

            def att_logits(b, c):
                key = ("att", b, c)
                dst = take(key)
                n = (b + 1) * P
                for g in range(2):
                    o = g * n
                    for s in range(b + 1):
                        last = s == b
                        nc.tensor.matmul(dst[:, 0, o + s * P:o + (s + 1) * P], q2T[g][:, c, :],
                                         qkT[:, s, c // 4, c % 4, :], start=True, stop=False)
                        ins = nc.tensor.matmul(dst[:, 0, o + s * P:o + (s + 1) * P],
                                               ident[0:FH, 2 * c + g:2 * c + g + 1].broadcast_to([FH, P]),
                                               neg_cumT[:, s * P:(s + 1) * P], start=False, stop=not last)
                        if last:
                            ins = nc.tensor.matmul(dst[:, 0, o + s * P:o + (s + 1) * P], ident16[:, :],
                                                   causal16[:, :], start=False, stop=True)
                fills(key, ins)

            def att_turn(b, c):
                n = b * (FH // 2) + c
                pe.wait_ge(probs_ready, n + 1)
                o = (n % 2) * D
                for i in range(2 * (b + 1)):
                    ins = nc.tensor.transpose(pair_of(("att", b, c))[:, 1, i * P:(i + 1) * P],
                                              scratch[:, o + i * P:o + (i + 1) * P], ident[:, :])
                ins.then_inc(probsT_full, 1)

            def att_values(b, c):
                n = b * (FH // 2) + c
                pe.wait_ge(probsT_ready, n + 1)
                o = (n % 2) * D + HALF
                for g in range(2):
                    for s in range(b + 1):
                        i = g * (b + 1) + s
                        ins = nc.tensor.matmul(pair_of(("att", b, c))[:, 0, g * FHD:(g + 1) * FHD],
                                               scratch[:, o + i * P:o + (i + 1) * P],
                                               v2[:, s, (2 * c + g) * FHD:(2 * c + g + 1) * FHD],
                                               start=(s == 0), stop=(s == b))
                ins.then_inc(pv_full, 1)

            def experts_begin(ph):
                if ph:
                    pe.wait_ge(acc_free, ph)
                else:
                    pe.wait_ge(*freed(("r", 1)))
                for i in range(2):
                    nc.tensor.matmul(acc[:, i, :], zeros16[:, 0:P], zeros16[:, :], start=True, stop=False)

            def half(ph, r, q):
                for k, j in enumerate(PE_SLOTS):
                    if j // SUB != q or is_last(r, j):
                        continue
                    pe.wait_ge(v_loaded[j], r * 16 + 16)
                    pe.wait_ge(diag_ready, r * len(PE_SLOTS) + (k + 1))
                    for i in range(2):
                        ins = nc.tensor.matmul(acc[:, i, :], diag[:, k, :], v_ring[:, j, i * HALF:(i + 1) * HALF],
                                               start=False, stop=False)
                    ins.then_inc(v_free, 1)

            def experts(ph, first, last):
                in_halves(pe, half, ph, first, last)

            def experts_end(ph):
                for i in range(2):
                    ins = nc.tensor.matmul(acc[:, i, :], zeros16[:, 0:P], zeros16[:, :], start=False, stop=True)
                ins.then_inc(acc_full, 1)

            pe.sem_inc(v_free, len(PE_SLOTS))
            pe.wait_ge(consts, 3)
            for b in range(TILES):
                transpose_rows(("mix0", b), rows)
            for b in range(TILES):
                pe.wait_ge(*freed(("T", "mix0", b)))
            dst = take("glr")
            product_T("glr", 0, [0, 1], lambda m, mm, nt: dst[0:mm, 0, 0:nt], GRANK)
            pe.wait_ge(*freed("glr"))
            pe.wait_ge(small_loaded, 48)
            dst = flat(take("z"))
            for g in range(GH):
                ins = nc.tensor.matmul(dst[:, g * TILES * P:(g + 1) * TILES * P], w_g2[:, g * P:(g + 1) * P],
                                       glrT[:, :], start=True, stop=True)
            fills("z", ins)
            for key in ("q", "k"):
                dst = flat(take(key))
                for i in range(2):
                    product_T(key, i, [0, 1], lambda m, mm, nt: dst[0:mm, (2 * i + m) * nt:(2 * i + m + 1) * nt])
            for i in range(LEVELS):
                key = "v" if i < 4 else "r"
                if i % 4 == 0:
                    dst = take((key, 0))
                ins = product(key, i % 4, xT[:, 0, :, :], dst)
                if i % 4 == 3:
                    fills((key, 0), ins)
                level(0, i)

            def weight_out(layer, b, blocks):
                for i in blocks:
                    last_product(("wo", layer, b), i, xT[:, t_at((f"o{layer}", b)) % 2, :, :], pair_of(("wo", layer, b)))

            def attention(b, first, last):
                for i in range(first, last):
                    if i < FH // 2:
                        att_logits(b, i)
                    if 1 <= i <= FH // 2:
                        att_turn(b, i - 1)
                    if i >= 2:
                        att_values(b, i - 2)

            gla_heads(0)
            v1 = take(("v", 1))
            pe.wait_ge(kept_ready, 1)
            for i in range(2):
                last_product("v", i, xT_kept, v1)
            transpose_keys(0)
            transpose_rows(("o0", 0), rows)
            pe.wait_ge(*freed(("T", "o0", 0)))
            take(("wo", 0, 0))
            weight_out(0, 0, range(4))
            for i in range(2, 4):
                last_product("v", i, xT_kept, v1)
            transpose_rows(("ffn0", 0), xn[:, 0, :])
            pe.wait_ge(*freed(("T", "ffn0", 0)))
            queries(0, 0, 0)
            scores(0, 0, 0)
            r1 = take(("r", 1))
            for i in range(4):
                last_product("r", i, xT_kept, r1)
            queries(0, 0, 1)
            scores(0, 0, 1)

            experts_begin(0)
            experts(0, 0, 1)
            queries(0, 0, 2)
            experts(0, 1, 2)
            scores(0, 0, 2)
            experts(0, 2, 4)
            queries(0, 0, 3)
            experts(0, 4, 5)
            scores(0, 0, 3)
            experts(0, 5, 6)
            pe.wait_ge(z_ready, 2)
            pe.wait_ge(*full(("o", 0)))
            dst = take("kdec")
            for g in range(GH):
                ins = nc.tensor.transpose(dst[:, 0, g * P:(g + 1) * P],
                                          scratch[:, 3 * D + g * P:3 * D + (g + 1) * P], ident[:, :])
            fills("kdec", ins)
            experts(0, 6, 7)
            pe.wait_ge(*freed("kdec"))
            dst = flat(take("state"))
            for g in range(GH):
                c = slice(g * GDV, (g + 1) * GDV)
                ins = nc.tensor.matmul(dst[:, c], kdec[:, g, :], vtok[:, 0, c], start=True, stop=True)
            fills("state", ins)
            experts(0, 7, 9)
            for i in range(LEVELS):
                experts(0, 9 + i, 10 + i)
                level(1, i)
            experts(0, 17, 18)
            gla_heads(1)
            experts(0, 18, 20)
            transpose_rows(("o0", 1), rows)
            experts(0, 20, 21)
            pe.wait_ge(*freed(("T", "o0", 1)))
            take(("wo", 0, 1))
            weight_out(0, 1, (0, 1))
            experts(0, 21, 22)
            weight_out(0, 1, (2, 3))
            experts(0, 22, 24)
            transpose_rows(("ffn0", 1), xn[:, 1, :])
            experts(0, 24, 25)
            pe.wait_ge(*freed(("T", "ffn0", 1)))
            queries(0, 1, 0)
            experts(0, 25, 26)
            scores(0, 1, 0)
            experts(0, 26, HALVES)
            experts_end(0)

            for ph, b in ((1, 0), (2, 1)):
                before = PHASES[ph]
                s_kv, s_mix = t_at(("kv", b)) % 2, t_at(("mix1", b)) % 2
                experts_begin(ph)
                experts(ph, 0, 1)
                queries(*before, 1)
                experts(ph, 1, 2)
                scores(*before, 1)
                experts(ph, 2, 3)
                transpose_rows(("kv", b), rows)
                experts(ph, 3, 4)
                pe.wait_ge(*freed(("T", "kv", b)))
                dst = flat(take(("K", b)))
                for n in range(4):
                    product_T(("K", b), n, [s_kv], lambda m, mm, nt: dst[:, (2 * n + m) * P:(2 * n + m + 1) * P])
                    if n == 1:
                        experts(ph, 4, 5)
                experts(ph, 5, 7)
                queries(*before, 2)
                experts(ph, 7, 8)
                scores(*before, 2)
                dst = take(("V", b))
                for n in range(4):
                    last_product(("V", b), n, xT[:, s_kv, :, :], dst)
                    if n == 1:
                        experts(ph, 8, 9)
                dst2 = take(("fl", b))
                product_T(("fl", b), 0, [s_kv], lambda m, mm, nt: dst2[0:mm, 0, 0:P], FH)
                experts(ph, 9, 10)
                queries(*before, 3)
                experts(ph, 10, 11)
                scores(*before, 3)
                transpose_rows(("mix1", b), rows)
                experts(ph, 11, 12)
                pe.wait_ge(*freed(("T", "mix1", b)))
                dst = flat(take(("Q", b)))
                for n in range(4):
                    product_T(("Q", b), n, [s_mix], lambda m, mm, nt: dst[:, (2 * n + m) * P:(2 * n + m + 1) * P])
                    if n == 1:
                        experts(ph, 12, 13)
                experts(ph, 13, 14)
                for key in ("Q", "K", "V"):
                    pe.wait_ge(*freed((key, b)))
                pe.wait_ge(cum_ready, b + 1)
                attention(b, 0, 3)
                experts(ph, 14, 16)
                attention(b, 3, 6)
                experts(ph, 16, 18)
                attention(b, 6, FH // 2 + 2)
                experts(ph, 18, 19)
                transpose_rows(("o1", b), rows)
                experts(ph, 19, 20)
                pe.wait_ge(*freed(("T", "o1", b)))
                take(("wo", 1, b))
                weight_out(1, b, (0, 1))
                experts(ph, 20, 21)
                weight_out(1, b, (2, 3))
                experts(ph, 21, 22)
                if b == 0:
                    transpose_keys(1)
                experts(ph, 22, 23)
                transpose_rows(("ffn1", b), xn[:, b, :])
                experts(ph, 23, 24)
                pe.wait_ge(*freed(("T", "ffn1", b)))
                queries(1, b, 0)
                experts(ph, 24, 25)
                scores(1, b, 0)
                experts(ph, 25, HALVES)
                experts_end(ph)

            experts_begin(3)
            experts(3, 0, 1)
            for j in range(1, 4):
                queries(1, 1, j)
                experts(3, 3 * j - 2, 3 * j - 1)
                scores(1, 1, j)
                experts(3, 3 * j - 1, 3 * j + 1)
            experts(3, 10, HALVES - 2)
            experts(3, HALVES - 2, HALVES)
            experts_end(3)


_INS = ["x", "norm_mix", "norm_ffn", "gla_w_in", "gla_w_g2", "gla_b_g", "gla_norm_o", "gla_w_o", "kv_norm", "kv_w",
        "fox_b_f", "fox_w_q", "fox_w_o", "peer_w_q", "peer_sub_keys", "peer_u", "peer_v", "norm_final"]


def kernel(**inputs):
    import numpy as _np
    import concourse.bacc as _bacc
    from concourse import mybir as _mybir
    from concourse.bass_utils import run_bass_kernel_spmd as _run

    nc = _bacc.Bacc("TRN2", target_bir_lowering=False, num_devices=1)
    arrays, args = {}, {}
    for name in _INS:
        v = _np.ascontiguousarray(inputs[name])
        arrays[f"in_{name}"] = v
        args[name] = nc.dram_tensor(f"in_{name}", v.shape, _mybir.dt.from_np(v.dtype), kind="ExternalInput").ap()
    out = nc.dram_tensor("out_0", inputs["x"].shape, _mybir.dt.from_np(_np.dtype("float32")),
                         kind="ExternalOutput").ap()
    yoco_kernel(nc, args, out)
    r = _run(nc, [arrays], core_ids=[0])
    return r.results[0]["out_0"]
```

```python
from contextlib import ExitStack

import concourse.bass as bass
from concourse import mybir

F32 = mybir.dt.float32
BF16 = mybir.dt.bfloat16
U32 = mybir.dt.uint32
U8 = mybir.dt.uint8
ALU = mybir.AluOpType
ACT = mybir.ActivationFunctionType
AX_X = mybir.AxisListType.X

P = 128
D = 1024
KC = D // P
HALF = 512
TILES = 2
EPS = 1e-6
LOW = -3.0e38

GH, GDK, GDV, GRANK, GTAU = 4, 128, 256, 16, 16.0
LEVELS = 8
FH, FHD = 16, 64
RH, RK, RTOP = 8, 128, 16
EXPERTS = RK * RK
SLOTS = RH * RTOP

RING = 8
SUB = 4
ISSUE = 4
ROUNDS = SLOTS // RING
VEC_SLOTS = [2, 3]
PE_SLOTS = [j for j in range(RING) if j not in VEC_SLOTS]
VEC = len(VEC_SLOTS)
QUARTER = ROUNDS // 4
HALVES = ROUNDS * RING // SUB
LAST_VEC = RING - 3
PHASES = [(layer, b) for layer in range(2) for b in range(TILES)]

WCOLS = 256
NW = 4
RING_BLOCKS = 8
LATE = NW + RING_BLOCKS
NARROW = LATE + 2



KEPT_BLOCKS = {(("pq", 0, 1), i): (("pq", 0, 0), i) for i in (2, 3)}
KEPT_BLOCKS.update({(("pq", 1, 1), i): (("pq", 1, 0), i) for i in range(4, 8)})
KEPT_BLOCKS.update({(("K", 1), i): (("K", 0), i) for i in range(4)})


FIRST_QUERIES = [0, 2, 3, 1]


def weight_blocks(a):
    w_in, w_kv = a["gla_w_in"][0], a["kv_w"]
    out = [("gain", ("mix", 0), a["norm_mix"][0:1, :])]

    def cols(key, w, first, n):
        for i in range(0, n, WCOLS):
            out.append(("w", (key, i // WCOLS), w[:, first + i:first + min(i + WCOLS, n)]))

    cols("glr", w_in, 3 * D, GRANK)
    cols("q", w_in, 0, HALF)
    cols("k", w_in, HALF, HALF)
    cols("v", w_in, D, D)
    out.append(("go", None, a["gla_norm_o"][0:1, :]))
    cols("r", w_in, 2 * D, D)
    out.append(("keys", (("keys", 0), 0), a["peer_sub_keys"][0]))
    out.append(("gain", ("ffn", 0), a["norm_ffn"][0:1, :]))
    peer_q = a["peer_w_q"]

    def route(layer, b, j):
        for i in (2 * j, 2 * j + 1):
            if (("pq", layer, b), i) not in KEPT_BLOCKS:
                out.append(("w", (("pq", layer, b), i), peer_q[layer][:, i * WCOLS:(i + 1) * WCOLS]))

    cols(("wo", 0, 0), a["gla_w_o"][0], 0, D)
    for j in range(4):
        route(0, 0, j)
    cols(("wo", 0, 1), a["gla_w_o"][0], 0, D)
    route(0, 1, 0)
    for b in range(TILES):
        before = (0, 1) if b == 0 else (1, 0)
        if b == 0:
            out.append(("gains", None, [a["kv_norm"].rearrange("(o d) -> o d", o=1), a["norm_mix"][1:2, :],
                                        a["norm_ffn"][1:2, :], a["norm_final"].rearrange("(o d) -> o d", o=1)]))
        route(*before, 1)
        if b == 0:
            cols(("K", b), w_kv, 0, D)
        route(*before, 2)
        cols(("V", b), w_kv, D, D)
        cols(("fl", b), w_kv, 2 * D, FH)
        route(*before, 3)
        cols(("Q", b), a["fox_w_q"][0], 0, D)
        cols(("wo", 1, b), a["fox_w_o"][0], 0, D)
        if b == 0:
            out.append(("keys", (("keys", 1), 0), a["peer_sub_keys"][1]))
        route(1, b, 0)
    for j in range(1, 4):
        route(1, 1, j)
    return out


def weight_releases(stream):
    out = [key for kind, key, _ in stream if kind in ("w", "keys") and key[0] not in ("k", "v", "r") and
           key not in KEPT_BLOCKS.values()]
    for before, held in (((("keys", 0), 0), [("v", 0), ("v", 1)]), ((("pq", 0, 0), 0), [("v", 2), ("v", 3)]),
                         ((("pq", 0, 0), 4), [("r", i) for i in range(4)]),
                         ((("pq", 0, 1), 4), [(("pq", 0, 0), 2), (("pq", 0, 0), 3)]),
                         ((("V", 1), 0), [(("K", 0), i) for i in range(4)]),
                         ((("wo", 0, 1), 0), [("k", 0), ("k", 1)])):
        at = out.index(before)
        out[at:at] = held
    return out + [(("pq", 1, 0), i) for i in range(4, 8)]


OWN_PLACES = {("glr", 0): 3, ("q", 0): 0, ("q", 1): 1, ("k", 0): 2, ("k", 1): 3, (("keys", 0), 0): 0,
              (("wo", 0, 0), 0): 1, (("wo", 0, 0), 1): NW, (("wo", 0, 0), 2): NW + 1, (("wo", 0, 0), 3): 0,
              (("pq", 0, 0), 0): 1, (("pq", 0, 0), 1): 0, (("pq", 0, 0), 2): 1, (("pq", 0, 0), 3): 0,
              (("K", 0), 0): LATE, (("K", 0), 1): LATE + 1, (("K", 0), 2): 0, (("K", 0), 3): 1,
              (("pq", 1, 0), 4): LATE, (("pq", 1, 0), 5): LATE + 1, (("pq", 1, 0), 6): 0, (("pq", 1, 0), 7): 1,
              (("fl", 0), 0): NARROW, (("fl", 1), 0): NARROW}
OWN_PLACES.update({("v", i): NW + i for i in range(4)})
OWN_PLACES.update({("r", i): NW + 4 + i for i in range(4)})
OWN_PLACES.update({(("pq", 0, 0), 4 + i): NW + p for i, p in enumerate((2, 3, 6, 7))})


def weight_places(stream):
    out, turn = {}, 0
    gla_done = (("wo", 0, 1), 0)
    last = {LATE: (0, gla_done), LATE + 1: (0, gla_done)}
    for kind, key, _ in stream:
        if kind not in ("w", "keys"):
            continue
        if key in OWN_PLACES:
            place = OWN_PLACES[key]
        else:
            place, turn = 2 + turn % 2, turn + 1
        n, before = last.get(place, (0, None))
        out[key] = (place, n + 1, before)
        last[place] = (n + 1, key)
    for key, kept in KEPT_BLOCKS.items():
        out[key] = out[kept]
    return out


def pair_uses():
    out = []

    def turn(*keys, among=(0, 1, 2)):
        for key in keys:
            last = next((p for _, p in reversed(out) if p in among), among[-1])
            out.append((key, among[(among.index(last) + 1) % len(among)]))

    turn(("T", "mix0", 0), ("T", "mix0", 1), "glr", "z", "q", ("k", 0))
    for i in range(LEVELS):
        if i % 4 == 0:
            out.append((("v" if i == 0 else "r", 0), 0))
        turn(("level", 0, i), among=(1, 2))
    turn(("o", 0))
    out.append((("v", 1), 3))
    turn(("keys", 0, 0), ("keys", 0, 1), ("T", "o0", 0), ("wo", 0, 0), ("T", "ffn0", 0), ("route", 0, 0, 0))
    out.append((("r", 1), 3))
    turn(*[("route", 0, 0, j) for j in FIRST_QUERIES[1:]], ("k", 1))
    turn("kdec", "state", *[("level", 1, i) for i in range(LEVELS)])
    turn(("o", 1), ("T", "o0", 1), ("wo", 0, 1), ("T", "ffn0", 1), ("route", 0, 1, 0))
    for b in range(TILES):
        before = (0, 1) if b == 0 else (1, 0)
        turn(("route", *before, 1), ("gain", "kv", b), ("T", "kv", b), ("K", b), ("route", *before, 2), ("V", b),
             ("fl", b), ("gain", "mix1", b), ("route", *before, 3), ("T", "mix1", b), ("Q", b),
             *[("att", b, c) for c in range(FH // 2)])
        turn(("T", "o1", b), ("wo", 1, b), ("gain", "ffn1", b))
        if b == 0:
            turn(("keys", 1, 0), ("keys", 1, 1))
        turn(("T", "ffn1", b), ("route", 1, b, 0))
    turn(*[("route", 1, 1, j) for j in range(1, 4)], ("gain", "final", 0), ("gain", "final", 1))
    return out


T_USES = [("mix0", 0), ("mix0", 1), ("o0", 0), ("ffn0", 0), ("o0", 1), ("ffn0", 1)]
for _b in range(TILES):
    T_USES += [("kv", _b), ("mix1", _b), ("o1", _b), ("ffn1", _b)]
NORMS = [("mix0", 0), ("mix0", 1), ("ffn0", 0), ("ffn0", 1), ("kv", 0), ("ffn1", 0), ("kv", 1), ("ffn1", 1),
         ("final", 0), ("final", 1)]
GAIN_OF = {"mix0": 0, "ffn0": 1}
GAIN_ROW = {"kv": 0, "mix1": 1, "ffn1": 2, "final": 3}
H_VERSIONS = [("mixed", 0, 0), ("mixed", 0, 1), ("done", 0, 0), ("mixed", 1, 0), ("done", 0, 1), ("mixed", 1, 1),
              ("done", 1, 0), ("done", 1, 1)]
H_OF_NORM = {("ffn0", 0): ("mixed", 0, 0), ("ffn0", 1): ("mixed", 0, 1), ("kv", 0): ("done", 0, 0),
             ("ffn1", 0): ("mixed", 1, 0), ("kv", 1): ("done", 0, 1), ("ffn1", 1): ("mixed", 1, 1),
             ("final", 0): ("done", 1, 0), ("final", 1): ("done", 1, 1)}


def yoco_kernel(nc, a, out):
    STREAM = weight_blocks(a)
    RELEASE_OF = {key: i for i, key in enumerate(weight_releases(STREAM))}
    RELEASE_OF.update({key: RELEASE_OF[kept] for key, kept in KEPT_BLOCKS.items()})
    PLACE_OF = weight_places(STREAM)
    PAIR_USE, PAIR_COUNT = {}, [0] * 4
    for key, p in pair_uses():
        PAIR_USE[key] = (p, PAIR_COUNT[p])
        PAIR_COUNT[p] += 1

    with ExitStack() as ctx:
        def sb(name, shape, dt=F32):
            return ctx.enter_context(nc.sbuf_tensor(name, shape, dt))

        def sem(name):
            return ctx.enter_context(nc.semaphore(name))

        h = sb("h", [P, TILES, D])
        xn = sb("xn", [P, TILES, D])
        rows = sb("rows", [P, D])
        xT = sb("xT", [P, 2, KC, P])
        gain = sb("gain", [P, D])
        wbuf = sb("wbuf", [P, NW, KC, WCOLS])
        narrow = sb("narrow", [P, KC, GRANK])
        u_ring = sb("u_ring", [P, RING, D])
        v_ring = sb("v_ring", [P, RING, D])
        square = sb("square", [P, D], BF16)
        ident = sb("ident", [P, P])
        ident16 = sb("ident16", [P, P], BF16)
        zeros16 = sb("zeros16", [P, HALF], BF16)
        causal16 = sb("causal16", [P, P], BF16)
        ones = sb("ones", [P, P])
        eps = sb("eps", [P, 1])
        sumsq = sb("sumsq", [P, len(NORMS)])
        rms = sb("rms", [P, len(NORMS)])
        rstd = sb("rstd", [P, len(NORMS)])
        qkT = sb("qkT", [P, TILES, 2, GH, P])
        vtok = sb("vtok", [P, TILES, D])
        gate_o = sb("gate_o", [P, TILES, D])
        b_g = sb("b_g", [P, GH])
        late = [sb(f"late{i}", [P, KC, WCOLS]) for i in range(2)]
        decay = late[0][:, 0:4, :].rearrange("p c (a t) -> p (c a) t", t=P).rearrange(
            "p (b h) t -> p b h t", b=TILES)
        state = late[0][:, 4:8, :]
        attnT = late[1][:, 0:2, :].rearrange("p c (a t) -> p (c a) t", t=P)
        kdec = attnT
        faded_end = late[1][:, 2:4, :].rearrange("p c n -> p (c n)")
        scratch = sb("scratch", [P, 5 * HALF])
        masks = sb("masks", [P, LEVELS, P], U8)
        head_ss = sb("head_ss", [P, TILES, GH])
        head_rms = sb("head_rms", [P, TILES, GH])
        head_rstd = sb("head_rstd", [P, TILES, GH])
        b_f = sb("b_f", [FH, 1])
        forget = sb("forget", [FH, 4, P])
        cumT = sb("cumT", [FH, TILES * P])
        neg_cumT = sb("neg_cumT", [FH, TILES * P])
        neg_max = sb("neg_max", [P, TILES, FH])
        prob_sum = sb("prob_sum", [P, TILES, FH])
        prob_inv = sb("prob_inv", [P, TILES, FH])
        keysT = sb("keysT", [P, 2 * RH, RK])
        glrT = keysT[0:GRANK, 0:TILES, :].rearrange("p g n -> p (g n)")
        w_g2 = keysT[0:GRANK, TILES:TILES + GH, :].rearrange("p g n -> p (g n)")
        queryT = sb("queryT", [P, 4, P])
        top = sb("top", [P, 4, RTOP])
        top_at = sb("top_at", [P, 4, RTOP], U32)
        top_id = sb("top_id", [P, 4, RTOP])
        best = sb("best", [P, TILES, RH, RTOP])
        best_at = sb("best_at", [P, 2, RTOP], U32)
        digit = sb("digit", [P, 2, 2, RTOP], U32)
        picked = sb("picked", [P, 2, 2, RTOP])
        ids_f = sb("ids_f", [P, 2, RTOP])
        iota16 = sb("iota16", [P, RTOP])
        ids = sb("ids", [P, TILES, SLOTS], U32)
        gates = sb("gates", [P, TILES, SLOTS])
        gate_e = sb("gate_e", [P, SLOTS])
        gate_sum = sb("gate_sum", [P, RH])
        gate_inv = sb("gate_inv", [P, RH])
        u_ids = sb("u_ids", [P, RING], U32)
        v_ids = sb("v_ids", [P, RING], U32)
        dots = sb("dots", [P, RING])
        gelus = sb("gelus", [P, RING])
        weights_s = sb("weights_s", [P, RING])
        diag = sb("diag", [P, len(PE_SLOTS), P])

        q2T = [gate_o[:, g, :].rearrange("p (c t) -> p c t", c=KC) for g in range(2)]
        v2 = vtok

        places = [wbuf[:, i, :, :] for i in range(NW)] + [
            ring[:, 2 * i:2 * i + 2, :].rearrange("p s d -> p (s d)").rearrange("p (c n) -> p c n", c=KC)
            for ring in (u_ring, v_ring) for i in range(RING_BLOCKS // 2)]
        xT_kept = xn[:, 1, :].rearrange("p (c t) -> p c t", c=KC)
        places += [late[0][:, :, :], late[1][:, :, :], narrow[:, :, :]]
        gain_o = gate_o[:, 1, :]

        acc = ctx.enter_context(nc.psum_tensor("acc", [P, 2, HALF], F32))
        pairs = [ctx.enter_context(nc.psum_tensor(f"pair{i}", [P, 2, HALF], F32)) for i in range(3)] + [acc]

        def flat(t):
            return t[:, :, :].rearrange("p a b -> p (a b)")

        x_loaded = [sem(f"x_loaded{b}") for b in range(TILES)]
        small_loaded = sem("small_loaded")
        gain_loaded, gain_used = sem("gain_loaded"), sem("gain_used")
        gain_o_loaded = sem("gain_o_loaded")
        kept_ready = sem("kept_ready")
        w_loaded = [sem(f"w_loaded{i}") for i in range(NARROW + 1)]
        w_used = sem("w_used")
        consts = sem("consts")
        masks_f_ready, masks_ready = sem("masks_f_ready"), sem("masks_ready")
        pair_full = [sem(f"pair_full{i}") for i in range(4)]
        pair_free = [sem(f"pair_free{i}") for i in range(4)]
        dve_step, act_step = sem("dve_step"), sem("act_step")
        h_ready = sem("h_ready")
        rms_ready = sem("rms_ready")
        q_zeroed = sem("q_zeroed")
        rows_ready = sem("rows_ready")
        z_ready, z_exp_ready, z_log_ready = sem("z_ready"), sem("z_exp_ready"), sem("z_log_ready")
        z_abs_ready = sem("z_abs_ready")
        diff_ready, fade_ready, faded_ready = sem("diff_ready"), sem("fade_ready"), sem("faded_ready")
        attn_ready = sem("attn_ready")
        head_ss_ready = sem("head_ss_ready")
        silu_ready = sem("silu_ready")
        f_abs_ready, f_log_ready, cum_ready = sem("f_abs_ready"), sem("f_log_ready"), sem("cum_ready")
        max_ready, probs_ready, probsT_full, probsT_ready = (sem("max_ready"), sem("probs_ready"),
                                                              sem("probsT_full"), sem("probsT_ready"))
        pv_full = sem("pv_full")
        queryT_full, queryT_ready = sem("queryT_full"), sem("queryT_ready")
        gate_x_ready, gate_e_ready, routed = sem("gate_x_ready"), sem("gate_e_ready"), sem("routed")
        ids_laid = sem("ids_laid")
        issued = sem("issued")
        u_loaded = [sem(f"u_loaded{j}") for j in range(RING)]
        v_loaded = [sem(f"v_loaded{j}") for j in range(RING)]
        u_free, v_free, vec_free = sem("u_free"), sem("v_free"), sem("vec_free")
        dots_free = sem("dots_free")
        gelu_ready = sem("gelu_ready")
        diag_ready = sem("diag_ready")
        acc_full, acc_free = sem("acc_full"), sem("acc_free")
        out_ready, out_stored = sem("out_ready"), sem("out_stored")

        def pair_of(key):
            return pairs[PAIR_USE[key][0]]

        def full(key):
            p, n = PAIR_USE[key]
            assert not of_weights(key)
            return pair_full[p], sum(q == p and m <= n and not of_weights(k) for k, (q, m) in PAIR_USE.items())

        def freed(key):
            p, n = PAIR_USE[key]
            return pair_free[p], n + 1

        def frees(key, ins):
            ins.then_inc(pair_free[PAIR_USE[key][0]], 1)

        def of_weights(key):
            name = key if isinstance(key, str) else key[0]
            if key in (("k", 0), ("v", 0), ("r", 0), ("K", 0)):
                return False
            return name in ("glr", "q", "k", "v", "r", "wo", "K", "V", "fl", "Q")

        def nth_query(layer, b, j):
            return (layer * TILES + b) * 4 + (FIRST_QUERIES.index(j) if layer == b == 0 else j)

        def multiplied(key):
            return w_used, RELEASE_OF[key] + 1

        def t_at(key):
            return T_USES.index(key)

        def version(key):
            return h_ready, H_VERSIONS.index(key) + 1

        def is_last(r, j):
            return type(r) is int and r == len(PHASES) * ROUNDS - 1 and j >= LAST_VEC

        def in_halves(eng, half, ph, first, last):
            at, turns = first, ph * ROUNDS
            if at % 2 and at < last:
                half(ph, turns + at // 2, 1)
                at += 1
            if last - at >= 4:
                with eng.Fori(turns + at // 2, turns + last // 2) as r:
                    half(ph, r, 0)
                    half(ph, r, 1)
                at = last // 2 * 2
            for i in range(at, last):
                half(ph, turns + i // 2, i % 2)

        block = ctx.enter_context(nc.Block())

        @block.sync
        def _(sp):
            for b in range(TILES):
                sp.dma_start(h[:, b, :], a["x"][0, b * P:(b + 1) * P, :]).then_inc(x_loaded[b], 16)
            n_gain = n_block = 0
            for kind, key, src in STREAM:
                if kind == "go":
                    sp.dma_start(gain_o, src.broadcast_to([P, D])).then_inc(gain_o_loaded, 16)
                elif kind == "gain":
                    if n_gain:
                        sp.wait_ge(gain_used, n_gain)
                    sp.dma_start(gain[:, :], src.broadcast_to([P, D])).then_inc(gain_loaded, 16)
                    n_gain += 1
                elif kind == "gains":
                    sp.wait_ge(gain_used, n_gain)
                    for i, row in enumerate(src):
                        sp.dma_start(gain[i:i + 1, :], row).then_inc(gain_loaded, 16)
                else:
                    place, _, before = PLACE_OF[key]
                    if before:
                        sp.wait_ge(*multiplied(before))
                    if kind == "keys":
                        dst = places[place].rearrange("p c n -> p (c n)").rearrange("p (g d) -> p g d", d=RK)
                        sp.dma_start(dst, src.rearrange("h c n d -> n (h c) d")).then_inc(w_loaded[place], 16)
                    else:
                        sp.dma_start(places[place][:, :, 0:src.shape[1]],
                                     src.rearrange("(c p) n -> p c n", p=P)).then_inc(w_loaded[place], 16)
                    n_block += 1
                    if n_block == 1:
                        sp.dma_start(w_g2[:, :], a["gla_w_g2"][0]).then_inc(small_loaded, 16)
                        with nc.allow_non_contiguous_dma(reason="640 numbers"):
                            sp.dma_start(b_g[:, :], a["gla_b_g"][0].rearrange("(h k) -> k h", k=GDK)
                                         ).then_inc(small_loaded, 16)
                            sp.dma_start(b_f[:, :], a["fox_b_f"].rearrange("(h o) -> h o", o=1)
                                         ).then_inc(small_loaded, 16)
            for b in range(TILES):
                sp.wait_ge(out_ready, b + 1)
                sp.dma_start(out[0, b * P:(b + 1) * P, :], xn[:, b, :]).then_inc(out_stored, 16)
            sp.wait_ge(out_stored, 16 * TILES)

        @block.gpsimd
        def _(pool):
            made = 0

            def chained(ins):
                nonlocal made
                made += 1
                ins.then_inc(consts, 1)
                pool.wait_ge(consts, made)

            nc.gpsimd.memset(zeros16[:, :], 0.0)
            nc.gpsimd.memset(ones[:, :], 1.0)
            nc.gpsimd.memset(eps[:, :], EPS)
            nc.gpsimd.memset(causal16[:, :], 0.0)
            nc.gpsimd.iota(iota16[:, :], pattern=[[1, RTOP]], base=0, channel_multiplier=0,
                           allow_small_or_imprecise_dtypes=True)
            nc.gpsimd.memset(ident16[:, :], 0.0)
            chained(nc.gpsimd.memset(ident[:, :], 0.0))
            nc.gpsimd.affine_select(out=ident16[:, :], in_=ident16[:, :], compare_op=ALU.not_equal, fill=1.0,
                                    base=0, pattern=[[-1, P]], channel_multiplier=1)
            chained(nc.gpsimd.affine_select(out=ident[:, :], in_=ident[:, :], compare_op=ALU.not_equal, fill=1.0,
                                            base=0, pattern=[[-1, P]], channel_multiplier=1))
            nc.gpsimd.affine_select(out=causal16[:, :], in_=causal16[:, :], compare_op=ALU.is_ge, fill=-1.0e38,
                                    base=0, pattern=[[-1, P]], channel_multiplier=1)
            mf = scratch[:, 0:LEVELS * P].rearrange("p (l t) -> p l t", l=LEVELS)
            chained(nc.gpsimd.memset(mf, 1.0))
            for i in range(LEVELS - 1):
                m = P >> (i + 1)
                v = mf[:, i, :].rearrange("p (n c) -> p n c", c=2 * m)
                n = P // (2 * m)
                chained(nc.gpsimd.affine_select(out=v, in_=v, compare_op=ALU.is_ge, fill=0.0, base=0,
                                                pattern=[[-2 * m, n], [0, 2 * m]], channel_multiplier=1))
                chained(nc.gpsimd.affine_select(out=v, in_=v, compare_op=ALU.is_ge, fill=0.0, base=m - 1,
                                                pattern=[[2 * m, n], [0, 2 * m]], channel_multiplier=-1))
                chained(nc.gpsimd.affine_select(out=v, in_=v, compare_op=ALU.is_ge, fill=0.0, base=-m,
                                                pattern=[[0, n], [1, 2 * m]], channel_multiplier=0))
            nc.gpsimd.affine_select(out=mf[:, LEVELS - 1, :], in_=mf[:, LEVELS - 1, :], compare_op=ALU.is_equal,
                                    fill=0.0, base=0, pattern=[[-1, P]], channel_multiplier=1
                                    ).then_inc(masks_f_ready, 1)
            u_rows = a["peer_u"].rearrange("l n d -> (l n) d")
            v_rows = a["peer_v"].rearrange("l n d -> (l n) d")

            def turn(ph, b, r, waits=None):
                for j0 in range(0, RING, ISSUE):
                    numbers = ids[:, b, bass.ds(r * RING + (j0 - ph * SLOTS), ISSUE)]
                    slots = range(j0, j0 + ISSUE)
                    n_laid = 2 * (j0 // ISSUE)
                    pool.wait_ge(u_free, r * RING + (j0 + ISSUE))
                    pool.sem_inc(issued, 1)
                    nc.gpsimd.tensor_copy(u_ids[:, j0:j0 + ISSUE], numbers).then_inc(ids_laid, 1)
                    if waits:
                        pool.wait_ge(*waits[n_laid])
                    pool.wait_ge(ids_laid, r * (2 * RING // ISSUE) + (n_laid + 1))
                    pool.sem_inc(issued, 1)
                    for j in slots:
                        pool.indirect_dma_start(
                            u_ring[:, j, :], None, u_rows, bass.IndirectOffsetOnAxis(ap=u_ids[:, j:j + 1], axis=0)
                        ).then_inc(u_loaded[j], 16)
                    on_pe = sum(j < j0 + ISSUE for j in PE_SLOTS)
                    on_dve = sum(j < j0 + ISSUE for j in VEC_SLOTS)
                    if any(j in PE_SLOTS for j in slots):
                        pool.wait_ge(v_free, r * len(PE_SLOTS) + on_pe)
                        pool.sem_inc(issued, 1)
                    if any(j in VEC_SLOTS for j in slots):
                        pool.wait_ge(vec_free, r * VEC + on_dve)
                        pool.sem_inc(issued, 1)
                    nc.gpsimd.tensor_copy(v_ids[:, j0:j0 + ISSUE], numbers).then_inc(ids_laid, 1)
                    if waits:
                        pool.wait_ge(*waits[n_laid + 1])
                    pool.wait_ge(ids_laid, r * (2 * RING // ISSUE) + (n_laid + 2))
                    pool.sem_inc(issued, 1)
                    for j in slots:
                        pool.indirect_dma_start(
                            v_ring[:, j, :], None, v_rows, bass.IndirectOffsetOnAxis(ap=v_ids[:, j:j + 1], axis=0)
                        ).then_inc(v_loaded[j], 16)

            for ph, (layer, b) in enumerate(PHASES):
                for quarter in range(4):
                    pool.wait_ge(routed, ph * 4 + quarter + 1)
                    first = ph * ROUNDS + quarter * QUARTER
                    if first == 0:
                        turn(0, 0, 0, [multiplied(key) for key in ((("wo", 0, 0), 2), ("r", 1),
                                                                   (("pq", 0, 0), 5), (("pq", 0, 0), 7))])
                    with pool.Fori(max(first, 1), first + QUARTER) as r:
                        turn(ph, b, r)

        @block.vector
        def _(dve):
            steps = 0

            def chained(ins):
                nonlocal steps
                steps += 1
                ins.then_inc(dve_step, 1)
                dve.wait_ge(dve_step, steps)

            def norm(key, dst, n):
                b = key[1]
                dve.wait_ge(rms_ready, n + 1)
                if key[0] != "mix1":
                    chained(nc.vector.reciprocal(rstd[:, n:n + 1], rms[:, n:n + 1]))
                spread = key[0] in GAIN_ROW
                if spread:
                    dve.wait_ge(*full(("gain",) + key))
                    g = flat(pair_of(("gain",) + key))
                else:
                    dve.wait_ge(gain_loaded, 16 * (GAIN_OF[key[0]] + 1))
                    g = gain[:, :]
                done, count = (out_ready, b + 1) if key[0] == "final" else (rows_ready, t_at(key) + 1)
                nc.vector.scalar_tensor_tensor(out=dst, in0=h[:, b, :], scalar=rstd[:, n:n + 1], in1=g,
                                               op0=ALU.mult, op1=ALU.mult).then_inc(done, 1)
                if spread:
                    dve.wait_ge(done, count)
                    dve.sem_inc(pair_free[PAIR_USE[("gain",) + key][0]], 1)
                elif b == TILES - 1:
                    dve.wait_ge(done, count)
                    dve.sem_inc(gain_used, 1)

            def level_refs(b, m):
                s = decay[:, b, :, :].rearrange("p h (n c) -> p (h n) c", c=2 * m)
                return s, s[:, :, m - 1:m].broadcast_to([P, GH * P // (2 * m), m])

            def level_diff(b, i):
                m = P >> (i + 1)
                s, ref = level_refs(b, m)
                d = scratch[:, (i % 2) * HALF:(i % 2 + 1) * HALF].rearrange("p (n c) -> p n c", c=2 * m)
                if i >= 2:
                    dve.wait_ge(faded_ready, b * (LEVELS - 1) + i - 1)
                nc.vector.tensor_tensor(d[:, :, 0:m], ref, s[:, :, 0:m], ALU.subtract)
                nc.vector.tensor_tensor(d[:, :, m:2 * m], s[:, :, m:2 * m], ref, ALU.subtract
                                        ).then_inc(diff_ready, 1)

            def level_apply(b, i):
                m = P >> (i + 1)
                e = scratch[:, (i % 2) * HALF:(i % 2 + 1) * HALF].rearrange("p (n c) -> p n c", c=2 * m)
                x = scratch[:, D + (i % 2) * HALF:D + (i % 2 + 1) * HALF].rearrange("p (n c) -> p n c", c=2 * m)
                kk = qkT[:, b, 1, :, :].rearrange("p h (n c) -> p (h n) c", c=2 * m)
                qq = qkT[:, b, 0, :, :].rearrange("p h (n c) -> p (h n) c", c=2 * m)
                dve.wait_ge(fade_ready, fades(b, i))
                if i >= 2:
                    dve.wait_ge(*full(("level", b, i - 2)))
                nc.vector.tensor_tensor(x[:, :, 0:m], kk[:, :, 0:m], e[:, :, 0:m], ALU.mult)
                nc.vector.tensor_tensor(x[:, :, m:2 * m], qq[:, :, m:2 * m], e[:, :, m:2 * m], ALU.mult
                                        ).then_inc(faded_ready, 1)

            def level_take(b, i):
                key = ("level", b, i)
                dve.wait_ge(*full(key))
                ins = nc.vector.copy_predicated(attnT[:, :, :],
                                                masks[:, i, :].unsqueeze(1).broadcast_to([P, GH, P]),
                                                pair_of(key)[:, 0, :].rearrange("p (h t) -> p h t", h=GH))
                frees(key, ins)
                dve.wait_ge(*freed(key))

            def fades(b, i):
                return b * (LEVELS - 1) + i + 1

            def level_begin(b):
                if b:
                    dve.wait_ge(*freed(("k", 1)))
                    dve.wait_ge(*full("state"))
                chained(nc.vector.memset(attnT[:, :, :], 0.0))
                level_diff(b, 0)

            def level_step(b, i):
                if i + 1 < LEVELS - 1:
                    level_diff(b, i + 1)
                if i < LEVELS - 1:
                    level_apply(b, i)
                if i:
                    level_take(b, i - 1)
                if i == LEVELS:
                    dve.sem_inc(attn_ready, 1)

            def gla_out(b):
                key = ("o", b)
                dve.wait_ge(head_ss_ready, b + 1)
                chained(nc.vector.reciprocal(head_rstd[:, b, :], head_rms[:, b, :]))
                dve.wait_ge(*full(("T", "mix0", 1) if b == 0 else ("T", "o0", 0)))
                o = flat(pair_of(key))
                for g in range(GH):
                    c = slice(g * GDV, (g + 1) * GDV)
                    ins = nc.vector.scalar_tensor_tensor(out=rows[:, c], in0=o[:, c], scalar=head_rstd[:, b, g:g + 1],
                                                         in1=gate_o[:, b, c], op0=ALU.mult, op1=ALU.mult)
                frees(key, ins)
                dve.wait_ge(*freed(key))
                dve.sem_inc(rows_ready, 1)

            def residual(layer, b):
                key = ("wo", layer, b)
                dve.wait_ge(*multiplied((key, 3)))
                frees(key, nc.vector.tensor_tensor(h[:, b, :], h[:, b, :], flat(pair_of(key)), ALU.add))
                dve.wait_ge(*freed(key))
                dve.sem_inc(h_ready, 1)

            def top16(src, n, groups, vals, at, work):
                for g in range(groups):
                    ins = nc.vector.max(vals[:, g, 0:8], src[:, g, :])
                chained(ins)
                for g in range(groups):
                    nc.vector.max_index(at[:, g, 0:8], vals[:, g, 0:8], src[:, g, :])
                    ins = nc.vector.match_replace(work[:, g, :], vals[:, g, 0:8], src[:, g, :], LOW)
                chained(ins)
                for g in range(groups):
                    ins = nc.vector.max(vals[:, g, 8:16], work[:, g, :])
                chained(ins)
                for g in range(groups):
                    ins = nc.vector.max_index(at[:, g, 8:16], vals[:, g, 8:16], work[:, g, :])
                return ins

            def choose_keys(layer, b, j):
                key = ("route", layer, b, j)
                dve.wait_ge(*full(key))
                s = pair_of(key)[:, 1, :].rearrange("p (g n) -> p g n", g=4)
                work = scratch[:, 0:HALF].rearrange("p (g n) -> p g n", g=4)
                ins = top16(s, RK, 4, top, top_at, work)
                frees(key, ins)
                dve.wait_ge(*freed(key))
                chained(nc.vector.tensor_copy(top_id[:, :, :], top_at[:, :, :]))

            def choose_pairs(layer, b, j):
                cand = scratch[:, HALF:2 * HALF].rearrange("p (g i j) -> p g i j", g=2, i=RTOP)
                tv = top[:, :, :].rearrange("p (g c) k -> p g c k", c=2)
                chained(nc.vector.tensor_tensor(cand, tv[:, :, 0, :].unsqueeze(3).broadcast_to([P, 2, RTOP, RTOP]),
                                                tv[:, :, 1, :].unsqueeze(2).broadcast_to([P, 2, RTOP, RTOP]),
                                                ALU.add))
                cv = scratch[:, HALF:2 * HALF].rearrange("p (g n) -> p g n", g=2)
                chained(top16(cv, RTOP * RTOP, 2, best[:, b, 2 * j:2 * j + 2, :], best_at,
                              scratch[:, 2 * HALF:3 * HALF].rearrange("p (g n) -> p g n", g=2)))
                e = gate_e[:, j * 2 * RTOP:(j + 1) * 2 * RTOP].rearrange("p (h k) -> p h k", h=2)
                bb = best[:, b, 2 * j:2 * j + 2, :]
                nc.vector.tensor_tensor(e, bb, bb[:, :, 0:1].broadcast_to([P, 2, RTOP]), ALU.subtract
                                        ).then_inc(gate_x_ready, 1)

            def number(layer, b, j):
                nc.vector.tensor_scalar(digit[:, :, 0, :], best_at[:, :, :], 4, None, ALU.logical_shift_right)
                chained(nc.vector.tensor_scalar(digit[:, :, 1, :], best_at[:, :, :], RTOP - 1, None, ALU.bitwise_and))
                hot = scratch[:, 3 * HALF:5 * HALF].rearrange("p (g s k) -> p g s k", g=4, k=RTOP)
                hot_s = hot.rearrange("p g s k -> p (g s) k")
                chained(nc.vector.tensor_tensor(
                    hot_s, iota16[:, :].unsqueeze(1).broadcast_to([P, 4 * RTOP, RTOP]),
                    digit[:, :, :, :].rearrange("p g c s -> p (g c s)").unsqueeze(2).broadcast_to([P, 4 * RTOP, RTOP]),
                    ALU.is_equal))
                chained(nc.vector.tensor_tensor(
                    hot, hot, top_id[:, :, :].unsqueeze(2).broadcast_to([P, 4, RTOP, RTOP]), ALU.mult))
                chained(nc.vector.tensor_reduce(picked[:, :, :, :].rearrange("p g c s -> p (g c s)"), hot_s,
                                                AX_X, ALU.add))
                own = slice(j * 2 * RTOP, (j + 1) * 2 * RTOP)
                chained(nc.vector.scalar_tensor_tensor(out=ids_f[:, :, :], in0=picked[:, :, 0, :], scalar=float(RK),
                                                       in1=picked[:, :, 1, :], op0=ALU.mult, op1=ALU.add))
                nc.vector.tensor_scalar(ids[:, b, own].rearrange("p (g s) -> p g s", g=2), ids_f[:, :, :],
                                        float(layer * EXPERTS), None, ALU.add)
                n = (layer * TILES + b) * 4 + j
                e = gate_e[:, own].rearrange("p (h k) -> p h k", h=2)
                dve.wait_ge(gate_e_ready, n + 1)
                chained(nc.vector.tensor_reduce(gate_sum[:, 2 * j:2 * j + 2], e, AX_X, ALU.add))
                chained(nc.vector.reciprocal(gate_inv[:, 2 * j:2 * j + 2], gate_sum[:, 2 * j:2 * j + 2]))
                nc.vector.tensor_tensor(gates[:, b, own].rearrange("p (h k) -> p h k", h=2), e,
                                        gate_inv[:, 2 * j:2 * j + 2].unsqueeze(2).broadcast_to([P, 2, RTOP]), ALU.mult
                                        ).then_inc(routed, 1)
                dve.wait_ge(routed, n + 1)

            def forget_gate(b):
                key = ("fl", b)
                z = pair_of(key)[0:FH, 0, 0:P]
                dve.wait_ge(*multiplied((key, 0)))
                dve.wait_ge(f_abs_ready, b + 1)
                ins = nc.vector.tensor_scalar(forget[:, 1, :], z, b_f[:, 0:1], 0.0, ALU.add, ALU.min)
                frees(key, ins)
                dve.wait_ge(*freed(key))
                dve.wait_ge(f_log_ready, b + 1)
                chained(nc.vector.tensor_tensor(forget[:, 3, :], forget[:, 1, :], forget[:, 2, :], ALU.subtract))
                t = slice(b * P, (b + 1) * P)
                chained(nc.vector.tensor_tensor_scan(cumT[:, t], ones[0:FH, :], forget[:, 3, :],
                                                     cumT[:, b * P - 1:b * P] if b else 0.0, ALU.mult, ALU.add))
                nc.vector.tensor_scalar(neg_cumT[:, t], cumT[:, t], -1.0, None, ALU.mult).then_inc(cum_ready, 1)

            def att_max(b, c):
                key = ("att", b, c)
                dve.wait_ge(*full(key))
                n = (b + 1) * P
                s = pair_of(key)[:, 0, 0:2 * n].rearrange("p (g s) -> p g s", g=2)
                nc.vector.tensor_reduce(neg_max[:, b, 2 * c:2 * c + 2], s, AX_X, ALU.max, negate=True
                                        ).then_inc(max_ready, 1)

            def att_norm(b, c):
                key = ("att", b, c)
                n = b * (FH // 2) + c
                dve.wait_ge(probs_ready, n + 1)
                chained(nc.vector.reciprocal(prob_inv[:, b, 2 * c:2 * c + 2], prob_sum[:, b, 2 * c:2 * c + 2]))
                dve.wait_ge(pv_full, n + 1)
                if c == 0:
                    dve.wait_ge(*full(("T", "mix1", b)))
                ins = nc.vector.tensor_tensor(
                    rows[:, c * P:(c + 1) * P].rearrange("p (g d) -> p g d", g=2),
                    pair_of(key)[:, 0, 0:P].rearrange("p (g d) -> p g d", g=2),
                    prob_inv[:, b, 2 * c:2 * c + 2].unsqueeze(2).broadcast_to([P, 2, FHD]), ALU.mult)
                frees(key, ins)
                if c == FH // 2 - 1:
                    dve.wait_ge(*freed(key))
                    dve.sem_inc(rows_ready, 1)

            def attention(b, first, last):
                for i in range(first, last):
                    if i < FH // 2:
                        att_max(b, i)
                    if i >= 2:
                        att_norm(b, i - 2)

            def half(ph, r, q):
                layer, b = PHASES[ph]
                dve.wait_ge(dots_free, r * (RING // SUB) + (q + 1))
                for j in range(q * SUB, (q + 1) * SUB):
                    dve.wait_ge(u_loaded[j], r * 16 + 16)
                    nc.vector.tensor_tensor_reduce(
                        out=u_ring[:, j, :], in0=u_ring[:, j, :], in1=xn[:, b, :], scale=1.0, scalar=0.0,
                        op0=ALU.mult, op1=ALU.add, accum_out=dots[:, j:j + 1]).then_inc(u_free, 1)
                    if j != SUB:
                        continue
                    dve.wait_ge(gelu_ready, r * (RING // SUB) + 1)
                    for k, jv in enumerate(VEC_SLOTS):
                        dve.wait_ge(v_loaded[jv], r * 16 + 16)
                        dve.wait_ge(vec_free, r * VEC + (VEC + k))
                        nc.vector.scalar_tensor_tensor(
                            out=h[:, b, :], in0=v_ring[:, jv, :], scalar=weights_s[:, jv:jv + 1],
                            in1=h[:, b, :], op0=ALU.mult, op1=ALU.add).then_inc(vec_free, 1)

            def experts(ph, first, last):
                in_halves(dve, half, ph, first, last)

            def experts_end(ph):
                layer, b = PHASES[ph]
                dve.wait_ge(vec_free, (ph + 1) * ROUNDS * VEC + VEC)
                dve.wait_ge(acc_full, ph + 1)
                nc.vector.tensor_tensor(h[:, b, :], h[:, b, :], flat(acc), ALU.add).then_inc(acc_free, 1)
                dve.wait_ge(acc_free, ph + 1)
                dve.sem_inc(h_ready, 1)

            dve.sem_inc(u_free, RING)
            dve.sem_inc(vec_free, VEC)
            dve.wait_ge(x_loaded[0], 16)
            norm(("mix0", 0), rows[:, :], 0)
            dve.wait_ge(*full(("T", "mix0", 0)))
            dve.wait_ge(x_loaded[1], 16)
            norm(("mix0", 1), rows[:, :], 1)
            dve.wait_ge(small_loaded, 48)
            dve.wait_ge(*full("z"))
            zp = flat(pair_of("z")).rearrange("p (h b t) -> p h b t", h=GH, b=TILES)
            dve.wait_ge(z_abs_ready, 1)
            late1 = late[1][:, :, :].rearrange("p c n -> p (c n)")
            zm = late1[:, 0:D].rearrange("p (b h t) -> p b h t", b=TILES, h=GH)
            for g in range(GH):
                ins = nc.vector.tensor_scalar(zm[:, :, g, :], zp[:, g, :, :], b_g[:, g:g + 1], 0.0, ALU.add, ALU.min)
            frees("z", ins)
            dve.wait_ge(*freed("z"))
            dve.wait_ge(z_log_ready, 1)
            dflat = decay[:, :, :, :].rearrange("p b h t -> p (b h t)")
            chained(nc.vector.tensor_tensor(dflat, late1[:, 0:D], scratch[:, D:2 * D], ALU.subtract))
            chained(nc.vector.tensor_scalar(dflat, dflat, 1.0 / GTAU, None, ALU.mult))
            for b in range(TILES):
                for g in range(GH):
                    t = late1[:, D + (b * GH + g) * P:D + (b * GH + g + 1) * P]
                    ins = nc.vector.tensor_tensor_scan(t, ones[:, :], decay[:, b, g, :], 0.0, ALU.mult, ALU.add)
            chained(ins)
            chained(nc.vector.tensor_copy(dflat, late1[:, D:2 * D]))
            kd = faded_end.rearrange("p (h t) -> p h t", h=GH)
            nc.vector.tensor_tensor(kd, decay[:, 0, :, P - 1:P].broadcast_to([P, GH, P]), decay[:, 0, :, :],
                                    ALU.subtract).then_inc(z_ready, 1)
            dve.wait_ge(masks_f_ready, 1)
            nc.vector.tensor_copy(masks[:, :, :], scratch[:, 0:LEVELS * P].rearrange("p (l t) -> p l t", l=LEVELS)
                                  ).then_inc(masks_ready, 1)
            dve.wait_ge(masks_ready, 1)
            level_begin(0)
            dve.wait_ge(z_exp_ready, 1)
            dve.wait_ge(*freed(("k", 0)))
            nc.vector.tensor_tensor(kd, kd, qkT[:, 0, 1, :, :], ALU.mult).then_inc(z_ready, 1)
            for i in range(LEVELS + 1):
                level_step(0, i)
            dve.wait_ge(silu_ready, 1)
            dve.wait_ge(gain_o_loaded, 16)
            chained(nc.vector.tensor_tensor(gate_o[:, 0, :], gate_o[:, 0, :], gain_o, ALU.mult))

            def first_fox(b):
                if b == 0:
                    nc.vector.memset(gate_o[FHD:P, 0, :], 0.0)
                    nc.vector.memset(gate_o[0:FHD, 1, :], 0.0).then_inc(q_zeroed, 1)
                norm(("kv", b), rows[:, :], NORMS.index(("kv", b)))

            def mixed(layer, b):
                residual(layer, b)
                norm((f"ffn{layer}", b), xn[:, b, :], NORMS.index((f"ffn{layer}", b)))

            gla_out(0)
            residual(0, 0)
            norm(("ffn0", 0), xn[:, 0, :], NORMS.index(("ffn0", 0)))
            choose_keys(0, 0, 0)
            choose_pairs(0, 0, 0)
            number(0, 0, 0)

            experts(0, 0, 1)
            dve.wait_ge(silu_ready, 2)
            nc.vector.tensor_tensor(gate_o[:, 1, :], rows[:, :], gain_o, ALU.mult)
            experts(0, 1, 2)
            choose_keys(0, 0, 1)
            experts(0, 2, 3)
            choose_pairs(0, 0, 1)
            experts(0, 3, 4)
            number(0, 0, 1)
            choose_keys(0, 0, 2)
            experts(0, 4, 5)
            choose_pairs(0, 0, 2)
            experts(0, 5, 6)
            number(0, 0, 2)
            choose_keys(0, 0, 3)
            experts(0, 6, 7)
            choose_pairs(0, 0, 3)
            experts(0, 7, 8)
            number(0, 0, 3)
            experts(0, 8, 9)
            level_begin(1)
            for i in range(LEVELS + 1):
                experts(0, 9 + i, 10 + i)
                level_step(1, i)
            dve.wait_ge(z_exp_ready, 2)
            qf = faded_end.rearrange("p (h t) -> p h t", h=GH)
            nc.vector.tensor_tensor(qf, qf, qkT[:, 1, 0, :, :], ALU.mult).then_inc(z_ready, 1)
            experts(0, 18, 20)
            gla_out(1)
            experts(0, 20, 23)
            residual(0, 1)
            experts(0, 23, 24)
            norm(("ffn0", 1), xn[:, 1, :], NORMS.index(("ffn0", 1)))
            experts(0, 24, 27)
            choose_keys(0, 1, 0)
            experts(0, 27, 28)
            choose_pairs(0, 1, 0)
            experts(0, 28, 29)
            number(0, 1, 0)
            experts(0, 29, HALVES)

            for ph, b in ((1, 0), (2, 1)):
                before = PHASES[ph]
                experts(ph, 0, 1)
                experts_end(ph - 1)
                experts(ph, 1, 3)
                first_fox(b)
                choose_keys(*before, 1)
                experts(ph, 3, 4)
                choose_pairs(*before, 1)
                experts(ph, 4, 5)
                number(*before, 1)
                experts(ph, 5, 9)
                choose_keys(*before, 2)
                experts(ph, 9, 10)
                norm(("mix1", b), rows[:, :], NORMS.index(("kv", b)))
                choose_pairs(*before, 2)
                experts(ph, 10, 11)
                forget_gate(b)
                number(*before, 2)
                experts(ph, 11, 12)
                choose_keys(*before, 3)
                experts(ph, 12, 13)
                choose_pairs(*before, 3)
                experts(ph, 13, 14)
                number(*before, 3)
                experts(ph, 14, 15)
                for i in range(5):
                    experts(ph, 15 + i, 16 + i)
                    attention(b, 2 * i, 2 * i + 2)
                experts(ph, 20, 23)
                residual(1, b)
                experts(ph, 23, 24)
                norm(("ffn1", b), xn[:, b, :], NORMS.index(("ffn1", b)))
                experts(ph, 24, 27)
                choose_keys(1, b, 0)
                experts(ph, 27, 28)
                choose_pairs(1, b, 0)
                experts(ph, 28, 29)
                number(1, b, 0)
                experts(ph, 29, HALVES)

            experts(3, 0, 1)
            experts_end(2)
            experts(3, 1, 3)
            for j in range(1, 4):
                choose_keys(1, 1, j)
                experts(3, 3 * j, 3 * j + 1)
                choose_pairs(1, 1, j)
                experts(3, 3 * j + 1, 3 * j + 2)
                number(1, 1, j)
                experts(3, 3 * j + 2, 3 * j + 3)
            norm(("final", 0), xn[:, 0, :], NORMS.index(("final", 0)))
            experts(3, 12, HALVES - 2)
            experts(3, HALVES - 2, HALVES)
            dve.wait_ge(gelu_ready, len(PHASES) * HALVES)
            dve.wait_ge(vec_free, (len(PHASES) * ROUNDS + 1) * VEC)
            for j in range(LAST_VEC, RING):
                dve.wait_ge(v_loaded[j], 16 * len(PHASES) * ROUNDS)
                chained(nc.vector.scalar_tensor_tensor(
                    out=h[:, 1, :], in0=v_ring[:, j, :], scalar=weights_s[:, j:j + 1], in1=h[:, 1, :],
                    op0=ALU.mult, op1=ALU.add))
            experts_end(3)
            norm(("final", 1), xn[:, 1, :], NORMS.index(("final", 1)))

        @block.scalar
        def _(act):
            steps = 0

            def chained(ins):
                nonlocal steps
                steps += 1
                ins.then_inc(act_step, 1)
                act.wait_ge(act_step, steps)

            def mean_square(n):
                key = NORMS[n]
                if key in H_OF_NORM:
                    act.wait_ge(*version(H_OF_NORM[key]))
                square_sum(n)
                root(n)

            def square_sum(n):
                chained(nc.scalar.activation(square[:, :], h[:, NORMS[n][1], :], ACT.Square,
                                             accum_out=sumsq[:, n:n + 1]))

            def root(n):
                nc.scalar.activation(rms[:, n:n + 1], sumsq[:, n:n + 1], ACT.Sqrt, bias=eps[:, 0:1], scale=1.0 / D
                                     ).then_inc(rms_ready, 1)

            def take_rows(key):
                use = ("T",) + key
                act.wait_ge(*full(use))
                frees(use, nc.scalar.activation(
                    xT[:, t_at(key) % 2, :, :].rearrange("p c t -> p (c t)"), flat(pair_of(use)), ACT.Copy))

            def fade(b, i):
                act.wait_ge(diff_ready, b * (LEVELS - 1) + i + 1)
                d = scratch[:, (i % 2) * HALF:(i % 2 + 1) * HALF]
                nc.scalar.activation(d, d, ACT.Exp).then_inc(fade_ready, 1)

            def heads_square(b):
                key = ("o", b)
                act.wait_ge(*full(key))
                o = flat(pair_of(key))
                for g in range(GH):
                    ins = nc.scalar.activation(square[:, g * GDV:(g + 1) * GDV], o[:, g * GDV:(g + 1) * GDV],
                                               ACT.Square, accum_out=head_ss[:, b, g:g + 1])
                chained(ins)
                nc.scalar.activation(head_rms[:, b, :], head_ss[:, b, :], ACT.Sqrt, bias=eps[:, 0:1],
                                     scale=1.0 / GDV).then_inc(head_ss_ready, 1)

            def take_query(layer, b, j):
                act.wait_ge(queryT_full, nth_query(layer, b, j) + 1)
                nc.scalar.activation(queryT[:, :, :].rearrange("p c t -> p (c t)"),
                                     pair_of(("route", layer, b, j))[:, 0, :], ACT.Copy).then_inc(queryT_ready, 1)

            def gate_exp(layer, b, j):
                act.wait_ge(gate_x_ready, (layer * TILES + b) * 4 + j + 1)
                e = gate_e[:, j * 2 * RTOP:(j + 1) * 2 * RTOP]
                nc.scalar.activation(e, e, ACT.Exp).then_inc(gate_e_ready, 1)

            def take_keys(layer):
                for i in range(2):
                    use = ("keys", layer, i)
                    act.wait_ge(*full(use))
                    frees(use, nc.scalar.activation(
                        keysT[:, i * KC:(i + 1) * KC, :].rearrange("p g n -> p (g n)"), flat(pair_of(use)), ACT.Copy))

            def probs_of(n):
                o = (n % 2) * D
                return scratch[:, o:o + 2 * TILES * P], scratch[:, o + HALF:o + D]

            def att_exp(b, c):
                n = b * (FH // 2) + c
                s_n = (b + 1) * P
                act.wait_ge(max_ready, n + 1)
                if c >= 2:
                    act.wait_ge(probsT_full, n - 1)
                for g in range(2):
                    hh = 2 * c + g
                    ins = nc.scalar.activation(probs_of(n)[0][:, g * s_n:(g + 1) * s_n],
                                               pair_of(("att", b, c))[:, 0, g * s_n:(g + 1) * s_n], ACT.Exp,
                                               bias=neg_max[:, b, hh:hh + 1], accum_out=prob_sum[:, b, hh:hh + 1])
                ins.then_inc(probs_ready, 1)

            def att_take(b, c):
                n = b * (FH // 2) + c
                act.wait_ge(probsT_full, n + 1)
                if c >= 2:
                    act.wait_ge(pv_full, n - 1)
                w = 2 * (b + 1) * P
                nc.scalar.activation(probs_of(n)[1][:, 0:w], pair_of(("att", b, c))[:, 1, 0:w], ACT.Copy
                                     ).then_inc(probsT_ready, 1)

            def half(ph, r, q):
                layer, b = PHASES[ph]
                s = slice(q * SUB, (q + 1) * SUB)
                act.wait_ge(u_free, r * RING + (RING + (q + 1) * SUB))
                nc.scalar.activation(gelus[:, s], dots[:, s], ACT.Gelu).then_inc(dots_free, 1)
                act.wait_ge(dots_free, r * (RING // SUB) + (RING // SUB + q + 1))
                if q == 0:
                    act.wait_ge(vec_free, r * VEC + VEC)
                for j in range(q * SUB, (q + 1) * SUB):
                    ins = nc.scalar.activation(
                        weights_s[:, j:j + 1], gelus[:, j:j + 1], ACT.Copy,
                        scale=gates[:, b, bass.ds(r * RING + (j - ph * SLOTS), 1)])
                ins.then_inc(gelu_ready, 1)
                act.wait_ge(gelu_ready, r * (RING // SUB) + (q + 1))
                for k, j in enumerate(PE_SLOTS):
                    if j // SUB == q and not is_last(r, j):
                        act.wait_ge(v_free, r * len(PE_SLOTS) + (k + 1))
                        nc.scalar.activation(diag[:, k, :], ident[:, :], ACT.Copy,
                                             scale=weights_s[:, j:j + 1]).then_inc(diag_ready, 1)

            def experts(ph, first, last):
                quarter = (last - 1) * 4 // HALVES
                act.wait_ge(routed, ph * 4 + quarter + 1)
                in_halves(act, half, ph, first, last)

            def take_k(b):
                frees(("k", b), nc.scalar.activation(
                    qkT[:, b, 1, :, :].rearrange("p h t -> p (h t)"), pair_of(("k", b))[:, 0, :], ACT.Copy))

            act.sem_inc(dots_free, RING // SUB)
            act.wait_ge(consts, 3)
            nc.scalar.activation(rms[:, 0:1], eps[:, :], ACT.Sqrt)
            for b in range(TILES):
                act.wait_ge(x_loaded[b], 16)
                square_sum(b)
            for b in range(TILES):
                root(b)
            for b in range(TILES):
                take_rows(("mix0", b))
            act.wait_ge(*multiplied(("glr", 0)))
            frees("glr", nc.scalar.activation(glrT[:, :], pair_of("glr")[0:GRANK, 0, 0:TILES * P], ACT.Copy))
            za = scratch[:, D:2 * D]
            act.wait_ge(*full("z"))
            act.wait_ge(small_loaded, 48)
            zp = flat(pair_of("z")).rearrange("p (h b t) -> p h b t", h=GH, b=TILES)
            za4 = za.rearrange("p (b h t) -> p b h t", b=TILES, h=GH)
            for g in range(GH):
                ins = nc.scalar.activation(za4[:, :, g, :], zp[:, g, :, :], ACT.Abs, bias=b_g[:, g:g + 1])
            ins.then_inc(z_abs_ready, 1)
            act.wait_ge(z_abs_ready, 1)
            chained(nc.scalar.activation(za, za, ACT.Exp, scale=-1.0))
            nc.scalar.activation(za, za, ACT.Ln, bias=1.0).then_inc(z_log_ready, 1)
            act.wait_ge(z_ready, 1)
            nc.scalar.activation(faded_end, faded_end, ACT.Exp).then_inc(z_exp_ready, 1)
            fade(0, 0)
            act.wait_ge(*multiplied(("q", 1)))
            frees("q", nc.scalar.activation(
                qkT[:, :, 0, :, :], flat(pair_of("q")).rearrange("p (h b t) -> p b h t", h=GH, b=TILES),
                ACT.Copy, scale=float(GDK) ** -0.5))
            act.wait_ge(*full(("k", 0)))
            take_k(0)
            for i in range(1, 4):
                fade(0, i)
            nc.scalar.activation(xT_kept, xT[:, 1, :, :], ACT.Copy).then_inc(kept_ready, 1)
            act.wait_ge(*full(("v", 0)))
            frees(("v", 0), nc.scalar.activation(vtok[:, 0, :], flat(pair_of(("v", 0))), ACT.Copy))
            for i in range(4, LEVELS - 1):
                fade(0, i)
            act.wait_ge(*full(("r", 0)))
            frees(("r", 0), nc.scalar.activation(gate_o[:, 0, :], flat(pair_of(("r", 0))), ACT.Silu))
            act.wait_ge(*freed(("r", 0)))
            act.sem_inc(silu_ready, 1)

            def attention(b, first, last):
                for i in range(first, last):
                    if i < FH // 2:
                        att_exp(b, i)
                    if 1 <= i <= FH // 2:
                        att_take(b, i - 1)

            heads_square(0)
            take_keys(0)
            take_rows(("o0", 0))
            mean_square(NORMS.index(("ffn0", 0)))
            take_rows(("ffn0", 0))
            take_query(0, 0, 0)
            act.wait_ge(*multiplied(("v", 3)))
            frees(("v", 1), nc.scalar.activation(vtok[:, 1, :], flat(pair_of(("v", 1))), ACT.Copy))
            gate_exp(0, 0, 0)
            act.wait_ge(*multiplied(("r", 3)))
            frees(("r", 1), nc.scalar.activation(rows[:, :], flat(pair_of(("r", 1))), ACT.Silu))
            act.wait_ge(*freed(("r", 1)))
            act.sem_inc(silu_ready, 1)
            for j in FIRST_QUERIES[1:]:
                take_query(0, 0, j)

            experts(0, 0, 3)
            gate_exp(0, 0, 1)
            experts(0, 3, 5)
            act.wait_ge(*multiplied(("k", 1)))
            take_k(1)
            gate_exp(0, 0, 2)
            experts(0, 5, 7)
            gate_exp(0, 0, 3)
            act.wait_ge(*full("kdec"))
            frees("kdec", nc.scalar.activation(kdec[:, :, :].rearrange("p h k -> p (h k)"),
                                               pair_of("kdec")[:, 0, :], ACT.Copy))
            experts(0, 7, 8)
            act.wait_ge(*full("state"))
            frees("state", nc.scalar.activation(state[:, :, :].rearrange("p h v -> p (h v)"),
                                                flat(pair_of("state")), ACT.Copy))
            for i in range(LEVELS - 1):
                experts(0, 8 + i, 9 + i)
                fade(1, i)
            experts(0, 15, 16)
            nc.scalar.activation(faded_end,
                                 decay[:, 1, :, :].rearrange("p h t -> p (h t)"), ACT.Exp).then_inc(z_exp_ready, 1)
            experts(0, 16, 19)
            heads_square(1)
            experts(0, 19, 21)
            take_rows(("o0", 1))
            experts(0, 21, 23)
            mean_square(NORMS.index(("ffn0", 1)))
            experts(0, 23, 25)
            take_rows(("ffn0", 1))
            experts(0, 25, 26)
            take_query(0, 1, 0)
            experts(0, 26, 28)
            gate_exp(0, 1, 0)
            experts(0, 28, HALVES)

            for ph, b in ((1, 0), (2, 1)):
                before = PHASES[ph]
                experts(ph, 0, 2)
                take_query(*before, 1)
                mean_square(NORMS.index(("kv", b)))
                experts(ph, 2, 4)
                gate_exp(*before, 1)
                take_rows(("kv", b))
                experts(ph, 4, 6)
                act.wait_ge(*(multiplied((("K", b), 3)) if b else full(("K", b))))
                frees(("K", b), nc.scalar.activation(
                    qkT[:, b, :, :, :].rearrange("p a c t -> p (a c) t"),
                    flat(pair_of(("K", b))).rearrange("p (c t) -> p c t", c=KC), ACT.Copy))
                experts(ph, 6, 8)
                take_query(*before, 2)
                experts(ph, 8, 10)
                act.wait_ge(*multiplied((("V", b), 3)))
                frees(("V", b), nc.scalar.activation(v2[:, b, :], flat(pair_of(("V", b))), ACT.Copy))
                act.wait_ge(*multiplied((("fl", b), 0)))
                if b:
                    act.wait_ge(cum_ready, b)
                nc.scalar.activation(forget[:, 0, :], pair_of(("fl", b))[0:FH, 0, 0:P], ACT.Abs,
                                     bias=b_f[:, 0:1]).then_inc(f_abs_ready, 1)
                act.wait_ge(f_abs_ready, b + 1)
                chained(nc.scalar.activation(forget[:, 2, :], forget[:, 0, :], ACT.Exp, scale=-1.0))
                nc.scalar.activation(forget[:, 2, :], forget[:, 2, :], ACT.Ln, bias=1.0).then_inc(f_log_ready, 1)
                gate_exp(*before, 2)
                experts(ph, 10, 11)
                take_query(*before, 3)
                experts(ph, 11, 12)
                take_rows(("mix1", b))
                experts(ph, 12, 13)
                gate_exp(*before, 3)
                experts(ph, 13, 14)
                act.wait_ge(*multiplied((("Q", b), 3)))
                act.wait_ge(q_zeroed, 1)
                src = flat(pair_of(("Q", b))).rearrange("p (c t) -> p c t", c=KC)
                for g in range(2):
                    pp = slice(g * FHD, (g + 1) * FHD)
                    ins = nc.scalar.activation(q2T[g][pp, :, :], src[pp, :, :], ACT.Copy,
                                               scale=float(FHD) ** -0.5)
                frees(("Q", b), ins)
                experts(ph, 14, 15)
                for i in range(5):
                    experts(ph, 15 + i, 16 + i)
                    attention(b, 2 * i, 2 * i + 2)
                experts(ph, 20, 21)
                take_rows(("o1", b))
                experts(ph, 21, 23)
                mean_square(NORMS.index(("ffn1", b)))
                experts(ph, 23, 24)
                if b == 0:
                    take_keys(1)
                experts(ph, 24, 25)
                take_rows(("ffn1", b))
                experts(ph, 25, 26)
                take_query(1, b, 0)
                experts(ph, 26, 28)
                gate_exp(1, b, 0)
                experts(ph, 28, HALVES)

            experts(3, 0, 2)
            for j in range(1, 4):
                take_query(1, 1, j)
                experts(3, 3 * j - 1, 3 * j + 1)
                gate_exp(1, 1, j)
                experts(3, 3 * j + 1, 3 * j + 2)
            mean_square(NORMS.index(("final", 0)))
            experts(3, 11, HALVES - 2)
            experts(3, HALVES - 2, HALVES)
            nc.scalar.activation(rms[:, len(NORMS) - 1:], eps[:, :], ACT.Sqrt)
            mean_square(NORMS.index(("final", 1)))

        @block.tensor
        def _(pe):
            order = list(PAIR_USE)
            taken = 0

            def take(key):
                nonlocal taken
                p, n = PAIR_USE[key]
                assert key == order[taken], (key, order[taken])
                taken += 1
                if n:
                    pe.wait_ge(pair_free[p], n)
                return pairs[p]

            def fills(key, ins):
                ins.then_inc(pair_full[PAIR_USE[key][0]], 1)

            def block_of(key):
                place, n, _ = PLACE_OF[key]
                pe.wait_ge(w_loaded[place], 16 * n)
                return places[place]

            def transpose_rows(key, src):
                use = ("T",) + key
                dst = take(use)
                pe.wait_ge(rows_ready, t_at(key) + 1)
                for c in range(KC):
                    ins = nc.tensor.transpose(dst[:, c // 4, (c % 4) * P:(c % 4 + 1) * P],
                                              src[:, c * P:(c + 1) * P], ident[:, :])
                fills(use, ins)

            def product_T(key, i, x, dst, n=WCOLS):
                w = block_of((key, i))
                for m in range(0, n, P):
                    mm = min(P, n - m)
                    for c in range(KC):
                        ins = nc.tensor.matmul(dst(m // P, mm), w[:, c, m:m + mm], x[:, c],
                                               start=(c == 0), stop=(c == KC - 1))
                return ins

            def last_product_T(key, i, x, dst, n=WCOLS):
                product_T(key, i, x, dst, n).then_inc(w_used, 1)

            def product(key, i, x, dst):
                w = block_of((key, i))
                for c in range(KC):
                    ins = nc.tensor.matmul(dst[:, i // 2, (i % 2) * WCOLS:(i % 2 + 1) * WCOLS],
                                           x[:, c, :], w[:, c, :], start=(c == 0), stop=(c == KC - 1))
                return ins

            def last_product(key, i, x, dst):
                product(key, i, x, dst).then_inc(w_used, 1)

            def transpose_keys(layer):
                raw = block_of((("keys", layer), 0)).rearrange("p c n -> p (c n)").rearrange("p (g d) -> p g d", d=RK)
                for i in range(2):
                    dst = take(("keys", layer, i))
                    for c in range(KC):
                        ins = nc.tensor.transpose(dst[:, c // 4, (c % 4) * P:(c % 4 + 1) * P],
                                                  raw[:, i * KC + c, :], ident[:, :])
                    fills(("keys", layer, i), ins)
                pe.wait_ge(*full(("keys", layer, 1)))
                pe.sem_inc(w_used, 1)

            def level(b, i):
                key = ("level", b, i)
                dst = take(key)
                if i < LEVELS - 1:
                    pe.wait_ge(faded_ready, b * (LEVELS - 1) + i + 1)
                for g in range(GH):
                    if i < LEVELS - 1:
                        o = D + (i % 2) * HALF + g * P
                        kk = qq = scratch[:, o:o + P]
                    else:
                        kk, qq = qkT[:, b, 1, g, :], qkT[:, b, 0, g, :]
                    ins = nc.tensor.matmul(dst[:, 0, g * P:(g + 1) * P], kk, qq, start=True, stop=True)
                fills(key, ins)

            def gla_heads(b):
                key = ("o", b)
                dst = flat(take(key))
                pe.wait_ge(attn_ready, b + 1)
                if b:
                    pe.wait_ge(z_ready, 3)
                    pe.wait_ge(*freed("state"))
                for g in range(GH):
                    c = slice(g * GDV, (g + 1) * GDV)
                    if b:
                        nc.tensor.matmul(dst[:, c], faded_end[:, g * P:(g + 1) * P], state[:, g, :],
                                         start=True, stop=False)
                    ins = nc.tensor.matmul(dst[:, c], attnT[:, g, :], vtok[:, b, c], start=(b == 0), stop=True)
                fills(key, ins)

            def spread_gain(name, b):
                key = ("gain", name, b)
                dst = take(key)
                n = len(GAIN_ROW)
                pe.wait_ge(gain_loaded, 16 * (len(GAIN_OF) + n))
                g = GAIN_ROW[name]
                for i in range(2):
                    ins = nc.tensor.matmul(dst[:, i, :], ident[0:n, g:g + 1].broadcast_to([n, P]),
                                           gain[0:n, i * HALF:(i + 1) * HALF], start=True, stop=True)
                fills(key, ins)

            def queries(layer, b, j):
                key = ("route", layer, b, j)
                n = nth_query(layer, b, j)
                dst = take(key)
                slot = t_at((f"ffn{layer}", b)) % 2
                kept = (("pq", layer, b), 2 * j) in KEPT_BLOCKS.values()
                for i in (2 * j, 2 * j + 1):
                    w = block_of((("pq", layer, b), i))
                    for m in range(2):
                        o = ((i % 2) * 2 + m) * P
                        for c in range(KC):
                            ins = nc.tensor.matmul(dst[:, 0, o:o + P], w[:, c, m * P:(m + 1) * P], xT[:, slot, c, :],
                                                   start=(c == 0), stop=(c == KC - 1))
                    if i != 2 * j:
                        ins.then_inc(queryT_full, 1)
                    elif not kept:
                        ins.then_inc(w_used, 1)
                if not kept:
                    pe.wait_ge(queryT_full, n + 1)
                    pe.sem_inc(w_used, 1)

            def scores(layer, b, j):
                key = ("route", layer, b, j)
                n = nth_query(layer, b, j)
                dst = pair_of(key)
                pe.wait_ge(queryT_ready, n + 1)
                for g in range(4):
                    ins = nc.tensor.matmul(dst[:, 1, g * P:(g + 1) * P], queryT[:, g, :], keysT[:, 4 * j + g, :],
                                           start=True, stop=True)
                fills(key, ins)

            def att_logits(b, c):
                key = ("att", b, c)
                dst = take(key)
                n = (b + 1) * P
                for g in range(2):
                    o = g * n
                    for s in range(b + 1):
                        last = s == b
                        nc.tensor.matmul(dst[:, 0, o + s * P:o + (s + 1) * P], q2T[g][:, c, :],
                                         qkT[:, s, c // 4, c % 4, :], start=True, stop=False)
                        ins = nc.tensor.matmul(dst[:, 0, o + s * P:o + (s + 1) * P],
                                               ident[0:FH, 2 * c + g:2 * c + g + 1].broadcast_to([FH, P]),
                                               neg_cumT[:, s * P:(s + 1) * P], start=False, stop=not last)
                        if last:
                            ins = nc.tensor.matmul(dst[:, 0, o + s * P:o + (s + 1) * P], ident16[:, :],
                                                   causal16[:, :], start=False, stop=True)
                fills(key, ins)

            def att_turn(b, c):
                n = b * (FH // 2) + c
                pe.wait_ge(probs_ready, n + 1)
                o = (n % 2) * D
                for i in range(2 * (b + 1)):
                    ins = nc.tensor.transpose(pair_of(("att", b, c))[:, 1, i * P:(i + 1) * P],
                                              scratch[:, o + i * P:o + (i + 1) * P], ident[:, :])
                ins.then_inc(probsT_full, 1)

            def att_values(b, c):
                n = b * (FH // 2) + c
                pe.wait_ge(probsT_ready, n + 1)
                o = (n % 2) * D + HALF
                for g in range(2):
                    for s in range(b + 1):
                        i = g * (b + 1) + s
                        ins = nc.tensor.matmul(pair_of(("att", b, c))[:, 0, g * FHD:(g + 1) * FHD],
                                               scratch[:, o + i * P:o + (i + 1) * P],
                                               v2[:, s, (2 * c + g) * FHD:(2 * c + g + 1) * FHD],
                                               start=(s == 0), stop=(s == b))
                ins.then_inc(pv_full, 1)

            def experts_begin(ph):
                if ph:
                    pe.wait_ge(acc_free, ph)
                else:
                    pe.wait_ge(*freed(("r", 1)))
                for i in range(2):
                    nc.tensor.matmul(acc[:, i, :], zeros16[:, 0:P], zeros16[:, :], start=True, stop=False)

            def half(ph, r, q):
                for k, j in enumerate(PE_SLOTS):
                    if j // SUB != q or is_last(r, j):
                        continue
                    pe.wait_ge(v_loaded[j], r * 16 + 16)
                    pe.wait_ge(diag_ready, r * len(PE_SLOTS) + (k + 1))
                    for i in range(2):
                        ins = nc.tensor.matmul(acc[:, i, :], diag[:, k, :], v_ring[:, j, i * HALF:(i + 1) * HALF],
                                               start=False, stop=False)
                    ins.then_inc(v_free, 1)

            def experts(ph, first, last):
                in_halves(pe, half, ph, first, last)

            def experts_end(ph):
                for i in range(2):
                    ins = nc.tensor.matmul(acc[:, i, :], zeros16[:, 0:P], zeros16[:, :], start=False, stop=True)
                ins.then_inc(acc_full, 1)

            pe.sem_inc(v_free, len(PE_SLOTS))
            pe.wait_ge(consts, 3)
            for b in range(TILES):
                transpose_rows(("mix0", b), rows)
            for b in range(TILES):
                pe.wait_ge(*freed(("T", "mix0", b)))
            dst = take("glr")
            xT_both = xT[:, :, :, :].rearrange("p b c t -> p c b t")
            last_product_T("glr", 0, xT_both, lambda m, mm: dst[0:mm, 0, 0:TILES * P], GRANK)
            pe.wait_ge(*freed("glr"))
            pe.wait_ge(small_loaded, 48)
            dst = flat(take("z"))
            for g in range(GH):
                ins = nc.tensor.matmul(dst[:, g * TILES * P:(g + 1) * TILES * P], w_g2[:, g * P:(g + 1) * P],
                                       glrT[:, :], start=True, stop=True)
            fills("z", ins)
            dst = flat(take("q"))
            for i in range(2):
                last_product_T("q", i, xT_both,
                               lambda m, mm: dst[0:mm, (2 * i + m) * TILES * P:(2 * i + m + 1) * TILES * P])
            dst = flat(take(("k", 0)))
            for i in range(2):
                ins = product_T("k", i, xT[:, 0, :, :], lambda m, mm: dst[0:mm, (2 * i + m) * P:(2 * i + m + 1) * P])
            fills(("k", 0), ins)
            for i in range(LEVELS):
                key = "v" if i < 4 else "r"
                if i % 4 == 0:
                    dst = take((key, 0))
                ins = product(key, i % 4, xT[:, 0, :, :], dst)
                if i % 4 == 3:
                    fills((key, 0), ins)
                level(0, i)

            def weight_out(layer, b, blocks):
                for i in blocks:
                    last_product(("wo", layer, b), i, xT[:, t_at((f"o{layer}", b)) % 2, :, :],
                                 pair_of(("wo", layer, b)))

            def attention(b, first, last):
                for i in range(first, last):
                    if i < FH // 2:
                        att_logits(b, i)
                    if 1 <= i <= FH // 2:
                        att_turn(b, i - 1)
                    if i >= 2:
                        att_values(b, i - 2)

            gla_heads(0)
            v1 = take(("v", 1))
            pe.wait_ge(kept_ready, 1)
            for i in range(2):
                last_product("v", i, xT_kept, v1)
            transpose_keys(0)
            transpose_rows(("o0", 0), rows)
            pe.wait_ge(*freed(("T", "o0", 0)))
            take(("wo", 0, 0))
            weight_out(0, 0, range(4))
            for i in range(2, 4):
                last_product("v", i, xT_kept, v1)
            transpose_rows(("ffn0", 0), xn[:, 0, :])
            pe.wait_ge(*freed(("T", "ffn0", 0)))
            queries(0, 0, 0)
            scores(0, 0, 0)
            r1 = take(("r", 1))
            for i in range(4):
                last_product("r", i, xT_kept, r1)
            for j in FIRST_QUERIES[1:]:
                queries(0, 0, j)
                scores(0, 0, j)

            experts_begin(0)
            experts(0, 0, 4)
            k1 = flat(take(("k", 1)))
            for i in range(2):
                last_product_T("k", i, xT_kept, lambda m, mm: k1[0:mm, (2 * i + m) * P:(2 * i + m + 1) * P])
            experts(0, 4, 6)
            pe.wait_ge(z_ready, 2)
            pe.wait_ge(*full(("o", 0)))
            dst = take("kdec")
            for g in range(GH):
                ins = nc.tensor.transpose(dst[:, 0, g * P:(g + 1) * P],
                                          faded_end[:, g * P:(g + 1) * P], ident[:, :])
            fills("kdec", ins)
            experts(0, 6, 7)
            pe.wait_ge(*freed("kdec"))
            dst = flat(take("state"))
            for g in range(GH):
                c = slice(g * GDV, (g + 1) * GDV)
                ins = nc.tensor.matmul(dst[:, c], kdec[:, g, :], vtok[:, 0, c], start=True, stop=True)
            fills("state", ins)
            experts(0, 7, 9)
            for i in range(LEVELS):
                experts(0, 9 + i, 10 + i)
                level(1, i)
            experts(0, 17, 18)
            gla_heads(1)
            experts(0, 18, 20)
            transpose_rows(("o0", 1), rows)
            experts(0, 20, 21)
            pe.wait_ge(*freed(("T", "o0", 1)))
            take(("wo", 0, 1))
            weight_out(0, 1, (0, 1))
            experts(0, 21, 22)
            weight_out(0, 1, (2, 3))
            experts(0, 22, 24)
            transpose_rows(("ffn0", 1), xn[:, 1, :])
            experts(0, 24, 25)
            pe.wait_ge(*freed(("T", "ffn0", 1)))
            queries(0, 1, 0)
            experts(0, 25, 26)
            scores(0, 1, 0)
            experts(0, 26, HALVES)
            experts_end(0)

            for ph, b in ((1, 0), (2, 1)):
                before = PHASES[ph]
                s_kv, s_mix = t_at(("kv", b)) % 2, t_at(("mix1", b)) % 2
                experts_begin(ph)
                experts(ph, 0, 1)
                queries(*before, 1)
                experts(ph, 1, 2)
                scores(*before, 1)
                spread_gain("kv", b)
                experts(ph, 2, 3)
                transpose_rows(("kv", b), rows)
                experts(ph, 3, 4)
                pe.wait_ge(*freed(("T", "kv", b)))
                dst = flat(take(("K", b)))
                for n in range(4):
                    ins = product_T(("K", b), n, xT[:, s_kv, :, :],
                                    lambda m, mm: dst[:, (2 * n + m) * P:(2 * n + m + 1) * P])
                    if b:
                        ins.then_inc(w_used, 1)
                    if n == 1:
                        experts(ph, 4, 5)
                if b == 0:
                    fills(("K", b), ins)
                experts(ph, 5, 7)
                queries(*before, 2)
                experts(ph, 7, 8)
                scores(*before, 2)
                dst = take(("V", b))
                for n in range(4):
                    last_product(("V", b), n, xT[:, s_kv, :, :], dst)
                    if n == 1:
                        experts(ph, 8, 9)
                dst2 = take(("fl", b))
                last_product_T(("fl", b), 0, xT[:, s_kv, :, :], lambda m, mm: dst2[0:mm, 0, 0:P], FH)
                spread_gain("mix1", b)
                experts(ph, 9, 10)
                queries(*before, 3)
                experts(ph, 10, 11)
                scores(*before, 3)
                transpose_rows(("mix1", b), rows)
                experts(ph, 11, 12)
                pe.wait_ge(*freed(("T", "mix1", b)))
                dst = flat(take(("Q", b)))
                for n in range(4):
                    last_product_T(("Q", b), n, xT[:, s_mix, :, :],
                                   lambda m, mm: dst[:, (2 * n + m) * P:(2 * n + m + 1) * P])
                    if n == 1:
                        experts(ph, 12, 13)
                experts(ph, 13, 15)
                for key in ("Q", "K", "V"):
                    pe.wait_ge(*freed((key, b)))
                pe.wait_ge(cum_ready, b + 1)
                for i in range(5):
                    attention(b, 2 * i, 2 * i + 2)
                    experts(ph, 15 + i, 16 + i)
                transpose_rows(("o1", b), rows)
                experts(ph, 20, 21)
                pe.wait_ge(*freed(("T", "o1", b)))
                take(("wo", 1, b))
                weight_out(1, b, (0, 1))
                experts(ph, 21, 22)
                weight_out(1, b, (2, 3))
                spread_gain("ffn1", b)
                experts(ph, 22, 23)
                if b == 0:
                    transpose_keys(1)
                experts(ph, 23, 24)
                transpose_rows(("ffn1", b), xn[:, b, :])
                experts(ph, 24, 25)
                pe.wait_ge(*freed(("T", "ffn1", b)))
                queries(1, b, 0)
                experts(ph, 25, 26)
                scores(1, b, 0)
                experts(ph, 26, HALVES)
                experts_end(ph)

            experts_begin(3)
            experts(3, 0, 1)
            for j in range(1, 4):
                queries(1, 1, j)
                experts(3, 3 * j - 2, 3 * j - 1)
                scores(1, 1, j)
                experts(3, 3 * j - 1, 3 * j + 1)
            spread_gain("final", 0)
            spread_gain("final", 1)
            experts(3, 10, HALVES - 2)
            experts(3, HALVES - 2, HALVES)
            experts_end(3)


_INS = ["x", "norm_mix", "norm_ffn", "gla_w_in", "gla_w_g2", "gla_b_g", "gla_norm_o", "gla_w_o", "kv_norm", "kv_w",
        "fox_b_f", "fox_w_q", "fox_w_o", "peer_w_q", "peer_sub_keys", "peer_u", "peer_v", "norm_final"]


def kernel(**inputs):
    import numpy as _np
    import concourse.bacc as _bacc
    from concourse import mybir as _mybir
    from concourse.bass_utils import run_bass_kernel_spmd as _run

    nc = _bacc.Bacc("TRN2", target_bir_lowering=False, num_devices=1)
    arrays, args = {}, {}
    for name in _INS:
        v = _np.ascontiguousarray(inputs[name])
        arrays[f"in_{name}"] = v
        args[name] = nc.dram_tensor(f"in_{name}", v.shape, _mybir.dt.from_np(v.dtype), kind="ExternalInput").ap()
    out = nc.dram_tensor("out_0", inputs["x"].shape, _mybir.dt.from_np(_np.dtype("float32")),
                         kind="ExternalOutput").ap()
    yoco_kernel(nc, args, out)
    r = _run(nc, [arrays], core_ids=[0])
    return r.results[0]["out_0"]
```
